# Optimizing a Trainium2 kernel written in Bass

```python
import math
import jax, jax.numpy as jnp
from jax import lax
import numpy as np

D_MODEL = 1024
BATCH = 1
SEQ = 512
DEPTH = 1

ROPE_THETA = 10000.0
EPS = 1e-6
Q_BLOCK = 128

MLA_HEADS = 4
MLA_Q_RANK = 256
MLA_KV_RANK = 256
MLA_NOPE_DIM = 128
MLA_ROPE_DIM = 64
MLA_V_DIM = 128

DIFF_HEADS = 4
DIFF_QK_DIM = 64
DIFF_V_DIM = 2 * DIFF_QK_DIM

MIX_WIDTH = MLA_HEADS * MLA_V_DIM + DIFF_HEADS * DIFF_V_DIM
IN_SPLITS = (MLA_Q_RANK, MLA_KV_RANK, MLA_ROPE_DIM,
             DIFF_HEADS * 2 * DIFF_QK_DIM, DIFF_HEADS * 2 * DIFF_QK_DIM, DIFF_HEADS * DIFF_V_DIM)
IN_COLS = sum(IN_SPLITS)

N_GROUPS = 4
EXPERTS_PER_GROUP = 8
N_EXPERTS = N_GROUPS * EXPERTS_PER_GROUP
TOP_K = 2
D_EXPERT = 512
MOE_BLOCK = 128


def rms_norm(x, g):
    xf = x.astype(jnp.float32)
    y = xf * lax.rsqrt(jnp.mean(xf * xf, axis=-1, keepdims=True) + EPS)
    return (y * g.astype(jnp.float32)).astype(x.dtype)

def rope(x, pos):
    d = x.shape[-1]
    inv = ROPE_THETA ** (-jnp.arange(0, d, 2, dtype=jnp.float32) / d)
    ang = pos.astype(jnp.float32)[:, None] * inv[None, :]
    shape = (1, x.shape[1]) + (1,) * (x.ndim - 3) + (d // 2,)
    cos = jnp.cos(ang).reshape(shape)
    sin = jnp.sin(ang).reshape(shape)
    xf = x.astype(jnp.float32)
    x1, x2 = xf[..., : d // 2], xf[..., d // 2:]
    return jnp.concatenate([x1 * cos - x2 * sin, x2 * cos + x1 * sin], axis=-1).astype(x.dtype)

def to_blocks(t):
    b, s = t.shape[0], t.shape[1]
    return t.reshape((b, s // Q_BLOCK, Q_BLOCK) + t.shape[2:]).swapaxes(0, 1)

def from_blocks(t):
    nb, b, qb = t.shape[0], t.shape[1], t.shape[2]
    return t.swapaxes(0, 1).reshape((b, nb * qb) + t.shape[3:])

def mla_attention(q_nope, q_pe, k_nope, k_pe, v):
    scale = (q_nope.shape[-1] + q_pe.shape[-1]) ** -0.5

    def block(args):
        qn, qr = args
        s = (jnp.einsum('bqhd,bkhd->bhqk', qn, k_nope)
             + jnp.einsum('bqhr,bkr->bhqk', qr, k_pe)).astype(jnp.float32) * scale
        p = jax.nn.softmax(s, axis=-1).astype(v.dtype)
        return jnp.einsum('bhqk,bkhd->bqhd', p, v)

    return from_blocks(lax.map(block, (to_blocks(q_nope), to_blocks(q_pe))))

def diff_attention(q1, q2, k1, k2, v, lam):
    scale = q1.shape[-1] ** -0.5

    def block(args):
        a1, a2 = args
        s1 = jnp.einsum('bqhd,bkhd->bhqk', a1, k1).astype(jnp.float32) * scale
        s2 = jnp.einsum('bqhd,bkhd->bhqk', a2, k2).astype(jnp.float32) * scale
        p = (jax.nn.softmax(s1, axis=-1) - lam * jax.nn.softmax(s2, axis=-1)).astype(v.dtype)
        return jnp.einsum('bhqk,bkhd->bqhd', p, v)

    return from_blocks(lax.map(block, (to_blocks(q1), to_blocks(q2))))

def hier_moe(h, w_rg, b_rg, w_re, b_re, w_gate, w_up, w_down):
    b, s, d = h.shape
    t = b * s
    a = t * TOP_K
    hf = h.reshape(t, d)
    hf32 = hf.astype(jnp.float32)
    g_logits = hf32 @ w_rg.astype(jnp.float32) + b_rg.astype(jnp.float32)
    g_prob, g_idx = lax.top_k(jax.nn.softmax(g_logits, axis=-1), 1)
    e_logits = (hf32 @ w_re.astype(jnp.float32) + b_re.astype(jnp.float32)).reshape(t, N_GROUPS, EXPERTS_PER_GROUP)
    e_sel = jnp.take_along_axis(e_logits, g_idx[:, :, None], axis=1)[:, 0]
    top_l, top_i = lax.top_k(e_sel, TOP_K)
    weights = (g_prob * jax.nn.softmax(top_l, axis=-1)).astype(h.dtype)
    eid = g_idx * EXPERTS_PER_GROUP + top_i

    e_flat = eid.reshape(a).astype(jnp.int32)
    t_flat = jnp.repeat(jnp.arange(t, dtype=jnp.int32), TOP_K)
    w_flat = weights.reshape(a)
    order = jnp.argsort(e_flat)
    e_s, t_s, w_s = e_flat[order], t_flat[order], w_flat[order]
    counts = jnp.zeros((N_EXPERTS,), jnp.int32).at[e_flat].add(1)
    starts = jnp.cumsum(counts) - counts
    padded = ((counts + MOE_BLOCK - 1) // MOE_BLOCK) * MOE_BLOCK
    pends = jnp.cumsum(padded)
    pstarts = pends - padded
    dest = pstarts[e_s] + (jnp.arange(a, dtype=jnp.int32) - starts[e_s])
    rows = a + N_EXPERTS * MOE_BLOCK
    nb = rows // MOE_BLOCK
    row_token = jnp.zeros((rows,), jnp.int32).at[dest].set(t_s)
    row_weight = jnp.zeros((rows,), h.dtype).at[dest].set(w_s)
    block_expert = jnp.minimum(
        jnp.searchsorted(pends, jnp.arange(nb, dtype=jnp.int32) * MOE_BLOCK, side='right'),
        N_EXPERTS - 1).astype(jnp.int32)
    xs = hf[row_token].reshape(nb, MOE_BLOCK, d)

    def expert_block(args):
        xb, e = args
        g = xb @ w_gate[e]
        u = xb @ w_up[e]
        return (jax.nn.silu(g) * u) @ w_down[e]

    ys = lax.map(expert_block, (xs, block_expert)).reshape(rows, d)
    out = jnp.zeros((t, d), h.dtype).at[row_token].add(ys * row_weight[:, None])
    return out.reshape(b, s, d)

def first_inputs(seed: int = 0) -> dict:
    key = jax.random.key(seed)
    ks = jax.random.split(key, 32)
    f32 = jnp.float32
    L, D = DEPTH, D_MODEL

    def nrm(k, shape, std):
        return jax.random.normal(k, shape, f32) * std

    def gain(k, shape):
        return 1.0 + 0.02 * jax.random.normal(k, shape, f32)

    return {
        'x': nrm(ks[0], (BATCH, SEQ, D), 1.0),
        'c': nrm(ks[1], (BATCH, D), 1.0),
        'w_ada': nrm(ks[2], (L, D, 6 * D), 0.5 * D ** -0.5),
        'b_ada': nrm(ks[3], (L, 6 * D), 0.02),
        'norm1_g': gain(ks[4], (L, D)),
        'w_in': nrm(ks[5], (L, D, IN_COLS), D ** -0.5),
        'q_a_norm_g': gain(ks[6], (L, MLA_Q_RANK)),
        'w_q_up': nrm(ks[7], (L, MLA_Q_RANK, MLA_HEADS * (MLA_NOPE_DIM + MLA_ROPE_DIM)), MLA_Q_RANK ** -0.5),
        'kv_a_norm_g': gain(ks[8], (L, MLA_KV_RANK)),
        'w_kv_up': nrm(ks[9], (L, MLA_KV_RANK, MLA_HEADS * (MLA_NOPE_DIM + MLA_V_DIM)), MLA_KV_RANK ** -0.5),
        'lambda_q1': nrm(ks[10], (L, DIFF_QK_DIM), 0.1),
        'lambda_k1': nrm(ks[11], (L, DIFF_QK_DIM), 0.1),
        'lambda_q2': nrm(ks[12], (L, DIFF_QK_DIM), 0.1),
        'lambda_k2': nrm(ks[13], (L, DIFF_QK_DIM), 0.1),
        'subln_g': gain(ks[14], (L, DIFF_V_DIM)),
        'w_out': nrm(ks[15], (L, MIX_WIDTH, D), MIX_WIDTH ** -0.5),
        'norm2_g': gain(ks[16], (L, D)),
        'w_router_group': nrm(ks[17], (L, D, N_GROUPS), D ** -0.5),
        'b_router_group': nrm(ks[18], (L, N_GROUPS), 0.01),
        'w_router_expert': nrm(ks[19], (L, D, N_EXPERTS), D ** -0.5),
        'b_router_expert': nrm(ks[20], (L, N_EXPERTS), 0.01),
        'w_expert_gate': nrm(ks[21], (L, N_EXPERTS, D, D_EXPERT), D ** -0.5),
        'w_expert_up': nrm(ks[22], (L, N_EXPERTS, D, D_EXPERT), D ** -0.5),
        'w_expert_down': nrm(ks[23], (L, N_EXPERTS, D_EXPERT, D), D_EXPERT ** -0.5),
        'final_norm_g': gain(ks[24], (D,)),
    }

def first_block(x, c, w_ada, b_ada, norm1_g, w_in, q_a_norm_g, w_q_up, kv_a_norm_g, w_kv_up,
              lambda_q1, lambda_k1, lambda_q2, lambda_k2, subln_g, w_out, norm2_g,
              w_router_group, b_router_group, w_router_expert, b_router_expert,
              w_expert_gate, w_expert_up, w_expert_down, final_norm_g):
    b, s, _ = x.shape
    pos = jnp.arange(s, dtype=jnp.int32)
    offsets = [int(v) for v in np.cumsum(IN_SPLITS)[:-1]]
    for l in range(DEPTH):
        mod = jax.nn.silu(c) @ w_ada[l] + b_ada[l]
        shift1, scale1, gate1, shift2, scale2, gate2 = jnp.split(mod, 6, axis=-1)

        h = rms_norm(x, norm1_g[l]) * (1.0 + scale1[:, None, :]) + shift1[:, None, :]
        z = h @ w_in[l]
        c_q, c_kv, k_pe, dq, dk, dv = jnp.split(z, offsets, axis=-1)

        q = (rms_norm(c_q, q_a_norm_g[l]) @ w_q_up[l]).reshape(b, s, MLA_HEADS, MLA_NOPE_DIM + MLA_ROPE_DIM)
        q_nope, q_pe = q[..., :MLA_NOPE_DIM], rope(q[..., MLA_NOPE_DIM:], pos)
        kv = (rms_norm(c_kv, kv_a_norm_g[l]) @ w_kv_up[l]).reshape(b, s, MLA_HEADS, MLA_NOPE_DIM + MLA_V_DIM)
        k_nope, v_mla = kv[..., :MLA_NOPE_DIM], kv[..., MLA_NOPE_DIM:]
        k_pe = rope(k_pe[:, :, None, :], pos)[:, :, 0, :]
        mla_out = mla_attention(q_nope, q_pe, k_nope, k_pe, v_mla).reshape(b, s, MLA_HEADS * MLA_V_DIM)

        dq = rope(dq.reshape(b, s, DIFF_HEADS, 2, DIFF_QK_DIM), pos)
        dk = rope(dk.reshape(b, s, DIFF_HEADS, 2, DIFF_QK_DIM), pos)
        dv = dv.reshape(b, s, DIFF_HEADS, DIFF_V_DIM)
        lambda_init = 0.8 - 0.6 * math.exp(-0.3 * l)
        lam = (jnp.exp(jnp.sum(lambda_q1[l].astype(jnp.float32) * lambda_k1[l].astype(jnp.float32)))
               - jnp.exp(jnp.sum(lambda_q2[l].astype(jnp.float32) * lambda_k2[l].astype(jnp.float32)))
               + lambda_init)
        d_out = diff_attention(dq[..., 0, :], dq[..., 1, :], dk[..., 0, :], dk[..., 1, :], dv, lam)
        d_out = (rms_norm(d_out, subln_g[l]) * (1.0 - lambda_init)).reshape(b, s, DIFF_HEADS * DIFF_V_DIM)

        mix = jnp.concatenate([mla_out, d_out], axis=-1) @ w_out[l]
        x = x + gate1[:, None, :] * mix

        h2 = rms_norm(x, norm2_g[l]) * (1.0 + scale2[:, None, :]) + shift2[:, None, :]
        moe = hier_moe(h2, w_router_group[l], b_router_group[l], w_router_expert[l], b_router_expert[l],
                       w_expert_gate[l], w_expert_up[l], w_expert_down[l])
        x = x + gate2[:, None, :] * moe
    return rms_norm(x, final_norm_g)


MEM_LEN = 256
HEAD_DIM = 64
N_HEADS = D_MODEL // HEAD_DIM
N_KV_GROUPS = 4
HEADS_PER_GROUP = N_HEADS // N_KV_GROUPS
CMP_BLOCK = 32
CMP_STRIDE = 16
SEL_BLOCK = 64
SEL_TOP_N = 16
WINDOW = 512
SEL_Q_CHUNK = 16
CONV_CH = D_MODEL
CONV_WIDTH = 31
X_HEADS = 4
X_HEAD_DIM = D_MODEL // X_HEADS
D_FF = int(math.ceil(8 * D_MODEL / 3 / 256)) * 256
REL_BUCKETS = 32
REL_MAX_DIST = 128

SPLIT_SIZES = (
    2 * CONV_CH,
    N_HEADS * HEAD_DIM,
    N_KV_GROUPS * HEAD_DIM,
    N_KV_GROUPS * HEAD_DIM,
    N_KV_GROUPS * HEAD_DIM,
    N_KV_GROUPS * HEAD_DIM,
    N_KV_GROUPS * HEAD_DIM,
    N_KV_GROUPS * HEAD_DIM,
    3 * N_HEADS,
    D_MODEL,
    D_MODEL,
)
N_IN = sum(SPLIT_SIZES)
SPLIT_POINTS = tuple(int(v) for v in np.cumsum(SPLIT_SIZES)[:-1])


def rms_norm_2(x, g):
    xf = x.astype(jnp.float32)
    y = xf * lax.rsqrt(jnp.mean(xf * xf, axis=-1, keepdims=True) + EPS)
    return (y * g.astype(jnp.float32)).astype(x.dtype)

def layer_norm(x, g, b):
    xf = x.astype(jnp.float32)
    mu = jnp.mean(xf, axis=-1, keepdims=True)
    xc = xf - mu
    y = xc * lax.rsqrt(jnp.mean(xc * xc, axis=-1, keepdims=True) + EPS)
    return (y * g.astype(jnp.float32) + b.astype(jnp.float32)).astype(x.dtype)

def t5_bucket(dist):
    n = jnp.maximum(dist, 0)
    max_exact = REL_BUCKETS // 2
    nf = jnp.maximum(n, 1).astype(jnp.float32)
    large = max_exact + (jnp.log(nf / max_exact) / math.log(REL_MAX_DIST / max_exact)
                         * (REL_BUCKETS - max_exact)).astype(jnp.int32)
    large = jnp.minimum(large, REL_BUCKETS - 1)
    return jnp.where(n < max_exact, n, large)

def masked_softmax(s, mask):
    s = jnp.where(mask, s, -1e30)
    m = jnp.max(s, axis=-1, keepdims=True)
    p = jnp.where(mask, jnp.exp(s - m), 0.0)
    return p / jnp.maximum(jnp.sum(p, axis=-1, keepdims=True), 1e-30)

def conv_module(u, dw_w, dw_b, ln_g, ln_b, pw_w):
    a, gt = jnp.split(u, 2, axis=-1)
    v = a * jax.nn.sigmoid(gt)
    v = lax.conv_general_dilated(
        v, dw_w[:, None, :], window_strides=(1,),
        padding=((CONV_WIDTH - 1, 0),),
        dimension_numbers=("NWC", "WIO", "NWC"),
        feature_group_count=CONV_CH) + dw_b
    v = jax.nn.silu(layer_norm(v, ln_g, ln_b))
    return v @ pw_w

def compress_blocks(blocks, pos, w1, w2):
    z = blocks + pos[None, None, :, None, :]
    z = jnp.einsum("bnlgd,lde->bnge", z, w1)
    return jax.nn.silu(z) @ w2

def nsa_attention(q, kc, vc, ks, vs, kw, vw, gate_logits, cmp_pos, cmp_w1, cmp_w2, rel_bias):
    B, S = q.shape[0], q.shape[1]
    G, R, Dh = N_KV_GROUPS, HEADS_PER_GROUP, HEAD_DIM
    scale = 1.0 / math.sqrt(Dh)
    qg = q.reshape(B, S, G, R, Dh)
    t = jnp.arange(S)

    n_cmp = (S - CMP_BLOCK) // CMP_STRIDE + 1
    cidx = np.arange(n_cmp)[:, None] * CMP_STRIDE + np.arange(CMP_BLOCK)[None, :]
    k_cmp = compress_blocks(kc[:, cidx], cmp_pos[0], cmp_w1[0], cmp_w2[0])
    v_cmp = compress_blocks(vc[:, cidx], cmp_pos[1], cmp_w1[1], cmp_w2[1])
    c_end = jnp.arange(n_cmp) * CMP_STRIDE + CMP_BLOCK - 1
    dist_c = t[:, None] - c_end[None, :]
    bias_c = rel_bias[t5_bucket(dist_c)].reshape(S, n_cmp, G, R).transpose(2, 3, 0, 1)
    s_c = jnp.einsum("bsgrd,bngd->bgrsn", qg, k_cmp).astype(jnp.float32) * scale + bias_c
    p_cmp = masked_softmax(s_c, dist_c >= 0)
    o_cmp = jnp.einsum("bgrsn,bngd->bsgrd", p_cmp.astype(v_cmp.dtype), v_cmp)

    n_sel = S // SEL_BLOCK
    top_n = min(SEL_TOP_N, n_sel)
    jj = np.arange(n_cmp)[:, None] * CMP_STRIDE
    mm0 = np.arange(n_sel)[None, :] * SEL_BLOCK
    overlap = ((jj < mm0 + SEL_BLOCK) & (jj + CMP_BLOCK > mm0)).astype(np.float32)
    imp = jnp.einsum("bgrsn,nm->bsgm", p_cmp, jnp.asarray(overlap))
    blk_t = (t // SEL_BLOCK)[:, None]
    mm = jnp.arange(n_sel)[None, :]
    forced = (mm == 0) | (mm == blk_t) | (mm == blk_t - 1)
    valid = mm <= blk_t
    score = jnp.where(forced[None, :, None, :], jnp.inf,
                      jnp.where(valid[None, :, None, :], imp, -jnp.inf))
    _, sel_idx = lax.top_k(score, top_n)

    ksg = ks.reshape(B, n_sel, SEL_BLOCK, G, Dh).transpose(0, 3, 1, 2, 4)
    vsg = vs.reshape(B, n_sel, SEL_BLOCK, G, Dh).transpose(0, 3, 1, 2, 4)
    bias_g = rel_bias.reshape(REL_BUCKETS, G, R)
    nc = S // SEL_Q_CHUNK
    q_ch = qg.reshape(B, nc, SEL_Q_CHUNK, G, R, Dh).swapaxes(0, 1)
    i_ch = sel_idx.reshape(B, nc, SEL_Q_CHUNK, G, top_n).swapaxes(0, 1)
    starts = jnp.arange(nc) * SEL_Q_CHUNK
    b_ix = jnp.arange(B)[:, None, None, None]
    g_ix = jnp.arange(G)[None, None, :, None]
    n_keys = top_n * SEL_BLOCK

    def sel_chunk(args):
        qc, ic, st = args
        kg = ksg[b_ix, g_ix, ic].reshape(B, SEL_Q_CHUNK, G, n_keys, Dh)
        vg = vsg[b_ix, g_ix, ic].reshape(B, SEL_Q_CHUNK, G, n_keys, Dh)
        kpos = (ic[..., None] * SEL_BLOCK + jnp.arange(SEL_BLOCK)).reshape(B, SEL_Q_CHUNK, G, n_keys)
        tq = st + jnp.arange(SEL_Q_CHUNK)
        dist = tq[None, :, None, None] - kpos
        bias = bias_g[t5_bucket(dist), g_ix]
        s = jnp.einsum("bqgrd,bqgkd->bqgrk", qc, kg).astype(jnp.float32) * scale \
            + bias.swapaxes(-1, -2)
        p = masked_softmax(s, (dist >= 0)[:, :, :, None, :])
        return jnp.einsum("bqgrk,bqgkd->bqgrd", p.astype(vg.dtype), vg)

    o_slc = lax.map(sel_chunk, (q_ch, i_ch, starts)).swapaxes(0, 1).reshape(B, S, G, R, Dh)

    nq = S // Q_BLOCK
    kwp = jnp.pad(kw, ((0, 0), (WINDOW, 0), (0, 0), (0, 0)))
    vwp = jnp.pad(vw, ((0, 0), (WINDOW, 0), (0, 0), (0, 0)))
    q_bl = qg.reshape(B, nq, Q_BLOCK, G, R, Dh).swapaxes(0, 1)

    def win_block(args):
        qb, i = args
        start = i * Q_BLOCK
        kb = lax.dynamic_slice_in_dim(kwp, start, Q_BLOCK + WINDOW, axis=1)
        vb = lax.dynamic_slice_in_dim(vwp, start, Q_BLOCK + WINDOW, axis=1)
        tq = start + jnp.arange(Q_BLOCK)
        kpos = start - WINDOW + jnp.arange(Q_BLOCK + WINDOW)
        dist = tq[:, None] - kpos[None, :]
        mask = (dist >= 0) & (dist < WINDOW) & (kpos[None, :] >= 0)
        bias = rel_bias[t5_bucket(dist)].reshape(Q_BLOCK, Q_BLOCK + WINDOW, G, R).transpose(2, 3, 0, 1)
        s = jnp.einsum("bqgrd,bkgd->bgrqk", qb, kb).astype(jnp.float32) * scale + bias
        p = masked_softmax(s, mask)
        return jnp.einsum("bgrqk,bkgd->bqgrd", p.astype(vb.dtype), vb)

    o_win = lax.map(win_block, (q_bl, jnp.arange(nq))).swapaxes(0, 1).reshape(B, S, G, R, Dh)

    g = jax.nn.sigmoid(gate_logits).reshape(B, S, 3, G, R, 1)
    o = g[:, :, 0] * o_cmp + g[:, :, 1] * o_slc + g[:, :, 2] * o_win
    return o.reshape(B, S, N_HEADS * HEAD_DIM)

def hybrid_mixer(h, w_in, conv_dw_w, conv_dw_b, conv_ln_g, conv_ln_b, conv_pw_w,
                 cmp_pos, cmp_w1, cmp_w2, w_out, rel_bias):
    B, S = h.shape[0], h.shape[1]
    (u_conv, q, kc, vc, ks, vs, kw, vw, g_nsa_heads, g_conv, g_attn) = jnp.split(
        h @ w_in, SPLIT_POINTS, axis=-1)
    kv_shape = (B, S, N_KV_GROUPS, HEAD_DIM)
    conv_out = conv_module(u_conv, conv_dw_w, conv_dw_b, conv_ln_g, conv_ln_b, conv_pw_w)
    nsa_out = nsa_attention(
        q.reshape(B, S, N_HEADS, HEAD_DIM),
        kc.reshape(kv_shape), vc.reshape(kv_shape), ks.reshape(kv_shape),
        vs.reshape(kv_shape), kw.reshape(kv_shape), vw.reshape(kv_shape),
        g_nsa_heads.reshape(B, S, 3, N_HEADS), cmp_pos, cmp_w1, cmp_w2, rel_bias)
    y = jax.nn.sigmoid(g_conv) * conv_out + jax.nn.sigmoid(g_attn) * nsa_out
    return y @ w_out

def cross_attention(h, mem, wq, wkv, wo):
    B, S = h.shape[0], h.shape[1]
    M = mem.shape[1]
    q = (h @ wq).reshape(B, S, X_HEADS, X_HEAD_DIM)
    k, v = jnp.split(mem @ wkv, 2, axis=-1)
    k = k.reshape(B, M, X_HEADS, X_HEAD_DIM)
    v = v.reshape(B, M, X_HEADS, X_HEAD_DIM)
    s = jnp.einsum("bshd,bmhd->bhsm", q, k).astype(jnp.float32) / math.sqrt(X_HEAD_DIM)
    p = jax.nn.softmax(s, axis=-1).astype(v.dtype)
    o = jnp.einsum("bhsm,bmhd->bshd", p, v).reshape(B, S, X_HEADS * X_HEAD_DIM)
    return o @ wo

def swiglu(h, w_in, w_out):
    a, b = jnp.split(h @ w_in, 2, axis=-1)
    return (jax.nn.silu(a) * b) @ w_out

def second_inputs(seed: int = 0) -> dict:
    key = jax.random.key(seed)
    ks = jax.random.split(key, 24)
    f32 = jnp.float32

    def nrm(k, shape, scale):
        return jax.random.normal(k, shape, f32) * scale

    def gain(k, shape):
        return 1.0 + 0.02 * jax.random.normal(k, shape, f32)

    return {
        "x": jax.random.normal(ks[0], (BATCH, SEQ, D_MODEL), f32),
        "mem": jax.random.normal(ks[1], (BATCH, MEM_LEN, D_MODEL), f32),
        "norm_mix_g": gain(ks[2], (DEPTH, D_MODEL)),
        "w_in": nrm(ks[3], (DEPTH, D_MODEL, N_IN), D_MODEL ** -0.5),
        "conv_dw_w": nrm(ks[4], (DEPTH, CONV_WIDTH, CONV_CH), CONV_WIDTH ** -0.5),
        "conv_dw_b": nrm(ks[5], (DEPTH, CONV_CH), 0.02),
        "conv_ln_g": gain(ks[6], (DEPTH, CONV_CH)),
        "conv_ln_b": nrm(ks[7], (DEPTH, CONV_CH), 0.02),
        "conv_pw_w": nrm(ks[8], (DEPTH, CONV_CH, D_MODEL), CONV_CH ** -0.5),
        "cmp_pos": nrm(ks[9], (DEPTH, 2, CMP_BLOCK, HEAD_DIM), 0.1),
        "cmp_w1": nrm(ks[10], (DEPTH, 2, CMP_BLOCK, HEAD_DIM, HEAD_DIM), (CMP_BLOCK * HEAD_DIM) ** -0.5),
        "cmp_w2": nrm(ks[11], (DEPTH, 2, HEAD_DIM, HEAD_DIM), HEAD_DIM ** -0.5),
        "w_out": nrm(ks[12], (DEPTH, D_MODEL, D_MODEL), D_MODEL ** -0.5),
        "norm_x_g": gain(ks[13], (DEPTH, D_MODEL)),
        "xq_w": nrm(ks[14], (DEPTH, D_MODEL, X_HEADS * X_HEAD_DIM), D_MODEL ** -0.5),
        "xkv_w": nrm(ks[15], (DEPTH, D_MODEL, 2 * X_HEADS * X_HEAD_DIM), D_MODEL ** -0.5),
        "xo_w": nrm(ks[16], (DEPTH, X_HEADS * X_HEAD_DIM, D_MODEL), (X_HEADS * X_HEAD_DIM) ** -0.5),
        "norm_ffn_g": gain(ks[17], (DEPTH, D_MODEL)),
        "ffn_in_w": nrm(ks[18], (DEPTH, D_MODEL, 2 * D_FF), D_MODEL ** -0.5),
        "ffn_out_w": nrm(ks[19], (DEPTH, D_FF, D_MODEL), D_FF ** -0.5),
        "rel_bias": nrm(ks[20], (REL_BUCKETS, N_HEADS), 0.5),
        "final_norm_g": gain(ks[21], (D_MODEL,)),
    }

def second_block(x, mem, norm_mix_g, w_in, conv_dw_w, conv_dw_b, conv_ln_g, conv_ln_b,
              conv_pw_w, cmp_pos, cmp_w1, cmp_w2, w_out, norm_x_g, xq_w, xkv_w, xo_w,
              norm_ffn_g, ffn_in_w, ffn_out_w, rel_bias, final_norm_g):
    for l in range(DEPTH):
        h = rms_norm_2(x, norm_mix_g[l])
        x = x + hybrid_mixer(h, w_in[l], conv_dw_w[l], conv_dw_b[l], conv_ln_g[l], conv_ln_b[l],
                             conv_pw_w[l], cmp_pos[l], cmp_w1[l], cmp_w2[l], w_out[l], rel_bias)
        h = rms_norm_2(x, norm_x_g[l])
        x = x + cross_attention(h, mem, xq_w[l], xkv_w[l], xo_w[l])
        h = rms_norm_2(x, norm_ffn_g[l])
        x = x + swiglu(h, ffn_in_w[l], ffn_out_w[l])
    return rms_norm_2(x, final_norm_g)


def setup_inputs(seed=0):
    out = dict(first_inputs(seed))
    for name, value in second_inputs(seed + 1).items():
        if name != "x":
            out[name + "_2"] = value
    return out


def reference(
    x, c, w_ada, b_ada, norm1_g, w_in, q_a_norm_g, w_q_up, kv_a_norm_g, w_kv_up, lambda_q1,
    lambda_k1, lambda_q2, lambda_k2, subln_g, w_out, norm2_g, w_router_group, b_router_group,
    w_router_expert, b_router_expert, w_expert_gate, w_expert_up, w_expert_down, final_norm_g,
    mem_2, norm_mix_g_2, w_in_2, conv_dw_w_2, conv_dw_b_2, conv_ln_g_2, conv_ln_b_2,
    conv_pw_w_2, cmp_pos_2, cmp_w1_2, cmp_w2_2, w_out_2, norm_x_g_2, xq_w_2, xkv_w_2, xo_w_2,
    norm_ffn_g_2, ffn_in_w_2, ffn_out_w_2, rel_bias_2, final_norm_g_2,
):
    x = first_block(
        x, c, w_ada, b_ada, norm1_g, w_in, q_a_norm_g, w_q_up, kv_a_norm_g, w_kv_up, lambda_q1,
        lambda_k1, lambda_q2, lambda_k2, subln_g, w_out, norm2_g, w_router_group,
        b_router_group, w_router_expert, b_router_expert, w_expert_gate, w_expert_up,
        w_expert_down, final_norm_g,
    )
    return second_block(
        x, mem_2, norm_mix_g_2, w_in_2, conv_dw_w_2, conv_dw_b_2, conv_ln_g_2, conv_ln_b_2,
        conv_pw_w_2, cmp_pos_2, cmp_w1_2, cmp_w2_2, w_out_2, norm_x_g_2, xq_w_2, xkv_w_2,
        xo_w_2, norm_ffn_g_2, ffn_in_w_2, ffn_out_w_2, rel_bias_2, final_norm_g_2,
    )


_drawn_inputs = setup_inputs


def setup_inputs(seed=0):
    import zlib

    import numpy as np

    out = dict(_drawn_inputs(seed))
    spreads = {}
    factors = {'norm1_g': 8.0,
     'q_a_norm_g': 8.0,
     'kv_a_norm_g': 8.0,
     'lambda_q1': 8.0,
     'lambda_q2': 3.873,
     'subln_g': 8.0,
     'norm2_g': 3.931,
     'b_router_group': 6.704,
     'b_router_expert': 7.667,
     'norm_mix_g_2': 6.523,
     'conv_dw_b_2': 12.44,
     'conv_ln_g_2': 23.568,
     'conv_ln_b_2': 22.421,
     'cmp_pos_2': 3.44,
     'norm_x_g_2': 182.685,
     'norm_ffn_g_2': 11.589,
     'final_norm_g_2': 22.832}
    for name, (base, spread) in spreads.items():
        noise = np.random.default_rng([zlib.crc32(name.encode()), seed]).standard_normal(out[name].shape)
        drawn = base * np.exp(spread * noise) if base else spread * noise
        out[name] = __import__('jax').numpy.asarray(drawn.astype(out[name].dtype))
    for name, factor in factors.items():
        out[name] = (out[name] * factor).astype(out[name].dtype)
    return out
```

```python
from contextlib import ExitStack

import concourse.bass as bass
from concourse import mybir

F32 = mybir.dt.float32
I32 = mybir.dt.int32
ALU = mybir.AluOpType
ACT = mybir.ActivationFunctionType
AX = mybir.AxisListType.X

P = 128
S = 512
TT = S // P
D = 1024
KT = D // P
EPS = 1e-6
C = 512
SLOT = KT * C
N_DENSE_SLOTS = 4
N_SLOTS = 6
MLA_SCALE = (128 + 64) ** -0.5
DIFF_SCALE = 64 ** -0.5
LAMBDA_INIT = 0.8 - 0.6
NEG = -1e30
N_EXP = 32
D_EXP = 512
CAP = P
N_OVER = 7
N_BLOCKS = N_EXP + N_OVER
CONV_W = 31
PAD = CONV_W - 1
VW_ = PAD + S
NH = 16
NCMP = 32
D_FF = 2816
FT = D_FF // P
NG = 1040
MEM = 256

K1_ID, K1_MASK, K1_N = 0, 128, 256
K2_COS, K2_SIN, K2_LT, K2_IOTA, K2_TOK, K2_ANTI, K2_N = 0, 128, 384, 512, 640, 644, 772
V_N1, V_N2, V_MIX, V_XN, V_FFN, V_QA, V_KVA, V_SUB, V_DWB, V_LNG, V_LNB, V_C = (
    0, 8, 16, 24, 32, 40, 42, 44, 45, 53, 61, 69)
V_DW, V_POS, V_W2, V_N = 77, 77 + KT * CONV_W, 77 + KT * CONV_W + 32, 77 + KT * CONV_W + 32 + 128


GROUPS = []
FIRST = {}
CHUNK_LAST = []
CHUNK_DMAS = []


def plan(stage, engines, chunks=0, dmas=1):
    FIRST[stage] = len(GROUPS)
    GROUPS.extend(engines)
    per = len(engines) // chunks if chunks else 0
    for c in range(chunks):
        CHUNK_LAST.append(FIRST[stage] + per * (c + 1) - 1)
        CHUNK_DMAS.append(dmas)


plan("ada0", ["act"] * 4, 4)
plan("modcols", ["dve"])
plan("c", ["act"] * 4, 1)
plan("ada1", ["act"] * 2, 2)
plan("kpe", ["dve"] * 4, 1)
plan("dq", ["dve"] * 4, 1)
plan("ada2", ["act"] * 2, 2)
plan("dk", ["dve"] * 4, 1)
plan("ada3", ["act"] * 2, 2)
plan("dv", ["act"] * 4, 1)
plan("ada4", ["act"] * 2, 2)
plan("modcols2", ["dve"])
plan("up", ["act"] * 12 + ["dve"] * 4, 1, 2)
plan("wo", ["dve"] * 8, 2)
B1_CHUNKS = len(CHUNK_LAST)
plan("router", ["dve"] * 4)
plan("rank", ["dve"])
plan("over", ["dve"])
plan("slots", ["dve"])
B2_FIRST = len(GROUPS)
plan("toep", ["act"] * 3)
plan("glu_g", ["act"] * 8, 2)
plan("glu_a", ["dve"] * 8, 2)
plan("q2", ["act"] * 8, 2)
plan("kvc", ["act"] * 4, 1)
plan("kk", ["act"] * 4, 1, 2)
plan("vv", ["act"] * 4, 1, 2)
plan("gh", ["act"] * 4, 1)
plan("gates_falling", ["act"])
plan("gc", ["act"] * 8, 2)
plan("ln_mean", ["dve"])
plan("ga0", ["act"] * 4, 1)
plan("ln_var", ["dve"])
plan("ga1", ["act"] * 4, 1)
plan("pos", ["act"] * 2, 1)
plan("cmp1", ["act"] * 4, 1, 2)
plan("cmp2", ["act"] * 2)
plan("pw", ["dve"] * 8, 2)
plan("wo2", ["dve"] * 8, 2)
plan("xk", ["act"] * 8, 2)
plan("xv", ["act"] * 4, 2)
plan("xq", ["act"] * 8, 2)
plan("xo", ["dve"] * 8, 2)
plan("ffin", ["act", "act", "dve", "dve"] * (FT // 2), FT // 2, 2)
FFOUT = [4, 4, 4, 4, 4, 2]


def emptied(engine, g):
    return sum(e == engine for e in GROUPS[:g + 1])


CHUNK_DMAS += [1] * len(FFOUT)


def loaded_value(c):
    return 16 * sum(CHUNK_DMAS[i] for i in range(c % N_DENSE_SLOTS, c + 1, N_DENSE_SLOTS))


XP = {}
at = 0
for _stage, _n in (("norm1", KT), ("latents", 4), ("kpe", 1), ("dq", 4), ("dk", 4), ("qpe", 2), ("norm2", KT),
                   ("mix", KT), ("mem", KT), ("normx", KT), ("ffn", KT)):
    XP[_stage] = at
    at += _n
NORM_NO = {"norm1": 0, "norm2": 1, "mix": 2, "normx": 3, "ffn": 4}
ADA_GROUP = [FIRST["ada0"] + j for j in range(4)] + [FIRST[f"ada{(j - 2) // 2}"] + j % 2 for j in range(4, 12)]


def first_score(t):
    return t if t < 16 else 16 + 2 * (t - 16)


def unit_of(n):
    return n if n < 16 else 16 + (n - 16) // 2


MORE_SEMS = (["cmp_half", "sq_used", "onehot_loaded", "bias_rows_ready", "bias_stored", "pads_set", "conv_ready", "centred", "squared",
              "ln_var_ready", "ln_std_ready", "ln_scaled", "conv_act_ready", "cmp_bias_loaded", "cmp_scores_full",
              "cmp_shifted", "cmp_exp", "cmp_probs", "cmp_t_full", "cmp_t_ready", "bias_loaded0", "bias_loaded1",
              "nsa_full", "nsa_scored", "nsa_exp", "nsa_rcp", "nsa_probs", "nsa_t_full", "nsa_t_ready0", "nsa_t_ready1",
              "nsa_out", "nsa_kept", "mem_loaded", "x_full", "x_scored", "x_exp", "x_rcp", "x_probs", "x_t_full",
              "x_t_ready", "x_out", "x_kept", "ff_used", "ff_full", "x_ff", "fg2_loaded", "router_loaded", "zeros_set", "zeros_stored", "h2_ready", "h2_stored", "pool_step", "router_exp_in", "router_exp_out", "onehot_ready",
              "idx_ready", "ctl_ready", "gate_full", "up_full", "down_full", "xt_full", "xt_ready", "silu_ready",
              "a_ready", "at_full", "at_ready", "y_ready", "x_moe", "x_final"]
             + [f"{n}{b}" for n in ("gate_loaded", "up_loaded", "down_loaded", "xg_loaded", "y_stored") for b in range(2)]
             + [f"yg_loaded{n}" for n in range(4)]
             + ["ov_" + n for n in ("loaded", "gathered", "xt_full", "xt_ready", "up_full", "silu_ready", "a_ready",
                                    "at_full", "at_ready", "down_full", "y_ready", "stored")])


def build(nc, io):
    ctx = ExitStack()
    with ctx:
        def sb(name, shape, dt=F32):
            return ctx.enter_context(nc.sbuf_tensor(name, shape, dt))

        def sem(name):
            return ctx.enter_context(nc.semaphore(name))

        def dram(name, shape, dt=F32):
            return nc.dram_tensor(name, shape, dt, kind="Internal").ap()

        slots = sb("slots", [P, N_SLOTS * SLOT])
        X = sb("X", [P, TT, D])
        area = sb("area", [P, 22016])
        late = sb("late", [P, 1024])
        k1 = sb("k1", [P, K1_N])
        cols = sb("cols", [P, V_N])
        ones = sb("ones", [P, P])
        ones_d = sb("ones_d", [P, P])
        ctl = sb("ctl", [P, 8], I32)
        idx = sb("idx", [P, N_BLOCKS], I32)
        dest = sb("dest", [P, 2 * TT], I32)
        wts = sb("wts", [P, 2, TT])
        small = sb("small", [P, 320])
        banks = [ctx.enter_context(nc.psum_tensor(f"bank{i}", [P, C], F32)) for i in range(8)]

        def slot(i):
            return slots[:, i * SLOT:(i + 1) * SLOT]

        def A(off, n, *dims):
            v = area[:, off:off + n]
            return v.rearrange("p (a b) -> p a b", a=dims[0]) if dims else v

        def E(off, n, *dims):
            v = slots[:, 4 * SLOT + off:4 * SLOT + off + n]
            return v.rearrange("p (a b) -> p a b", a=dims[0]) if dims else v

        ID = k1[:, K1_ID:K1_ID + P]
        MASK = k1[:, K1_MASK:K1_N].rearrange("p (a b) -> p a b", a=TT)
        COS = late[:, K2_COS:K2_SIN].rearrange("p (t b) -> p t b", t=TT)
        SIN = late[:, K2_SIN:K2_LT].rearrange("p (t b) -> p t b", t=TT)
        LT = late[:, K2_LT:K2_IOTA]
        IOTA = late[:, K2_IOTA:K2_TOK]
        TOK = late[:, K2_TOK:K2_ANTI]
        ANTI = late[:, K2_ANTI:K2_N]

        def col(v, n):
            return cols[:, v + n:v + n + 1]

        hT = A(0, 4096, KT)
        mixT = A(0, 4096, KT)
        gate1, shift2, scale2, gate2 = (A(4096 + i * D, D) for i in range(4))
        modb = A(4096, 4096, 8)
        DV = A(8192, 2048, TT)
        CTN = A(10240, 2048, TT)
        KPE = A(12288, C)
        DQ = A(12800, 2048, 4)
        DK = A(14848, 2048, 4)
        Z = A(16896, 2048, TT)
        QN = A(16896, 2048, 4)
        RQ = A(18944, 2048, TT)
        KN = A(18944, 2048, 4)
        RT = A(20992, C)
        QPE = A(20992, 1024, 2)
        early = E(0, 2048, 4)
        ada_acc = E(2048, 2048, 4)
        XN1 = E(4096, 4096, TT)
        QRT = E(4096, 1024, TT)
        PT = [E(0, 2048, TT), E(2048, 2048, TT)]
        PB = E(4096, 2048, 4)
        VM = E(6144, 2048, TT)
        A1, B1, A2, B2 = (small[:, i * 8:i * 8 + 8] for i in range(4))
        ssq = small[:, 32:48]
        rstd = small[:, 48:64]
        csil = small[:, 64:72]
        lamv = small[:, 72:80]
        nmx = small[:, 80:96]
        sums = small[:, 96:112]
        rcp = small[:, 112:128]
        badar = A(21504, C)
        lamin = A(14848, 256)
        SUBS = A(16896, 2048, 4)
        WOT = E(0, 1024, 2)
        varc, var4, stdc, std4 = small[:, 128:136], small[:, 136:140], small[:, 140:148], small[:, 148:152]

        XN2 = A(8192, 4096, TT)
        XN3 = A(0, 4096, TT)
        h2T = A(0, 4096, KT)
        H2 = A(12288, 4096, TT)
        G2B = A(20992, D)
        FGB = A(19968, D)
        WR = A(18944, 288, KT)
        BR = A(19300, 36)
        LO = A(4096, 1024, 8)
        HI = A(19364, 8 * N_BLOCKS, 8)
        XG = A(0, 2048, 2)
        XT = [A(2048, 1024, KT), A(3072, 1024, KT)]
        SG = A(4096, 1024, 2)
        AA = A(5120, 1024, 2)
        AT = [A(6144, 512, 4), A(6656, 512, 4)]
        Y = A(8192, 2048, 2)
        YG = A(10240, 4096, 4)

        OH = A(14336, NG)
        RB = A(16000, NH)
        BROW = A(16400, NG)
        XN4 = A(8432, 4096, TT)
        V = A(4096, KT * VW_, KT)
        GC = A(4096, 4096, KT)
        CV = A(8432, 4096, KT)
        Q = A(12528, 4096, KT)
        KK = [A(16624, 2048, 4), A(18672, 2048, 4)]
        VV = E(0, 2048, TT)
        KC, VC = E(2048, 1024, 2), E(3072, 1024, 2)
        GA = E(4096, 4096, KT)
        GS = A(20720, TT * 48, TT)
        GRISE = A(21600, TT * 48, TT)
        KCT = A(20912, 4 * NCMP, 4)
        VC4 = A(21040, 4 * 64, 4)
        ZC = A(21296, 2 * 124, 2)
        POSB = A(21544, 2)
        SQ = [late[:, 0:C], late[:, C:2 * C]]
        RSQ = late[:, 0:C]
        PN = A(0, 2048, TT)
        PTN = [A(2048, 2048, TT), A(8432, 2048, TT)]
        PCT = A(10480, 2048, TT)
        BCT = E(2048, 2048, NH)
        TMP = E(2048, C)
        BT = [late[:, 0:C], late[:, C:2 * C]]
        MTOK = E(0, 2048, 2)
        MT = E(2048, 2048, KT)
        XK = E(4096, 2048, KT)
        XV = E(6144, 2048, 2)
        OT = A(4096, 4096, KT)
        XQ = A(12528, 4096, KT)
        PX = A(16624, 1024, 4)
        PTX = [A(17648, 1024, 2), A(18672, 1024, 2)]
        GT = A(8432, FT * C, FT)
        SA = A(19696, 2048, 4)
        FG2 = A(4096, D)

        g_dram = dram("bias_falling", [NH, NG])
        h2_dram = dram("h2_rows", [S, D])
        ys_dram = dram("expert_rows", [N_BLOCKS * CAP, D])

        names = ["w_loaded0", "w_loaded1", "w_loaded2", "w_loaded3", "x_loaded", "consts", "bada", "lamload",
                 "proj_done", "act_emptied", "dve_emptied", "ones_set", "ada_acc", "mod_ready",
                 "act_step", "dve_step", "csil_ready",
                 "ssq_ready", "var_ready", "std_ready", "xn_ready", "xpose_full", "bank6_emptied", "bank7_emptied",
                 "latent_ssq", "latent_var", "latent_std", "latents_ready", "rope_ready",
                 "lam_ready", "lam_exp", "scores_full", "exp_done", "max_ready", "rcp_ready", "scaled",
                 "probs_mla", "probs_diff", "pt_full", "pt_ready", "pv_full", "pv_emptied",
                 "sub_squares", "sub_full", "sub_var", "sub_std", "sub_ready", "x_ready", "out_done"] + MORE_SEMS
        s = {n: sem(n) for n in names}
        w_loaded = [s[f"w_loaded{i}"] for i in range(N_DENSE_SLOTS)]
        xpose_emptied = [s["bank6_emptied"], s["bank7_emptied"]]
        emptied_sem = {"act": s["act_emptied"], "dve": s["dve_emptied"]}
        block = ctx.enter_context(nc.Block())

        def at_least(engine, semaphore, value):
            if not isinstance(value, int) or value > 0:
                engine.wait_ge(semaphore, value)

        def RS(off, n):
            return A(16384 + off, n)

        def RM(t):
            return RS(672 + 32 * t, 32)

        def R3(off, *dims):
            return bass.AP(area, 16384 + off, [[22016, P]] + [list(d) for d in dims])

        def w3(ap):
            return ap.rearrange("(k p) n -> p k n", p=P)

        ADA_PARTS = [[0, 1, 2, 3], [4, 5], [6, 7], [8, 9], [10, 11]]
        CHUNK_NO = {}
        at = 0
        for name, n in (("ada0", 4), ("c", 1), ("ada1", 2), ("kpe", 1), ("dq", 1), ("ada2", 2), ("dk", 1), ("ada3", 2),
                        ("dv", 1), ("ada4", 2), ("up", 1), ("wo", 2),
                        ("glu_g", 2), ("glu_a", 2), ("q2", 2), ("kvc", 1), ("kk", 1), ("vv", 1), ("gh", 1), ("gc", 2),
                        ("ga0", 1), ("ga1", 1), ("pos", 1), ("cmp1", 1), ("pw", 2), ("wo2", 2), ("xk", 2), ("xv", 2), ("xq", 2),
                        ("xo", 2), ("ffin", FT // 2), ("ffout", len(FFOUT))):
            CHUNK_NO[name] = at
            at += n

        @block.sync
        def _(sp):
            def chunk(c, loads):
                prev = c - N_DENSE_SLOTS
                if prev >= len(CHUNK_LAST):
                    sp.wait_ge(s["ff_used"], prev - len(CHUNK_LAST) + 1)
                elif prev >= 0 and not B1_CHUNKS <= c < B1_CHUNKS + N_DENSE_SLOTS:
                    sp.wait_ge(s["proj_done"], CHUNK_LAST[prev] + 1)
                i = c % N_DENSE_SLOTS
                for off, src in loads:
                    k, n = src.shape[1], src.shape[2]
                    dst = slot(i)[:, off:off + k * n].rearrange("p (k n) -> p k n", k=k)
                    sp.dma_start(dst, src).then_inc(w_loaded[i], 16)

            w_ada, w_in, w_out = w3(io["w_ada"][0]), w3(io["w_in"][0]), w3(io["w_out"][0])
            sp.dma_start(X[:], io["x"][0].rearrange("(t p) d -> p t d", p=P)).then_inc(s["x_loaded"], 16)

            def ada(part):
                for n, j in enumerate(ADA_PARTS[part]):
                    chunk(CHUNK_NO[f"ada{part}"] + n, [(0, w_ada[:, :, j * C:(j + 1) * C])])

            ada(0)
            sp.wait_ge(s["zeros_set"], 1)
            sp.dma_start(ys_dram[N_EXP * CAP:, :].rearrange("(b p) d -> p b d", p=P),
                         bass.AP(area, 8192, [[22016, P], [0, N_OVER], [1, D]])).then_inc(s["zeros_stored"], 16)
            chunk(CHUNK_NO["c"], [(0, w_in[:, :, 0:512])])
            ada(1)
            chunk(CHUNK_NO["kpe"], [(0, w_in[:, :, 512:576])])
            chunk(CHUNK_NO["dq"], [(0, w_in[:, :, 576:1088])])
            ada(2)
            chunk(CHUNK_NO["dk"], [(0, w_in[:, :, 1088:1600])])
            ada(3)
            chunk(CHUNK_NO["dv"], [(0, w_in[:, :, 1600:2112])])
            ada(4)
            chunk(CHUNK_NO["up"], [(0, w3(io["w_q_up"][0])), (2 * 768, w3(io["w_kv_up"][0]))])
            for n in range(2):
                chunk(CHUNK_NO["wo"] + n, [(0, w_out[:, :, n * C:(n + 1) * C])])
            sp.wait_ge(s["pv_emptied"], 8)
            sp.wait_ge(s["sub_ready"], 4)
            sp.dma_start(G2B, io["norm2_g"][0].partition_broadcast(P)).then_inc(s["router_loaded"], 16)
            sp.dma_start(FGB, io["final_norm_g"].partition_broadcast(P)).then_inc(s["router_loaded"], 16)
            sp.dma_start(WR[:, :, 0:4], w3(io["w_router_group"][0])).then_inc(s["router_loaded"], 16)
            sp.dma_start(WR[:, :, 4:36], w3(io["w_router_expert"][0])).then_inc(s["router_loaded"], 16)
            sp.dma_start(BR, io["b_router"].partition_broadcast(P)).then_inc(s["router_loaded"], 16)

            wg = io["w_expert_gate"][0].rearrange("e (k p) n -> p e k n", p=P)
            wu = io["w_expert_up"][0].rearrange("e (k p) n -> p e k n", p=P)
            wd = io["w_expert_down"][0].rearrange("e (k p) n -> p e k n", p=P)

            def expert_weight(i, w, e, loaded):
                k, n = w.shape[2], w.shape[3]
                sp.dma_start(slot(i).rearrange("p (a k n) -> p a k n", a=1, k=k), w[:, bass.ds(e, 1), :, :]
                             ).then_inc(loaded, 16)

            sp.wait_ge(s["proj_done"], FIRST["wo"])
            expert_weight(0, wg, 0, s["gate_loaded0"])
            expert_weight(1, wu, 0, s["up_loaded0"])
            sp.wait_ge(s["proj_done"], FIRST["wo"] + 8)
            expert_weight(2, wd, 0, s["down_loaded0"])
            expert_weight(3, wg, 1, s["gate_loaded1"])
            sp.wait_ge(s["x_ready"], 8)
            expert_weight(4, wu, 1, s["up_loaded1"])
            expert_weight(5, wd, 1, s["down_loaded1"])
            for t in range(TT):
                sp.wait_ge(s["h2_ready"], t + 1)
                sp.dma_start(h2_dram[t * P:(t + 1) * P, :], H2[:, t, :]).then_inc(s["h2_stored"], 16)
            with sp.Fori(1, N_EXP // 2) as it:
                for r in range(2):
                    e = 2 * it + r
                    sp.wait_ge(s["gate_full"], e - 1)
                    expert_weight(3 * r, wg, e, s[f"gate_loaded{r}"])
                    sp.wait_ge(s["up_full"], e - 1)
                    expert_weight(3 * r + 1, wu, e, s[f"up_loaded{r}"])
                    sp.wait_ge(s["down_full"], 2 * e - 2)
                    expert_weight(3 * r + 2, wd, e, s[f"down_loaded{r}"])
            sp.wait_ge(s["down_full"], 2 * N_EXP)
            sp.wait_ge(s["ctl_ready"], 1)
            n_over = sp.value_load(ctl[0:1, 7:8], min_val=0, max_val=N_OVER)
            with sp.If(n_over > 0):
                with sp.Fori(0, N_OVER) as j:
                    sp.wait_ge(s["ov_down_full"], 2 * j)
                    e = sp.value_load(ctl[0:1, bass.ds(j, 1)], min_val=0, max_val=N_EXP - 1)
                    expert_weight(0, wg, e, s["ov_loaded"])
                    expert_weight(1, wu, e, s["ov_loaded"])
                    expert_weight(2, wd, e, s["ov_loaded"])
                sp.wait_ge(s["ov_down_full"], 2 * N_OVER)
            sp.dma_start(OH[0:33, :], io["onehot"]).then_inc(s["onehot_loaded"], 16)
            sp.dma_start(RB[0:32, :], io["rel_bias_2"]).then_inc(s["onehot_loaded"], 16)
            w2, pw, wo2 = w3(io["w_in_2"][0]), w3(io["conv_pw_w_2"][0]), w3(io["w_out_2"][0])
            xq, xkv, xo = w3(io["xq_w_2"][0]), w3(io["xkv_w_2"][0]), w3(io["xo_w_2"][0])
            ffin, ffout = w3(io["ffn_in_w_2"][0]), w3(io["ffn_out_w_2"][0])

            def halves(stage, w, first):
                for n in range(2):
                    chunk(CHUNK_NO[stage] + n, [(0, w[:, :, first + n * C:first + (n + 1) * C])])

            halves("glu_g", w2, 1024)
            halves("glu_a", w2, 0)
            sp.wait_ge(s["act_emptied"], emptied("act", FIRST["toep"] + 2))
            sp.dma_start(g_dram, BROW[0:NH, :]).then_inc(s["bias_stored"], 16)
            halves("q2", w2, 2048)
            chunk(CHUNK_NO["kvc"], [(0, w2[:, :, 3072:3584])])

            def two(stage, first, second):
                c = CHUNK_NO[stage]
                sp.wait_ge(s["proj_done"], CHUNK_LAST[c - N_DENSE_SLOTS] + 1)
                for n, at in enumerate((first, second)):
                    sp.dma_start(slot(c % 4).rearrange("p (k n) -> p k n", k=KT)[:, :, n * 256:n * 256 + 256],
                                 w2[:, :, at:at + 256]).then_inc(w_loaded[c % N_DENSE_SLOTS], 16)

            two("kk", 3584, 4096)
            two("vv", 3840, 4352)
            chunk(CHUNK_NO["gh"], [(0, w2[:, :, 4608:4656])])
            halves("gc", w2, 4656)
            chunk(CHUNK_NO["ga0"], [(0, w2[:, :, 5680:6192])])
            chunk(CHUNK_NO["ga1"], [(0, w2[:, :, 6192:6704])])
            chunk(CHUNK_NO["pos"], [(0, io["cmp_w1_flat"])])
            c = CHUNK_NO["cmp1"]
            sp.wait_ge(s["proj_done"], CHUNK_LAST[c - N_DENSE_SLOTS] + 1)
            for a in range(2):
                sp.dma_start(slot(c % N_DENSE_SLOTS)[64 * a:64 * a + 64, :], io["cmp_w1"][0]
                             ).then_inc(w_loaded[c % N_DENSE_SLOTS], 16)
            halves("pw", pw, 0)
            sp.wait_ge(s["proj_done"], FIRST["cmp1"] + 4)
            sp.wait_ge(s["bias_stored"], 16)
            for i in range(TT):
                sp.dma_start(BCT[32 * i:32 * i + 32, :, :],
                             bass.AP(g_dram.tensor, 415 - i * P, [[16, NCMP], [NG, NH], [1, P]])
                             ).then_inc(s["cmp_bias_loaded"], 16)

            def bias_tile(h):
                sp.dma_start(BT[h % 2], bass.AP(g_dram.tensor, h * NG, [[1, P], [1, C]])
                             ).then_inc(s[f"bias_loaded{h % 2}"], 16)

            sp.wait_ge(s["ln_scaled"], KT)
            bias_tile(0)
            bias_tile(1)
            halves("wo2", wo2, 0)
            halves("xk", xkv, 0)
            for h in range(2, NH):
                sp.wait_ge(s["nsa_scored"], 8 * (h - 1))
                bias_tile(h)
            sp.wait_ge(s["nsa_kept"], NH // 2)
            sp.dma_start(MTOK, io["mem_2"][0].rearrange("(t p) d -> p t d", p=P)).then_inc(s["mem_loaded"], 16)
            halves("xv", xkv, 1024)
            halves("xq", xq, 0)
            halves("xo", xo, 0)
            for j in range(FT // 2):
                if j == 2:
                    sp.wait_ge(s["proj_done"], FIRST["xo"] + 8)
                    sp.dma_start(FG2, io["final_norm_g_2"].partition_broadcast(P)).then_inc(s["fg2_loaded"], 16)
                chunk(CHUNK_NO["ffin"] + j, [(0, ffin[:, :, j * 256:j * 256 + 256]),
                                             (2048, ffin[:, :, D_FF + j * 256:D_FF + j * 256 + 256])])
            k0 = 0
            for n, k in enumerate(FFOUT):
                chunk(CHUNK_NO["ffout"] + n, [(0, ffout[:, k0:k0 + k, :])])
                k0 += k
            for t in range(TT):
                sp.wait_ge(s["x_final"], TT + t + 1)
                sp.dma_start(io["out"][0, t * P:(t + 1) * P, :], X[:, t, :]).then_inc(s["out_done"], 16)
            sp.wait_ge(s["out_done"], 16 * TT)

        @block.tensor
        def _(pe):
            def bank_of(g):
                if g >= 4:
                    engine = GROUPS[g - 4]
                    pe.wait_ge(emptied_sem[engine], emptied(engine, g - 4))
                return banks[g % 4]

            def all_emptied(g):
                for engine in ("act", "dve"):
                    pe.wait_ge(emptied_sem[engine], emptied(engine, g - 1))

            def loaded(c):
                pe.wait_ge(w_loaded[c % N_DENSE_SLOTS], loaded_value(c))
                return slot(c % N_DENSE_SLOTS)

            def accumulate(out, pairs):
                for n, (lhsT, rhs) in enumerate(pairs):
                    last = nc.tensor.matmul(out, lhsT, rhs, start=(n == 0), stop=(n == len(pairs) - 1))
                return last

            def token_major(stage, xT, n_cols, chunk_no, tiles=TT, first=0):
                w = loaded(chunk_no)[:, 0:KT * n_cols].rearrange("p (k n) -> p k n", k=KT)
                for t in range(tiles):
                    g = FIRST[stage] + first + t
                    accumulate(bank_of(g)[:, 0:n_cols],
                               [(xT[:, k, t * P:(t + 1) * P], w[:, k, :]) for k in range(KT)]
                               ).then_inc(s["proj_done"], 1)

            def feature_major(stage, xT, chunk_no, first=0, n_tiles=4, tokens=S):
                w = loaded(chunk_no)[:, 0:KT * n_tiles * P].rearrange("p (k n) -> p k n", k=KT)
                for j in range(n_tiles):
                    g = FIRST[stage] + first + j
                    accumulate(bank_of(g)[:, 0:tokens],
                               [(w[:, k, j * P:(j + 1) * P], xT[:, k, 0:tokens]) for k in range(KT)]
                               ).then_inc(s["proj_done"], 1)

            def transposes(n, pieces):
                if n >= 2:
                    pe.wait_ge(xpose_emptied[n % 2], n // 2)
                for c0, src in pieces:
                    rows = src.shape[1]
                    last = nc.tensor.transpose(banks[6 + n % 2][0:rows, c0:c0 + P], src, ID)
                last.then_inc(s["xpose_full"], 1)

            def transpose_tokens(stage, XT, n_tiles, width=P, c_first=0):
                for c in range(n_tiles):
                    transposes(XP[stage] + c, [(t * P, XT[:, t, c * width:(c + 1) * width]) for t in range(TT)])

            def transposed_emptied(n):
                pe.wait_ge(xpose_emptied[0], (n + 1) // 2)
                pe.wait_ge(xpose_emptied[1], n // 2)

            def norm_transposes(n, XN):
                pe.wait_ge(s["xn_ready"], TT * (NORM_NO[n] + 1))
                transpose_tokens(n, XN, KT)
                transposed_emptied(XP[n] + KT)
            def ada(part):
                for n, j in enumerate(ADA_PARTS[part]):
                    g = FIRST[f"ada{part}"] + n
                    pe.wait_ge(s["ada_acc"], j + 1)
                    bank = bank_of(g)
                    b = 2 * (j % 2)
                    accumulate(bank[:, :], [(ones[:, :], ada_acc[:, b, :]), (ones[:, :], ada_acc[:, b + 1, :]),
                                            (ID[0:12, j:j + 1].to_broadcast([12, P]), badar[0:12, 0:C])]
                               ).then_inc(s["proj_done"], 1)

            def mod_columns(stage, rows):
                bank = bank_of(FIRST[stage])
                for n in range(16):
                    row = rows[n // 4]
                    last = nc.tensor.matmul(bank[:, n:n + 1], row[0:1, (n % 4) * P:(n % 4 + 1) * P], ones[0:1, 0:1],
                                            start=True, stop=True)
                last.then_inc(s["proj_done"], 1)

            pe.wait_ge(s["consts"], 48)
            pe.wait_ge(s["ones_set"], 1)
            pe.wait_ge(s["bada"], 16)
            ada(0)
            pe.wait_ge(s["act_emptied"], emptied("act", FIRST["modcols"] - 1))
            mod_columns("modcols", [early[:, i, :] for i in range(4)])
            norm_transposes("norm1", XN1)
            token_major("c", hT, C, CHUNK_NO["c"])
            ada(1)
            token_major("kpe", hT, 64, CHUNK_NO["kpe"])
            pe.wait_ge(s["latents_ready"], TT)
            transpose_tokens("latents", Z, 4)
            token_major("dq", hT, C, CHUNK_NO["dq"])
            pe.wait_ge(s["rope_ready"], TT)
            transpose_tokens("kpe", RQ, 1, 64)
            ada(2)
            pe.wait_ge(s["rope_ready"], 2 * TT)
            transpose_tokens("dq", Z, 4)
            token_major("dk", hT, C, CHUNK_NO["dk"])
            ada(3)
            pe.wait_ge(s["rope_ready"], 3 * TT)
            transpose_tokens("dk", RQ, 4)
            token_major("dv", hT, C, CHUNK_NO["dv"])
            ada(4)
            pe.wait_ge(s["act_emptied"], emptied("act", FIRST["modcols2"] - 1))
            mod_columns("modcols2", [modb[:, i, :] for i in (2, 3, 4, 5)])
            transposed_emptied(XP["dk"] + 4)
            w = loaded(CHUNK_NO["up"])
            wq = w[:, 0:1536].rearrange("p (k h n) -> p k h n", k=2, n=192)
            wkv = w[:, 1536:1536 + 2048].rearrange("p (k h n) -> p k h n", k=2, n=256)
            g = FIRST["up"]
            for h in range(4):
                accumulate(bank_of(g)[:, :], [(wq[:, k, h, 0:P], CTN[:, k, :]) for k in range(2)]
                           ).then_inc(s["proj_done"], 1)
                g += 1
            for h in range(4):
                accumulate(bank_of(g)[:, :], [(wkv[:, k, h, 0:P], CTN[:, 2 + k, :]) for k in range(2)]
                           ).then_inc(s["proj_done"], 1)
                g += 1
            for t in range(TT):
                accumulate(bank_of(g)[:, :].rearrange("p (h n) -> p h n", h=4),
                           [(CTN[:, 2 + k, t * P:(t + 1) * P], wkv[:, k, :, P:2 * P]) for k in range(2)]
                           ).then_inc(s["proj_done"], 1)
                g += 1
            for t in range(TT):
                accumulate(bank_of(g)[:, 0:256].rearrange("p (h n) -> p h n", h=4),
                           [(CTN[:, k, t * P:(t + 1) * P], wq[:, k, :, P:192]) for k in range(2)]
                           ).then_inc(s["proj_done"], 1)
                g += 1
            pe.wait_ge(s["rope_ready"], 4 * TT)
            transpose_tokens("qpe", QRT, 2)

            all_emptied(g)
            transposed_emptied(XP["qpe"] + 2)

            def scores(t):
                h, i = t // TT % 4, t % TT
                if t < 16:
                    n, a = t, 64 * (h % 2)
                    if n >= 4:
                        pe.wait_ge(s["exp_done"], n - 3)
                    accumulate(banks[2 + n % 4][:, :],
                               [(QN[:, h, i * P:(i + 1) * P], KN[:, h, :]),
                                (QPE[a:a + 64, h // 2, i * P:(i + 1) * P], KPE[a:a + 64, :])]
                               ).then_inc(s["scores_full"], 1)
                else:
                    for half in range(2):
                        n, a = 16 + 2 * (t - 16) + half, 64 * half
                        pe.wait_ge(s["exp_done"], n - 3)
                        accumulate(banks[2 + n % 4][:, :], [(DQ[a:a + 64, h, i * P:(i + 1) * P], DK[a:a + 64, h, :])]
                                   ).then_inc(s["scores_full"], 1)

            def outputs(h):
                pe.wait_ge(s["pt_ready"], TT * (h + 1))
                if h >= 2:
                    pe.wait_ge(s["pv_emptied"], h - 1)
                V, c0 = (VM, h * P) if h < 4 else (DV, (h - 4) * P)
                accumulate(banks[h % 2][:, :], [(V[:, j, c0:c0 + P], PT[h % 2][:, j, :]) for j in range(TT)]
                           ).then_inc(s["pv_full"], 1)

            scores(0)
            for t in range(32):
                if t + 1 < 32:
                    scores(t + 1)
                if t < 16:
                    pe.wait_ge(s["probs_mla"], t + 1)
                else:
                    pe.wait_ge(s["probs_diff"], t - 15)
                if t >= 2:
                    pe.wait_ge(s["pt_ready"], t - 1)
                pb = PB[:, first_score(t) % 4, :]
                for j in range(TT):
                    last = nc.tensor.transpose(banks[6 + t % 2][:, j * P:(j + 1) * P], pb[:, j * P:(j + 1) * P], ID)
                last.then_inc(s["pt_full"], 1)
                if t >= 4 and t % TT == 0:
                    outputs(t // TT - 1)
            outputs(7)
            for h in range(4):
                pe.wait_ge(s["sub_squares"], h + 1)
                accumulate(banks[2 + h][:, :], [(ones[:, :], SUBS[:, h, :])]).then_inc(s["sub_full"], 1)

            pe.wait_ge(s["pv_emptied"], 8)
            pe.wait_ge(s["sub_ready"], 4)
            for n in range(2):
                token_major("wo", mixT, C, CHUNK_NO["wo"] + n, first=4 * n)
            pe.wait_ge(s["pt_ready"], 32)
            norm_transposes("norm2", XN2)
            pe.wait_ge(s["router_loaded"], 80)
            for t in range(TT):
                g = FIRST["router"] + t
                accumulate(bank_of(g)[:, 0:36], [(h2T[:, k, t * P:(t + 1) * P], WR[:, k, :]) for k in range(KT)]
                           ).then_inc(s["proj_done"], 1)
            pe.wait_ge(s["onehot_ready"], 1)
            bank = bank_of(FIRST["rank"])
            for t in range(TT):
                accumulate(bank[:, t * 32:t * 32 + 32],
                           [(LT if u == t else ones[:, :], RM(u)) for u in range(t + 1)])
            accumulate(bank[0:32, 128:256], [(RM(u), ones[:, :]) for u in range(TT)]).then_inc(s["proj_done"], 1)
            pe.wait_ge(s["onehot_ready"], 2)
            bank = bank_of(FIRST["over"])
            accumulate(bank[:, 0:32], [(RS(1056, P)[0:32, :], LT[0:32, 0:32])])
            accumulate(bank[:, 32:64], [(RS(1056, P)[0:32, :], ID[0:32, 0:32])]).then_inc(s["proj_done"], 1)
            pe.wait_ge(s["onehot_ready"], 3)
            accumulate(bank_of(FIRST["slots"])[:, 0:N_BLOCKS], [(LO[:, n, :], HI[:, n, :]) for n in range(8)]
                       ).then_inc(s["proj_done"], 1)

            all_emptied(FIRST["slots"] + 1)
            transposed_emptied(XP["norm2"] + KT)

            def moe_transpose_x(e, it, b):
                at_least(pe, s[f"xg_loaded{b}"], 16 * (it + 1))
                at_least(pe, s["xt_ready"], 2 * e)
                at_least(pe, s["at_ready"], e - 1)
                for half in range(2):
                    for k in range(4):
                        c = 4 * half + k
                        last = nc.tensor.transpose(banks[6 + half][:, k * P:(k + 1) * P], XG[:, b, c * P:(c + 1) * P],
                                                   ID)
                    last.then_inc(s["xt_full"], 1)

            def moe_up(e, it, b):
                pe.wait_ge(s["xt_ready"], 2 * e + 2)
                at_least(pe, s["a_ready"], e - 1)
                for which, loaded_sem, full_sem in ((0, f"gate_loaded{b}", "gate_full"), (1, f"up_loaded{b}", "up_full")):
                    pe.wait_ge(s[loaded_sem], 16 * (it + 1))
                    w = slot(3 * b + which).rearrange("p (k n) -> p k n", k=KT)
                    accumulate(banks[2 * which + b][:, :], [(XT[b][:, k, :], w[:, k, :]) for k in range(KT)]
                               ).then_inc(s[full_sem], 1)

            def moe_transpose_a(e, b):
                pe.wait_ge(s["a_ready"], e + 1)
                at_least(pe, s["at_ready"], e)
                for k in range(4):
                    last = nc.tensor.transpose(banks[7][:, k * P:(k + 1) * P], AA[:, b, k * P:(k + 1) * P], ID)
                last.then_inc(s["at_full"], 1)

            def moe_down(e, it, b):
                pe.wait_ge(s["at_ready"], e + 1)
                pe.wait_ge(s[f"down_loaded{b}"], 16 * (it + 1))
                w = slot(3 * b + 2).rearrange("p (k n) -> p k n", k=4)
                for half in range(2):
                    at_least(pe, s["y_ready"], 2 * e - 1 + half)
                    accumulate(banks[4 + half][:, :],
                               [(AT[b][:, k, :], w[:, k, half * C:(half + 1) * C]) for k in range(4)]
                               ).then_inc(s["down_full"], 1)

            def moe_step(it, r):
                e, b = 2 * it + r, r % 2
                pe.wait_ge(s["xt_ready"], 2 * e + 2)
                moe_transpose_a(e - 1, 1 - b)
                moe_up(e, it + r // 2, b)
                moe_transpose_x(e + 1, it + (r + 1) // 2, 1 - b)
                moe_down(e - 1, it + (r - 1) // 2, 1 - b)

            moe_transpose_x(0, 0, 0)
            moe_up(0, 0, 0)
            moe_transpose_x(1, 0, 1)
            moe_step(0, 1)
            moe_step(0, 2)
            with pe.Fori(1, N_EXP // 2 - 1) as it:
                moe_step(it, 1)
                moe_step(it, 2)
            e = N_EXP - 1
            pe.wait_ge(s["xt_ready"], 2 * N_EXP)
            moe_transpose_a(e - 1, 0)
            moe_up(e, e // 2, 1)
            moe_down(e - 1, e // 2, 0)
            moe_transpose_a(e, 1)
            moe_down(e, e // 2, 1)

            pe.wait_ge(s["y_ready"], 2 * N_EXP)
            pe.wait_ge(s["ctl_ready"], 1)
            n_over = pe.value_load(ctl[0:1, 7:8], min_val=0, max_val=N_OVER)
            with pe.If(n_over > 0):
                with pe.Fori(0, N_OVER) as j:
                    pe.wait_ge(s["ov_gathered"], 16 * j + 16)
                    for half in range(2):
                        for k in range(4):
                            c = 4 * half + k
                            last = nc.tensor.transpose(banks[6 + half][:, k * P:(k + 1) * P],
                                                       XG[:, 0, c * P:(c + 1) * P], ID)
                        last.then_inc(s["ov_xt_full"], 1)
                    pe.wait_ge(s["ov_xt_ready"], 2 * j + 2)
                    pe.wait_ge(s["ov_loaded"], 48 * j + 48)
                    for which in range(2):
                        w = slot(which).rearrange("p (k n) -> p k n", k=KT)
                        accumulate(banks[2 * which][:, :], [(XT[0][:, k, :], w[:, k, :]) for k in range(KT)]
                                   ).then_inc(s["ov_up_full"], 1)
                    pe.wait_ge(s["ov_a_ready"], j + 1)
                    for k in range(4):
                        last = nc.tensor.transpose(banks[7][:, k * P:(k + 1) * P], AA[:, 0, k * P:(k + 1) * P], ID)
                    last.then_inc(s["ov_at_full"], 1)
                    pe.wait_ge(s["ov_at_ready"], j + 1)
                    w = slot(2).rearrange("p (k n) -> p k n", k=4)
                    for half in range(2):
                        accumulate(banks[4 + half][:, :],
                                   [(AT[0][:, k, :], w[:, k, half * C:(half + 1) * C]) for k in range(4)]
                                   ).then_inc(s["ov_down_full"], 1)
                    pe.wait_ge(s["ov_y_ready"], 2 * j + 2)
            pe.wait_ge(s["onehot_loaded"], 32)
            pe.wait_ge(s["bias_rows_ready"], 1)
            for n in range(3):
                width = C if n < 2 else NG - 2 * C
                g = FIRST["toep"] + n
                accumulate(bank_of(g)[0:NH, 0:width], [(RB[0:33, :], OH[0:33, n * C:n * C + width])]
                           ).then_inc(s["proj_done"], 1)
            norm_transposes("mix", XN4)
            for n in range(2):
                feature_major("glu_g", hT, CHUNK_NO["glu_g"] + n, 4 * n)
            for n in range(2):
                feature_major("glu_a", hT, CHUNK_NO["glu_a"] + n, 4 * n)
            for n in range(2):
                feature_major("q2", hT, CHUNK_NO["q2"] + n, 4 * n)
            feature_major("kvc", hT, CHUNK_NO["kvc"])
            feature_major("kk", hT, CHUNK_NO["kk"])
            token_major("vv", hT, C, CHUNK_NO["vv"])
            token_major("gh", hT, 48, CHUNK_NO["gh"])
            pe.wait_ge(s["act_emptied"], emptied("act", FIRST["gates_falling"] - 1))
            for t in range(TT):
                last = nc.tensor.matmul(bank_of(FIRST["gates_falling"])[:, t * 48:(t + 1) * 48], ANTI, GRISE[:, t, :],
                                        start=True, stop=True)
            last.then_inc(s["proj_done"], 1)
            for n in range(2):
                feature_major("gc", hT, CHUNK_NO["gc"] + n, 4 * n)
            pe.wait_ge(s["conv_ready"], KT)
            accumulate(bank_of(FIRST["ln_mean"])[:, :], [(ones_d[:, :], CV[:, c, :]) for c in range(KT)]
                       ).then_inc(s["proj_done"], 1)
            feature_major("ga0", hT, CHUNK_NO["ga0"])
            bank = bank_of(FIRST["ln_var"])
            for c in range(KT):
                pe.wait_ge(s["squared"], c + 1)
                last = nc.tensor.matmul(bank[:, :], ones_d[:, :], SQ[c % 2], start=(c == 0), stop=(c == KT - 1))
                last.then_inc(s["proj_done" if c == KT - 1 else "sq_used"], 1)
            feature_major("ga1", hT, CHUNK_NO["ga1"])
            w = loaded(CHUNK_NO["pos"])[:, 0:2048].rearrange("p (a j e) -> p a j e", a=2, e=64)
            for a in range(2):
                accumulate(bank_of(FIRST["pos"] + a)[0:64, 0:1],
                           [(w[:, a, j, :], cols[:, V_POS + 16 * a + j:V_POS + 16 * a + j + 1]) for j in range(16)]
                           ).then_inc(s["proj_done"], 1)
            w = loaded(CHUNK_NO["cmp1"]).rearrange("p (a l e) -> p a l e", a=2, e=64)
            for a in range(2):
                for half in range(2):
                    r = slice(64 * half, 64 * half + 64)
                    bank = bank_of(FIRST["cmp1"] + 2 * a + half)
                    off = 4 * SLOT + 2048 + 1024 * a
                    accumulate(bank[0:64, 0:62].rearrange("p (c n) -> p c n", c=2),
                               [(w[r, a, l, :], bass.AP(slots, 64 * half * N_SLOTS * SLOT + off + l,
                                                        [[N_SLOTS * SLOT, 64], [C, 2], [16, 31]])) for l in range(32)]
                               ).then_inc(s["proj_done"], 1)
            pe.wait_ge(s["act_emptied"], emptied("act", FIRST["cmp1"] + 3))
            accumulate(bank_of(FIRST["cmp2"])[0:64, 0:124], [(cols[0:64, V_W2:V_W2 + 64], ZC[0:64, 0, :])]
                       ).then_inc(s["proj_done"], 1)
            bank = bank_of(FIRST["cmp2"] + 1)
            for u in range(4):
                last = nc.tensor.matmul(bank[0:31, u * 64:u * 64 + 64], ZC[0:64, 1, u * 31:u * 31 + 31],
                                        cols[0:64, V_W2 + 64:V_W2 + P], start=True, stop=True)
            last.then_inc(s["proj_done"], 1)
            transposed_emptied(XP["mix"] + KT)
            pe.wait_ge(s["act_emptied"], emptied("act", FIRST["cmp2"] + 1))
            pe.wait_ge(s["cmp_bias_loaded"], 64)
            for a in range(2):
                if a:
                    pe.wait_ge(s["cmp_half"], 1)
                for i in range(TT):
                    for h in range(a, NH, 2):
                        r, u = slice(64 * a, 64 * a + 64), 2 * (h // 4 % 2) + h // 8
                        last = nc.tensor.matmul(banks[4 + i][:, h * NCMP:(h + 1) * NCMP],
                                                Q[r, h // 2, i * P:(i + 1) * P], KCT[r, u, :], start=(h == 0), stop=False)
                if a == 0:
                    last.then_inc(s["cmp_half"], 1)
            for i in range(TT):
                r = slice(32 * i, 32 * i + 32)
                for h in range(NH):
                    last = nc.tensor.matmul(banks[4 + i][:, h * NCMP:(h + 1) * NCMP], BCT[r, h, :], ID[r, r],
                                            start=False, stop=(h == NH - 1))
                last.then_inc(s["cmp_scores_full"], 1)
            pe.wait_ge(s["conv_act_ready"], KT)
            for n in range(2):
                feature_major("pw", CV, CHUNK_NO["pw"] + n, 4 * n)
            all_emptied(FIRST["pw"] + 8)

            def nsa_scores(w):
                h, branch, i = w // 8, w // 4 % 2, w % 4
                a, g = 64 * (h % 2), h // 4
                if w >= 4:
                    pe.wait_ge(s["nsa_scored"], w - 3)
                n = (i + 1) * P
                accumulate(banks[2 + w % 4][:, 0:n], [(Q[a:a + 64, h // 2, i * P:(i + 1) * P], KK[branch][a:a + 64, g, 0:n])]
                           ).then_inc(s["nsa_full"], 1)

            def nsa_outputs(hb):
                h, branch = hb // 2, hb % 2
                a, g, r, u = 64 * (h % 2), h // 4, 32 * (h % 4), 2 * (h // 4 % 2) + h // 8
                bank = banks[h // 2 % 2]
                if branch == 0:
                    if h >= 4 and h % 2 == 0:
                        pe.wait_ge(s["nsa_kept"], h // 2 - 1)
                    nc.tensor.matmul(bank[a:a + 64, :], VC4[r:r + 32, u, :], PCT[r:r + 32, g, :], start=True, stop=False)
                pe.wait_ge(s["nsa_t_ready0"], 2 * hb + 2)
                pe.wait_ge(s["nsa_t_ready1"], 2 * hb + 2)
                for j in range(TT):
                    c0 = branch * 256 + g * 64
                    last = nc.tensor.matmul(bank[a:a + 64, j * P:C], VV[:, j, c0:c0 + 64], PTN[hb % 2][:, j, j * P:C],
                                            start=False, stop=(branch == 1 and j == TT - 1))
                last.then_inc(s["nsa_out"], 1)

            pe.wait_ge(s["cmp_shifted"], TT)
            nsa_scores(0)
            nsa_scores(1)
            for i in range(TT):
                pe.wait_ge(s["cmp_probs"], i + 1)
                if i >= 2:
                    pe.wait_ge(s["cmp_t_ready"], i - 1)
                for g in range(4):
                    last = nc.tensor.transpose(banks[6 + i % 2][:, g * P:(g + 1) * P], PN[:, i, g * P:(g + 1) * P], ID)
                last.then_inc(s["cmp_t_full"], 1)
            pe.wait_ge(s["cmp_t_ready"], TT)
            nsa_scores(2)
            for w in range(8 * NH):
                i = w % 4
                if w + 3 < 8 * NH:
                    nsa_scores(w + 3)
                pe.wait_ge(s["nsa_probs"], w + 1)
                if w >= 2:
                    pe.wait_ge(s[f"nsa_t_ready{w % 2}"], w // 2)
                for j in range(i + 1):
                    last = nc.tensor.transpose(banks[6 + w % 2][:, j * P:(j + 1) * P], PN[:, w % 4, j * P:(j + 1) * P],
                                               ID)
                last.then_inc(s["nsa_t_full"], 1)
                if w >= 4 and i == 1:
                    nsa_outputs(w // 4 - 1)
            nsa_outputs(2 * NH - 1)

            pe.wait_ge(s["nsa_kept"], NH // 2)
            for n in range(2):
                token_major("wo2", GC, C, CHUNK_NO["wo2"] + n, first=4 * n)
            pe.wait_ge(s["mem_loaded"], 16)
            for c in range(KT):
                transposes(XP["mem"] + c, [(t * P, MTOK[:, t, c * P:(c + 1) * P]) for t in range(2)])
            transposed_emptied(XP["mem"] + KT)
            for n in range(2):
                feature_major("xk", MT, CHUNK_NO["xk"] + n, 4 * n, tokens=MEM)
            for n in range(2):
                token_major("xv", MT, C, CHUNK_NO["xv"] + n, tiles=2, first=2 * n)
            norm_transposes("normx", XN4)
            for n in range(2):
                feature_major("xq", hT, CHUNK_NO["xq"] + n, 4 * n)
            all_emptied(FIRST["xq"] + 8)

            def x_scores(w):
                h, i = w // 4, w % 4
                if w >= 4:
                    pe.wait_ge(s["x_exp"], w - 3)
                accumulate(banks[2 + w % 4][:, 0:MEM], [(XQ[:, 2 * h + c, i * P:(i + 1) * P], XK[:, 2 * h + c, :])
                                                        for c in range(2)]).then_inc(s["x_full"], 1)

            def x_outputs(h):
                pe.wait_ge(s["x_t_ready"], 4 * h + 4)
                for half in range(2):
                    if h:
                        pe.wait_ge(s["x_kept"], 2 * h - 1 + half)
                    c0 = h * 256 + half * P
                    accumulate(banks[half][:, :], [(XV[:, m, c0:c0 + P], PTX[h % 2][:, m, :]) for m in range(2)]
                               ).then_inc(s["x_out"], 1)

            transposed_emptied(XP["normx"] + KT)
            x_scores(0)
            x_scores(1)
            for w in range(16):
                if w + 2 < 16:
                    x_scores(w + 2)
                pe.wait_ge(s["x_probs"], w + 1)
                if w >= 2:
                    pe.wait_ge(s["x_t_ready"], w - 1)
                for m in range(2):
                    last = nc.tensor.transpose(banks[6 + w % 2][:, m * P:(m + 1) * P], PX[:, w % 4, m * P:(m + 1) * P],
                                               ID)
                last.then_inc(s["x_t_full"], 1)
                if w >= 4 and w % 4 == 1:
                    x_outputs(w // 4 - 1)
            x_outputs(3)
            pe.wait_ge(s["x_kept"], 8)
            for n in range(2):
                token_major("xo", OT, C, CHUNK_NO["xo"] + n, first=4 * n)

            pe.wait_ge(s["x_t_ready"], 16)
            norm_transposes("ffn", XN4)
            for j in range(FT // 2):
                w = loaded(CHUNK_NO["ffin"] + j).rearrange("p (a k n) -> p a k n", a=2, k=KT)
                for n in range(4):
                    c0 = n % 2 * P
                    accumulate(bank_of(FIRST["ffin"] + 4 * j + n)[:, :],
                               [(w[:, n // 2, k, c0:c0 + P], hT[:, k, :]) for k in range(KT)]
                               ).then_inc(s["proj_done"], 1)
            all_emptied(FIRST["ffin"] + 2 * FT)
            transposed_emptied(XP["ffn"] + KT)
            k0 = 0
            for n, kn in enumerate(FFOUT):
                w = loaded(CHUNK_NO["ffout"] + n)[:, 0:kn * D].rearrange("p (k n) -> p k n", k=kn)
                for k in range(kn):
                    for t in range(TT):
                        for half in range(2):
                            kk = k0 + k
                            last = nc.tensor.matmul(banks[2 * t + half][:, :], GT[:, kk, t * P:(t + 1) * P],
                                                    w[:, k, half * C:(half + 1) * C], start=(kk == 0),
                                                    stop=(kk == FT - 1))
                            if kk == FT - 1:
                                last.then_inc(s["ff_full"], 1)
                if n < len(FFOUT) - 1:
                    last.then_inc(s["ff_used"], 1)
                k0 += kn

        @block.scalar
        def _(act):
            steps = [0]

            def then(ins):
                steps[0] += 1
                ins.then_inc(s["act_step"], 1)
                act.wait_ge(s["act_step"], steps[0])

            def full(g):
                act.wait_ge(s["proj_done"], g + 1)
                return banks[g % 4]

            def empty(ins):
                ins.then_inc(s["act_emptied"], 1)

            act.dma_start(cols[:], io["cols"]).then_inc(s["consts"], 16)
            act.dma_start(k1[:], io["k1"]).then_inc(s["consts"], 16)
            act.dma_start(late[:, 0:K2_N], io["k2"]).then_inc(s["consts"], 16)
            act.dma_start(badar[0:12, 0:C], io["b_ada"][0].rearrange("(a n) -> a n", a=12)).then_inc(s["bada"], 16)
            act.dma_start(lamin, io["lam"].partition_broadcast(P)).then_inc(s["lamload"], 16)
            act.wait_ge(s["consts"], 48)
            nc.scalar.activation(csil, cols[:, V_C:V_C + KT], ACT.Silu).then_inc(s["csil_ready"], 1)

            def transposed(n):
                act.wait_ge(s["xpose_full"], n + 1)
                return banks[6 + n % 2]

            def norm(XN, ready=None, first=1):
                k = norms[0]
                norms[0] += 1
                for t in range(TT):
                    if ready is not None:
                        act.wait_ge(ready, first + t)
                    nc.scalar.activation(XN[:, t, :], X[:, t, :], ACT.Square, accum_out=ssq[:, t:t + 1]
                                         ).then_inc(s["ssq_ready"], 1)
                act.wait_ge(s["var_ready"], k + 1)
                nc.scalar.activation(std4, var4, ACT.Sqrt).then_inc(s["std_ready"], 1)

            norms = [0]

            def norm_columns(stage, hT, scale, bias=None):
                for c in range(0, KT, 2):
                    n = XP[stage] + c
                    b = transposed(n)
                    if bias is None:
                        ins = nc.scalar.activation(hT[:, c, :], b[:, :], ACT.Copy, scale=scale[:, c:c + 1])
                    else:
                        ins = nc.scalar.activation(hT[:, c, :], b[:, :], ACT.Identity, bias=bias[:, c:c + 1],
                                                   scale=scale[:, c:c + 1])
                    ins.then_inc(xpose_emptied[n % 2], 1)

            def ada(part):
                for n, j in enumerate(ADA_PARTS[part]):
                    bank = full(FIRST[f"ada{part}"] + n)
                    out = early[:, j, :] if j < 4 else modb[:, j - 4, :]
                    empty(nc.scalar.activation(out, bank[:, :], ACT.Copy))

            act.wait_ge(s["x_loaded"], 16)
            norm(XN1)
            ada(0)
            act.wait_ge(s["mod_ready"], 1)
            norm_columns("norm1", hT, A1, B1)
            for t in range(TT):
                bank = full(FIRST["c"] + t)
                nc.scalar.activation(Z[:, t, :], bank[:, :], ACT.Copy)
                for half in range(2):
                    piece = slice(256 * half, 256 * half + 256)
                    last = nc.scalar.activation(RQ[:, t, piece], bank[:, piece], ACT.Square,
                                                accum_out=ssq[:, 4 + 2 * t + half:5 + 2 * t + half])
                empty(last)
            act.wait_ge(s["latent_var"], 1)
            nc.scalar.activation(stdc, varc, ACT.Sqrt).then_inc(s["latent_std"], 1)
            ada(1)
            for c in range(4):
                n = XP["latents"] + c
                nc.scalar.activation(CTN[:, c, :], transposed(n)[:, :], ACT.Copy, scale=col(V_QA, c)
                                     ).then_inc(xpose_emptied[n % 2], 1)
            n = XP["kpe"]
            nc.scalar.activation(KPE[0:64, :], transposed(n)[0:64, :], ACT.Copy)
            nc.scalar.activation(KPE[64:128, :], banks[6 + n % 2][0:64, :], ACT.Copy).then_inc(xpose_emptied[n % 2], 1)
            ada(2)
            for c in range(4):
                n = XP["dq"] + c
                nc.scalar.activation(DQ[:, c, :], transposed(n)[:, :], ACT.Copy, scale=DIFF_SCALE
                                     ).then_inc(xpose_emptied[n % 2], 1)
            ada(3)
            for c in range(4):
                n = XP["dk"] + c
                nc.scalar.activation(DK[:, c, :], transposed(n)[:, :], ACT.Copy).then_inc(xpose_emptied[n % 2], 1)
            act.wait_ge(s["zeros_stored"], 16)
            for t in range(TT):
                empty(nc.scalar.activation(DV[:, t, :], full(FIRST["dv"] + t)[:, :], ACT.Copy))
            ada(4)
            g = FIRST["up"]
            for h in range(4):
                empty(nc.scalar.activation(QN[:, h, :], full(g + h)[:, :], ACT.Copy, scale=MLA_SCALE))
            for h in range(4):
                empty(nc.scalar.activation(KN[:, h, :], full(g + 4 + h)[:, :], ACT.Copy))
            for t in range(TT):
                empty(nc.scalar.activation(VM[:, t, :], full(g + 8 + t)[:, :], ACT.Copy))
            for c in range(2):
                n = XP["qpe"] + c
                nc.scalar.activation(QPE[:, c, :], transposed(n)[:, :], ACT.Copy, scale=MLA_SCALE
                                     ).then_inc(xpose_emptied[n % 2], 1)
            act.wait_ge(s["lam_ready"], 1)
            nc.scalar.activation(lamv[:, 2:4], lamv[:, 0:2], ACT.Exp).then_inc(s["lam_exp"], 1)

            def keep_pt(t):
                h, i = t // TT, t % TT
                act.wait_ge(s["pt_full"], t + 1)
                if h >= 2:
                    act.wait_ge(s["pv_full"], h - 1)
                nc.scalar.activation(PT[h % 2][:, :, i * P:(i + 1) * P],
                                     banks[6 + t % 2][:, :].rearrange("p (j q) -> p j q", j=TT), ACT.Copy
                                     ).then_inc(s["pt_ready"], 1)

            def keep_outputs(h):
                act.wait_ge(s["pv_full"], h + 1)
                if h >= 4:
                    nc.scalar.activation(SUBS[:, h - 4, :], banks[h % 2][:, :], ACT.Square
                                         ).then_inc(s["sub_squares"], 1)
                nc.scalar.activation(mixT[:, h, :], banks[h % 2][:, :], ACT.Copy).then_inc(s["pv_emptied"], 1)

            for t in range(32):
                for n in range(first_score(t), first_score(t + 1)):
                    act.wait_ge(s["max_ready"], n + 1)
                    if n >= 4:
                        act.wait_ge(s["pt_full"], unit_of(n - 4) + 1)
                    nc.scalar.activation(PB[:, n % 4, :], banks[2 + n % 4][:, :], ACT.Exp, bias=nmx[:, n % 8:n % 8 + 1],
                                         accum_out=sums[:, n % 8:n % 8 + 1]).then_inc(s["exp_done"], 1)
                if t >= 1:
                    keep_pt(t - 1)
                if t >= 5 and t % TT == 1:
                    keep_outputs(t // TT - 1)
            keep_pt(31)
            keep_outputs(7)
            for h in range(4):
                act.wait_ge(s["sub_var"], h + 1)
                nc.scalar.activation(SUBS[:, h, :], SUBS[:, h, :], ACT.Sqrt).then_inc(s["sub_std"], 1)
            norm(XN2, s["x_ready"], 5)
            norm_columns("norm2", h2T, A2, B2)
            act.wait_ge(s["router_exp_in"], 1)
            nc.scalar.activation(RS(144, 16), RS(144, 16), ACT.Exp).then_inc(s["router_exp_out"], 1)
            act.wait_ge(s["router_exp_in"], 2)
            nc.scalar.activation(RS(1284, 4), RS(1280, 4), ACT.Exp).then_inc(s["router_exp_out"], 1)

            rows = ys_dram.rearrange("(b p) d -> p b d", p=P)

            def moe_keep_x(e, b):
                for half in range(2):
                    act.wait_ge(s["xt_full"], 2 * e + 1 + half)
                    if half == 0:
                        at_least(act, s["up_full"], e - 1)
                    nc.scalar.activation(XT[b][:, 4 * half:4 * half + 4, :],
                                         banks[6 + half][:, :].rearrange("p (k n) -> p k n", k=4), ACT.Copy
                                         ).then_inc(s["xt_ready"], 1)

            def moe_silu(e, b):
                act.wait_ge(s["gate_full"], e + 1)
                at_least(act, s["a_ready"], e - 1)
                nc.scalar.activation(SG[:, b, :], banks[b][:, :], ACT.Silu).then_inc(s["silu_ready"], 1)

            def moe_store(e, b):
                act.wait_ge(s["y_ready"], 2 * e + 2)
                act.dma_start(rows[:, bass.ds(e, 1), :], Y[:, b:b + 1, :]).then_inc(s[f"y_stored{b}"], 16)

            def moe_step(it, r):
                e, b = 2 * it + r, r % 2
                moe_silu(e, b)
                moe_keep_x(e + 1, 1 - b)
                moe_store(e - 1, 1 - b)

            moe_keep_x(0, 0)
            moe_silu(0, 0)
            moe_keep_x(1, 1)
            moe_step(0, 1)
            moe_step(0, 2)
            with act.Fori(1, N_EXP // 2 - 1) as it:
                moe_step(it, 1)
                moe_step(it, 2)
            e = N_EXP - 1
            moe_silu(e, 1)
            moe_store(e - 1, 0)
            moe_store(e, 1)
            act.wait_ge(s["ctl_ready"], 1)
            n_over = act.value_load(ctl[0:1, 7:8], min_val=0, max_val=N_OVER)
            with act.If(n_over > 0):
                with act.Fori(0, N_OVER) as j:
                    for half in range(2):
                        act.wait_ge(s["ov_xt_full"], 2 * j + 1 + half)
                        nc.scalar.activation(XT[0][:, 4 * half:4 * half + 4, :],
                                             banks[6 + half][:, :].rearrange("p (k n) -> p k n", k=4), ACT.Copy
                                             ).then_inc(s["ov_xt_ready"], 1)
                    act.wait_ge(s["ov_up_full"], 2 * j + 2)
                    nc.scalar.activation(SG[:, 0, :], banks[0][:, :], ACT.Silu).then_inc(s["ov_silu_ready"], 1)
                    act.wait_ge(s["ov_y_ready"], 2 * j + 2)
                    act.dma_start(rows[:, bass.ds(N_EXP + j, 1), :], Y[:, 0:1, :]).then_inc(s["ov_stored"], 16)
            norm(XN3, s["x_moe"], 1)
            act.wait_ge(s["onehot_loaded"], 32)
            nc.scalar.activation(RB[0:32, :], RB[0:32, :], ACT.Copy, scale=8.0).then_inc(s["act_step"], 1)
            steps[0] += 1
            act.wait_ge(s["act_step"], steps[0])
            act.wait_ge(s["pads_set"], 1)
            nc.scalar.activation(small[:, 153:154], small[:, 152:153], ACT.Copy).then_inc(s["bias_rows_ready"], 1)
            for n in range(3):
                width = C if n < 2 else NG - 2 * C
                bank = full(FIRST["toep"] + n)
                ins = nc.scalar.activation(BROW[0:NH, n * C:n * C + width], bank[0:NH, 0:width], ACT.Copy)
                empty(ins)
            norm(XN4, s["x_final"], 1)
            norm_columns("mix", hT, cols[:, V_MIX:V_MIX + KT])
            act.wait_ge(s["pads_set"], 2)
            for c in range(KT):
                empty(nc.scalar.activation(V[:, c, PAD:VW_], full(FIRST["glu_g"] + c)[:, :], ACT.Sigmoid))
            for c in range(KT):
                falling = bass.AP(area, 12528 + c * S + P - 1, [[22016, P], [P, TT], [-1, P]])
                empty(nc.scalar.activation(falling, full(FIRST["q2"] + c)[:, :].rearrange("p (t q) -> p t q", q=P),
                                           ACT.Copy))
            for n in range(4):
                out = (KC, VC)[n // 2][:, n % 2, :]
                empty(nc.scalar.activation(out, full(FIRST["kvc"] + n)[:, :], ACT.Copy))
            for n in range(4):
                bank = full(FIRST["kk"] + n)
                for half in range(2):
                    for a in range(2):
                        last = nc.scalar.activation(KK[n // 2][64 * a:64 * a + 64, 2 * (n % 2) + half, :],
                                                    bank[64 * half:64 * half + 64, :], ACT.Copy)
                empty(last)
            for t in range(TT):
                empty(nc.scalar.activation(VV[:, t, :], full(FIRST["vv"] + t)[:, :], ACT.Copy))
            for t in range(TT):
                empty(nc.scalar.activation(GRISE[:, t, :], full(FIRST["gh"] + t)[:, 0:48], ACT.Sigmoid))
            empty(nc.scalar.activation(GS[:].rearrange("p t n -> p (t n)"), full(FIRST["gates_falling"])[:, 0:TT * 48],
                                       ACT.Copy))
            act.wait_ge(s["conv_ready"], KT)
            for c in range(KT):
                empty(nc.scalar.activation(GC[:, c, :], full(FIRST["gc"] + c)[:, :], ACT.Sigmoid))
            for c in range(4):
                empty(nc.scalar.activation(GA[:, c, :], full(FIRST["ga0"] + c)[:, :], ACT.Sigmoid))
            for c in range(KT):
                act.wait_ge(s["centred"], c + 1)
                if c >= 2:
                    act.wait_ge(s["sq_used"], c - 1)
                nc.scalar.activation(SQ[c % 2], CV[:, c, :], ACT.Square).then_inc(s["squared"], 1)
            act.wait_ge(s["ln_var_ready"], 1)
            nc.scalar.activation(RSQ, RSQ, ACT.Sqrt).then_inc(s["ln_std_ready"], 1)
            for c in range(4):
                empty(nc.scalar.activation(GA[:, 4 + c, :], full(FIRST["ga1"] + c)[:, :], ACT.Sigmoid))
            for a in range(2):
                empty(nc.scalar.activation(POSB[0:64, a:a + 1], full(FIRST["pos"] + a)[0:64, 0:1], ACT.Copy))
            act.wait_ge(s["act_emptied"], emptied("act", FIRST["pos"] + 1))
            for n in range(4):
                a, half = n // 2, n % 2
                empty(nc.scalar.activation(ZC[0:64, a, 62 * half:62 * half + 62], full(FIRST["cmp1"] + n)[0:64, 0:62],
                                           ACT.Silu, bias=POSB[0:64, a:a + 1]))
            for c in range(KT):
                act.wait_ge(s["ln_scaled"], c + 1)
                nc.scalar.activation(CV[:, c, :], CV[:, c, :], ACT.Silu, bias=col(V_LNB, c), scale=col(V_LNG, c)
                                     ).then_inc(s["conv_act_ready"], 1)
            act.wait_ge(s["pads_set"], 4)
            bank = full(FIRST["cmp2"])
            for a in range(2):
                last = nc.scalar.activation(KCT[64 * a:64 * a + 64, :, 0:31],
                                            bank[0:64, 0:124].rearrange("p (u n) -> p u n", u=4), ACT.Copy)
            empty(last)
            bank = full(FIRST["cmp2"] + 1)
            for r in range(4):
                last = nc.scalar.activation(VC4[32 * r:32 * r + 31, :, :],
                                            bank[0:31, 0:256].rearrange("p (u n) -> p u n", u=4), ACT.Copy)
            empty(last)
            for i in range(TT):
                act.wait_ge(s["cmp_shifted"], i + 1)
                nc.scalar.activation(PN[:, i, :], PN[:, i, :], ACT.Exp).then_inc(s["cmp_exp"], 1)
            for i in range(TT):
                act.wait_ge(s["cmp_t_full"], i + 1)
                nc.scalar.activation(PCT[:, :, i * P:(i + 1) * P],
                                     banks[6 + i % 2][:, :].rearrange("p (g q) -> p g q", g=4), ACT.Copy
                                     ).then_inc(s["cmp_t_ready"], 1)

            def nsa_keep_t(w):
                hb, i = w // 4, w % 4
                act.wait_ge(s["nsa_t_full"], w + 1)
                if hb >= 2:
                    act.wait_ge(s["nsa_out"], hb - 1)
                n = (i + 1) * P
                nc.scalar.activation(PTN[hb % 2][:, 0:i + 1, i * P:(i + 1) * P],
                                     banks[6][:, 0:n].rearrange("p (j q) -> p j q", q=P), ACT.Copy
                                     ).then_inc(s["nsa_t_ready0"], 1)

            for w in range(8 * NH):
                i = w % 4
                n = (i + 1) * P
                act.wait_ge(s["nsa_scored"], w + 1)
                nc.scalar.activation(PN[:, i, 0:n], PN[:, i, 0:n], ACT.Exp, bias=nmx[:, w % 8:w % 8 + 1], scale=-1.0,
                                     accum_out=sums[:, w % 8:w % 8 + 1]).then_inc(s["nsa_exp"], 1)
                if w >= 2 and w % 2 == 0:
                    nsa_keep_t(w - 2)
            nsa_keep_t(8 * NH - 2)

            for c in range(KT):
                n = XP["mem"] + c
                nc.scalar.activation(MT[:, c, :], transposed(n)[:, 0:MEM], ACT.Copy).then_inc(xpose_emptied[n % 2], 1)
            for c in range(KT):
                empty(nc.scalar.activation(XK[:, c, :], full(FIRST["xk"] + c)[:, 0:MEM], ACT.Copy))
            norm(XN4, s["dve_emptied"], emptied("dve", FIRST["wo2"] + 4))
            for n in range(4):
                empty(nc.scalar.activation(XV[:, n % 2, n // 2 * C:n // 2 * C + C], full(FIRST["xv"] + n)[:, :], ACT.Copy))
            norm_columns("normx", hT, cols[:, V_XN:V_XN + KT])
            for c in range(KT):
                empty(nc.scalar.activation(XQ[:, c, :], full(FIRST["xq"] + c)[:, :], ACT.Copy, scale=1.0 / 16))

            def x_keep_t(w):
                h, i = w // 4, w % 4
                act.wait_ge(s["x_t_full"], w + 1)
                if h >= 2:
                    act.wait_ge(s["x_out"], 2 * (h - 1))
                nc.scalar.activation(PTX[h % 2][:, :, i * P:(i + 1) * P],
                                     banks[6 + w % 2][:, 0:MEM].rearrange("p (j q) -> p j q", q=P), ACT.Copy
                                     ).then_inc(s["x_t_ready"], 1)

            def x_keep_outputs(h):
                for half in range(2):
                    act.wait_ge(s["x_out"], 2 * h + half + 1)
                    nc.scalar.activation(OT[:, 2 * h + half, :], banks[half][:, :], ACT.Copy).then_inc(s["x_kept"], 1)

            for w in range(16):
                act.wait_ge(s["x_scored"], w + 1)
                if w >= 4:
                    act.wait_ge(s["x_t_full"], w - 3)
                nc.scalar.activation(PX[:, w % 4, :], banks[2 + w % 4][:, 0:MEM], ACT.Exp, bias=nmx[:, w % 8:w % 8 + 1],
                                     accum_out=sums[:, w % 8:w % 8 + 1]).then_inc(s["x_exp"], 1)
                if w >= 1:
                    x_keep_t(w - 1)
                if w >= 5 and w % 4 == 2:
                    x_keep_outputs(w // 4 - 1)
            x_keep_t(15)
            x_keep_outputs(3)
            norm(XN4, s["dve_emptied"], emptied("dve", FIRST["xo"] + 4))
            norm_columns("ffn", hT, cols[:, V_FFN:V_FFN + KT])
            for j in range(FT // 2):
                if j >= 2:
                    act.wait_ge(s["dve_emptied"], emptied("dve", FIRST["ffin"] + 4 * (j - 2) + 3))
                for n in range(2):
                    empty(nc.scalar.activation(SA[:, (2 * j + n) % 4, :], full(FIRST["ffin"] + 4 * j + n)[:, :], ACT.Silu))
            norm(A(0, 4096, TT), s["x_ff"], 1)

        @block.vector
        def _(dve):
            steps = [0]

            def then(ins):
                steps[0] += 1
                ins.then_inc(s["dve_step"], 1)
                dve.wait_ge(s["dve_step"], steps[0])

            def full(g):
                dve.wait_ge(s["proj_done"], g + 1)
                return banks[g % 4]

            norms = [0]

            def norm(XN):
                k = norms[0]
                norms[0] += 1
                dve.wait_ge(s["ssq_ready"], TT * (k + 1))
                nc.vector.tensor_scalar(var4, ssq[:, 0:TT], 1.0 / D, EPS, ALU.mult, ALU.add
                                        ).then_inc(s["var_ready"], 1)
                dve.wait_ge(s["std_ready"], k + 1)
                then(nc.vector.reciprocal(rstd[:, 0:TT], std4))
                for t in range(TT):
                    nc.vector.tensor_scalar(XN[:, t, :], X[:, t, :], rstd[:, t:t + 1], None, ALU.mult
                                            ).then_inc(s["xn_ready"], 1)

            def norm_columns(stage, hT, scale, bias=None):
                for c in range(1, KT, 2):
                    n = XP[stage] + c
                    dve.wait_ge(s["xpose_full"], n + 1)
                    if bias is None:
                        ins = nc.vector.tensor_scalar(hT[:, c, :], banks[6 + n % 2][:, :], scale[:, c:c + 1], None,
                                                      ALU.mult)
                    else:
                        ins = nc.vector.tensor_scalar(hT[:, c, :], banks[6 + n % 2][:, :], scale[:, c:c + 1],
                                                      bias[:, c:c + 1], ALU.mult, ALU.add)
                    ins.then_inc(xpose_emptied[n % 2], 1)

            def ada(part):
                for n, j in enumerate(ADA_PARTS[part]):
                    c = CHUNK_NO[f"ada{part}"] + n
                    dve.wait_ge(w_loaded[c % N_DENSE_SLOTS], loaded_value(c))
                    if j >= 2:
                        dve.wait_ge(s["proj_done"], ADA_GROUP[j - 2] + 1)
                    w = slot(c % N_DENSE_SLOTS).rearrange("p (k n) -> p k n", k=KT)
                    b = 2 * (j % 2)
                    for k in range(KT):
                        acc = ada_acc[:, b + k % 2, :]
                        if k >= 2:
                            dve.wait_ge(s["dve_step"], steps[0] - 1)
                            ins = nc.vector.scalar_tensor_tensor(acc, w[:, k, :], csil[:, k:k + 1], acc, ALU.mult,
                                                                 ALU.add)
                        else:
                            ins = nc.vector.tensor_scalar(acc, w[:, k, :], csil[:, k:k + 1], None, ALU.mult)
                        if k < KT - 1:
                            steps[0] += 1
                            ins.then_inc(s["dve_step"], 1)
                    ins.then_inc(s["ada_acc"], 1)

            ropes = [0]

            def rope(g, t, heads, out):
                n = heads * 64
                bank = full(g)
                x3 = bank[:, 0:n].rearrange("p (h b) -> p h b", b=32)
                o3 = out.rearrange("p (h b) -> p h b", b=32)
                cos = bass.AP(late, K2_COS + t * 32, [[1024, P], [0, 2 * heads], [1, 32]])
                nc.vector.tensor_tensor(o3, x3, cos, ALU.mult)
                swapped = bass.AP(bank, 32, [[C, P], [64, heads], [-32, 2], [1, 32]])
                sin = bass.AP(late, K2_SIN + t * 64, [[1024, P], [0, heads], [32, 2], [1, 32]])
                r4 = RT[:, 0:n].rearrange("p (h a b) -> p h a b", a=2, b=32)
                if ropes[0]:
                    dve.wait_ge(s["rope_ready"], ropes[0])
                ropes[0] += 1
                nc.vector.tensor_tensor(r4, swapped, sin, ALU.mult).then_inc(s["dve_emptied"], 1)
                dve.wait_ge(s["dve_emptied"], emptied("dve", g))
                nc.vector.tensor_tensor(out, out, RT[:, 0:n], ALU.add).then_inc(s["rope_ready"], 1)

            nc.vector.memset(ones_d[:], 1.0 / D)
            nc.vector.memset(ones[:], 1.0).then_inc(s["ones_set"], 1)
            dve.wait_ge(s["lamload"], 16)
            for i in range(2):
                nc.vector.tensor_tensor_reduce(out=lamin[:, 128 * i:128 * i + 64], in0=lamin[:, 128 * i:128 * i + 64],
                                               in1=lamin[:, 128 * i + 64:128 * i + 128], scale=1.0, scalar=0.0,
                                               op0=ALU.mult, op1=ALU.add, accum_out=lamv[:, i:i + 1]
                                               ).then_inc(s["lam_ready"], 1)
            dve.wait_ge(s["csil_ready"], 1)
            dve.wait_ge(s["x_loaded"], 16)
            norm(XN1)
            ada(0)
            bank = full(FIRST["modcols"])
            nc.vector.tensor_copy(B1, bank[:, 0:8])
            nc.vector.scalar_tensor_tensor(A1, bank[:, 8:16], 1.0, cols[:, V_N1:V_N1 + KT], ALU.add, ALU.mult
                                           ).then_inc(s["dve_emptied"], 1)
            dve.wait_ge(s["dve_emptied"], emptied("dve", FIRST["modcols"]))
            nc.vector.memset(small[:, 152:153], 0.0).then_inc(s["mod_ready"], 1)
            norm_columns("norm1", hT, A1, B1)
            ada(1)
            dve.wait_ge(s["act_emptied"], emptied("act", FIRST["c"] + 3))
            nc.vector.tensor_scalar(varc, ssq[:, 4:12], 1.0 / 256, EPS, ALU.mult, ALU.add).then_inc(s["latent_var"], 1)
            dve.wait_ge(s["latent_std"], 1)
            then(nc.vector.reciprocal(rstd[:, 4:12], stdc))
            for t in range(TT):
                for half in range(2):
                    piece = slice(256 * half, 256 * half + 256)
                    ins = nc.vector.tensor_scalar(Z[:, t, piece], Z[:, t, piece],
                                                  rstd[:, 4 + 2 * t + half:5 + 2 * t + half], None, ALU.mult)
                ins.then_inc(s["latents_ready"], 1)
            for t in range(TT):
                rope(FIRST["kpe"] + t, t, 1, RQ[:, t, 0:64])
            ada(2)
            dve.wait_ge(s["xpose_full"], XP["latents"] + 4)
            for t in range(TT):
                rope(FIRST["dq"] + t, t, 8, Z[:, t, :])
            ada(3)
            dve.wait_ge(s["xpose_full"], XP["kpe"] + 1)
            for t in range(TT):
                rope(FIRST["dk"] + t, t, 8, RQ[:, t, :])
            ada(4)
            bank = full(FIRST["modcols2"])
            nc.vector.tensor_copy(B2, bank[:, 0:8])
            nc.vector.scalar_tensor_tensor(A2, bank[:, 8:16], 1.0, cols[:, V_N2:V_N2 + KT], ALU.add, ALU.mult
                                           ).then_inc(s["dve_emptied"], 1)
            for t in range(TT):
                rope(FIRST["up"] + 12 + t, t, 4, QRT[:, t, :])
            dve.wait_ge(s["lam_exp"], 1)
            then(nc.vector.tensor_tensor(lamv[:, 4:5], lamv[:, 3:4], lamv[:, 2:3], ALU.subtract))
            then(nc.vector.tensor_scalar(lamv[:, 5:6], lamv[:, 4:5], -LAMBDA_INIT, None, ALU.add))

            def finish_probs(t):
                for n in range(first_score(t), first_score(t + 1)):
                    dve.wait_ge(s["exp_done"], n + 1)
                    i = n % 8
                    if t < 16:
                        nc.vector.reciprocal(rcp[:, i:i + 1], sums[:, i:i + 1]).then_inc(s["rcp_ready"], 1)
                    elif n % 2 == 0:
                        nc.vector.reciprocal(rcp[:, i:i + 1], sums[:, i:i + 1])
                    else:
                        then(nc.vector.reciprocal(rcp[:, i:i + 1], sums[:, i:i + 1]))
                        nc.vector.tensor_tensor(rcp[:, 8 + i:9 + i], rcp[:, i:i + 1], lamv[:, 5:6], ALU.mult
                                                ).then_inc(s["rcp_ready"], 1)
                        dve.wait_ge(s["scaled"], t - 15)
                        a, b = (n - 1) % 4, n % 4
                        nc.vector.scalar_tensor_tensor(PB[:, a, :], PB[:, a, :], rcp[:, i - 1:i], PB[:, b, :],
                                                       ALU.mult, ALU.add).then_inc(s["probs_diff"], 1)

            for t in range(33):
                if t < 32:
                    for n in range(first_score(t), first_score(t + 1)):
                        dve.wait_ge(s["scores_full"], n + 1)
                        nc.vector.reduce_max(nmx[:, n % 8:n % 8 + 1], banks[2 + n % 4][:, :], AX, negate=True
                                             ).then_inc(s["max_ready"], 1)
                if t >= 1:
                    finish_probs(t - 1)
            for h in range(4):
                dve.wait_ge(s["sub_full"], h + 1)
                nc.vector.tensor_scalar(SUBS[:, h, :], banks[2 + h][:, :], 1.0 / (P * (1 - LAMBDA_INIT) ** 2),
                                        EPS / (1 - LAMBDA_INIT) ** 2, ALU.mult, ALU.add).then_inc(s["sub_var"], 1)
            for h in range(4):
                dve.wait_ge(s["sub_std"], h + 1)
                then(nc.vector.reciprocal(SUBS[:, h, :], SUBS[:, h, :]))
                dve.wait_ge(s["pv_emptied"], 5 + h)
                nc.vector.scalar_tensor_tensor(mixT[:, 4 + h, :], mixT[:, 4 + h, :], col(V_SUB, 0), SUBS[:, h, :],
                                               ALU.mult, ALU.mult).then_inc(s["sub_ready"], 1)

            def residual(stage, gate):
                for n in range(8):
                    g = FIRST[stage] + n
                    half, t = n // 4, n % 4
                    piece = slice(half * C, half * C + C)
                    bank = full(g)
                    if gate is None:
                        nc.vector.tensor_tensor(X[:, t, piece], bank[:, :], X[:, t, piece], ALU.add
                                                ).then_inc(s["dve_emptied"], 1)
                    else:
                        nc.vector.tensor_tensor(WOT[:, n % 2, :], bank[:, :], gate[:, piece], ALU.mult
                                                ).then_inc(s["dve_emptied"], 1)
                        dve.wait_ge(s["dve_emptied"], emptied("dve", g))
                        nc.vector.tensor_tensor(X[:, t, piece], X[:, t, piece], WOT[:, n % 2, :], ALU.add
                                                ).then_inc(s["x_ready"], 1)

            residual("wo", gate1)
            norm(XN2)
            norm_columns("norm2", h2T, A2, B2)

            LG = 0
            dve.wait_ge(s["router_loaded"], 80)
            for t in range(TT):
                bank = full(FIRST["router"] + t)
                nc.vector.tensor_tensor(RS(LG + 36 * t, 36), bank[:, 0:36], BR, ALU.add).then_inc(s["dve_emptied"], 1)
            dve.wait_ge(s["dve_emptied"], emptied("dve", FIRST["router"] + 3))
            G3 = R3(LG, [36, 4], [1, 4])
            iota4 = bass.AP(late, K2_IOTA, [[1024, P], [0, 4], [1, 4]])
            iota8 = bass.AP(late, K2_IOTA, [[1024, P], [0, 4], [1, 8]])
            iota32 = bass.AP(late, K2_IOTA, [[1024, P], [0, 4], [1, 32]])

            def per_token(off, n):
                return R3(off, [1, 4], [0, n])

            def lowest_index(eq, iota, n, out):
                then(nc.vector.tensor_scalar(eq, eq, -1000.0, 1000.0, ALU.mult, ALU.add))
                then(nc.vector.tensor_tensor(eq, eq, iota, ALU.add))
                then(nc.vector.tensor_reduce(RS(out, 4), eq, AX, ALU.min))

            (GM, GSUM, GP, GI, M1, I1, M2, I2) = range(1248, 1280, 4)
            DM, XE, DEN, RD = 1280, 1284, 1288, 1292
            EID, RANK, OSA, OV, BLK, HI8, LO8, D8, T8 = range(1296, 1368, 8)
            then(nc.vector.tensor_reduce(RS(GM, 4), G3, AX, ALU.max))
            then(nc.vector.tensor_tensor(R3(144, [4, 4], [1, 4]), G3, per_token(GM, 4), ALU.subtract))
            then(nc.vector.tensor_scalar(RS(160, 16), RS(144, 16), 0.0, None, ALU.is_equal))
            nc.vector.memset(RS(1372, 1), 0.0).then_inc(s["router_exp_in"], 1)
            lowest_index(R3(160, [4, 4], [1, 4]), iota4, 4, GI)
            then(nc.vector.tensor_tensor(R3(176, [4, 4], [1, 4]), iota4, per_token(GI, 4), ALU.is_equal))
            then(nc.vector.tensor_tensor(R3(192, [32, 4], [8, 4], [1, 8]), R3(LG + 4, [36, 4], [8, 4], [1, 8]),
                                         R3(176, [4, 4], [1, 4], [0, 8]), ALU.mult))
            then(nc.vector.tensor_reduce(R3(320, [8, 4], [1, 8]), R3(192, [32, 4], [1, 8], [8, 4]), AX, ALU.add))
            ES = R3(320, [8, 4], [1, 8])
            ED = R3(352, [8, 4], [1, 8])
            OH = R3(384, [8, 4], [1, 8])
            then(nc.vector.tensor_reduce(RS(M1, 4), ES, AX, ALU.max))
            then(nc.vector.tensor_tensor(ED, ES, per_token(M1, 8), ALU.is_equal))
            lowest_index(ED, iota8, 8, I1)
            then(nc.vector.tensor_tensor(OH, iota8, per_token(I1, 8), ALU.is_equal))
            then(nc.vector.scalar_tensor_tensor(ES, OH, 3 * NEG, ES, ALU.mult, ALU.add))
            then(nc.vector.tensor_reduce(RS(M2, 4), ES, AX, ALU.max))
            then(nc.vector.tensor_tensor(ED, ES, per_token(M2, 8), ALU.is_equal))
            lowest_index(ED, iota8, 8, I2)
            nc.vector.tensor_tensor(RS(DM, 4), RS(M2, 4), RS(M1, 4), ALU.subtract).then_inc(s["router_exp_in"], 1)
            dve.wait_ge(s["router_exp_out"], 1)
            then(nc.vector.tensor_reduce(RS(GSUM, 4), R3(144, [4, 4], [1, 4]), AX, ALU.add))
            then(nc.vector.reciprocal(RS(GP, 4), RS(GSUM, 4)))
            dve.wait_ge(s["router_exp_out"], 2)
            then(nc.vector.tensor_scalar(RS(DEN, 4), RS(XE, 4), 1.0, None, ALU.add))
            then(nc.vector.reciprocal(RS(RD, 4), RS(DEN, 4)))
            then(nc.vector.tensor_tensor(wts[:, 0, :], RS(GP, 4), RS(RD, 4), ALU.mult))
            nc.vector.tensor_tensor(wts[:, 1, :], wts[:, 0, :], RS(XE, 4), ALU.mult)
            nc.vector.scalar_tensor_tensor(RS(EID, 4), RS(GI, 4), 8.0, RS(I1, 4), ALU.mult, ALU.add)
            then(nc.vector.scalar_tensor_tensor(RS(EID + 4, 4), RS(GI, 4), 8.0, RS(I2, 4), ALU.mult, ALU.add))
            for a in range(2):
                then(nc.vector.tensor_tensor(R3(416 + 128 * a, [32, 4], [1, 32]), iota32, per_token(EID + 4 * a, 32),
                                             ALU.is_equal))
            nc.vector.tensor_tensor(RS(672, 128), RS(416, 128), RS(544, 128), ALU.add).then_inc(s["onehot_ready"], 1)
            bank = full(FIRST["rank"])
            nc.vector.tensor_copy(RS(928, 128), bank[:, 0:128])
            counts, over = bank[0:32, 128:256], RS(1056, P)[0:32, :]
            then(nc.vector.tensor_scalar(over, counts, float(CAP), None, ALU.is_gt))
            then(nc.vector.scalar_tensor_tensor(over, counts, 2.0 * CAP, over, ALU.is_gt, ALU.add))
            nc.vector.scalar_tensor_tensor(over, counts, 3.0 * CAP, over, ALU.is_gt, ALU.add
                                           ).then_inc(s["dve_emptied"], 1)
            dve.wait_ge(s["dve_emptied"], emptied("dve", FIRST["rank"]))
            nc.vector.memset(RS(1372, 1), 0.0).then_inc(s["onehot_ready"], 1)

            def of_expert(table, out):
                for a in range(2):
                    then(nc.vector.tensor_tensor(R3(800, [32, 4], [1, 32]), R3(416 + 128 * a, [32, 4], [1, 32]), table,
                                                 ALU.mult))
                    then(nc.vector.tensor_reduce(RS(out + 4 * a, 4), R3(800, [32, 4], [1, 32]), AX, ALU.add))

            of_expert(R3(928, [32, 4], [1, 32]), RANK)
            bank = full(FIRST["over"])
            nc.vector.tensor_copy(RS(1184, 64), bank[:, 0:64]).then_inc(s["dve_emptied"], 1)
            dve.wait_ge(s["dve_emptied"], emptied("dve", FIRST["over"]))
            of_expert(R3(1184, [0, 4], [1, 32]), OSA)
            then(nc.vector.tensor_scalar(RS(OV, 8), RS(RANK, 8), float(CAP), None, ALU.is_ge))
            then(nc.vector.scalar_tensor_tensor(RS(BLK, 8), RS(RANK, 8), 2.0 * CAP, RS(OV, 8), ALU.is_ge, ALU.add))
            then(nc.vector.scalar_tensor_tensor(RS(BLK, 8), RS(RANK, 8), 3.0 * CAP, RS(BLK, 8), ALU.is_ge, ALU.add))
            then(nc.vector.scalar_tensor_tensor(RS(LO8, 8), RS(BLK, 8), -float(CAP), RS(RANK, 8), ALU.mult, ALU.add))
            then(nc.vector.scalar_tensor_tensor(RS(T8, 8), RS(OSA, 8), N_EXP - 1.0, RS(BLK, 8), ALU.add, ALU.add))
            then(nc.vector.tensor_tensor(RS(T8, 8), RS(T8, 8), RS(EID, 8), ALU.subtract))
            then(nc.vector.tensor_tensor(RS(T8, 8), RS(T8, 8), RS(OV, 8), ALU.mult))
            then(nc.vector.tensor_tensor(RS(HI8, 8), RS(T8, 8), RS(EID, 8), ALU.add))
            then(nc.vector.scalar_tensor_tensor(RS(D8, 8), RS(HI8, 8), float(CAP), RS(LO8, 8), ALU.mult, ALU.add))
            nc.vector.tensor_copy(dest[:, :], RS(D8, 8))
            for n in range(8):
                nc.vector.tensor_scalar(LO[:, n, :], IOTA, RS(LO8 + n, 1), None, ALU.is_equal)
                ins = nc.vector.tensor_scalar(HI[:, n, :], IOTA[:, 0:N_BLOCKS], RS(HI8 + n, 1), TOK[:, n % 4:n % 4 + 1],
                                              ALU.is_equal, ALU.mult)
            ins.then_inc(s["onehot_ready"], 1)
            bank = full(FIRST["slots"])
            nc.vector.tensor_copy(idx[:, :], bank[:, 0:N_BLOCKS]).then_inc(s["dve_emptied"], 1)
            dve.wait_ge(s["dve_emptied"], emptied("dve", FIRST["slots"]))
            nc.vector.memset(RS(1372, 1), 0.0).then_inc(s["idx_ready"], 1)
            J1, J2 = R3(1400, [32, N_OVER], [1, 32]), R3(1400 + 224, [32, N_OVER], [1, 32])
            j7 = bass.AP(late, K2_IOTA, [[1024, P], [1, N_OVER], [0, 32]])
            then(nc.vector.tensor_tensor(RS(1216, 32), RS(1184, 32), RS(1216, 32), ALU.add))
            then(nc.vector.tensor_tensor(J1, R3(1184, [0, N_OVER], [1, 32]), j7, ALU.is_le))
            then(nc.vector.tensor_tensor(J2, R3(1216, [0, N_OVER], [1, 32]), j7, ALU.is_gt))
            then(nc.vector.tensor_tensor(J1, J1, J2, ALU.mult))
            then(nc.vector.tensor_tensor(J1, J1, bass.AP(late, K2_IOTA, [[1024, P], [0, N_OVER], [1, 32]]), ALU.mult))
            then(nc.vector.tensor_reduce(RS(T8, N_OVER), J1, AX, ALU.add))
            nc.vector.tensor_copy(ctl[:, 0:N_OVER], RS(T8, N_OVER))
            nc.vector.tensor_copy(ctl[:, 7:8], RS(1216 + 31, 1)).then_inc(s["ctl_ready"], 1)

            def moe_keep_a(e, b):
                dve.wait_ge(s["at_full"], e + 1)
                at_least(dve, s["down_full"], 2 * e - 2)
                nc.vector.tensor_copy(AT[b], banks[7][:, :].rearrange("p (k n) -> p k n", k=4)
                                      ).then_inc(s["at_ready"], 1)

            def moe_multiply(e, b):
                dve.wait_ge(s["silu_ready"], e + 1)
                dve.wait_ge(s["up_full"], e + 1)
                at_least(dve, s["at_full"], e - 1)
                nc.vector.tensor_tensor(AA[:, b, :], banks[2 + b][:, :], SG[:, b, :], ALU.mult
                                        ).then_inc(s["a_ready"], 1)

            def moe_keep_y(e, it, b):
                at_least(dve, s[f"y_stored{b}"], 16 * it)
                for half in range(2):
                    dve.wait_ge(s["down_full"], 2 * e + 1 + half)
                    nc.vector.tensor_copy(Y[:, b, half * C:(half + 1) * C], banks[4 + half][:, :]
                                          ).then_inc(s["y_ready"], 1)

            def moe_step(it, r):
                e, b = 2 * it + r, r % 2
                moe_keep_a(e - 1, 1 - b)
                moe_multiply(e, b)
                moe_keep_y(e - 1, it + (r - 1) // 2, 1 - b)

            moe_multiply(0, 0)
            moe_step(0, 1)
            moe_step(0, 2)
            with dve.Fori(1, N_EXP // 2 - 1) as it:
                moe_step(it, 1)
                moe_step(it, 2)
            e = N_EXP - 1
            moe_step(e // 2, 1)
            moe_keep_a(e, 1)
            moe_keep_y(e, e // 2, 1)
            n_over = dve.value_load(ctl[0:1, 7:8], min_val=0, max_val=N_OVER)
            with dve.If(n_over > 0):
                dve.wait_ge(s["y_stored0"], 16 * N_EXP // 2)
                with dve.Fori(0, N_OVER) as j:
                    dve.wait_ge(s["ov_silu_ready"], j + 1)
                    nc.vector.tensor_tensor(AA[:, 0, :], banks[2][:, :], SG[:, 0, :], ALU.mult
                                            ).then_inc(s["ov_a_ready"], 1)
                    dve.wait_ge(s["ov_at_full"], j + 1)
                    nc.vector.tensor_copy(AT[0], banks[7][:, :].rearrange("p (k n) -> p k n", k=4)
                                          ).then_inc(s["ov_at_ready"], 1)
                    dve.wait_ge(s["ov_stored"], 16 * j)
                    for half in range(2):
                        dve.wait_ge(s["ov_down_full"], 2 * j + 1 + half)
                        nc.vector.tensor_copy(Y[:, 0, half * C:(half + 1) * C], banks[4 + half][:, :]
                                              ).then_inc(s["ov_y_ready"], 1)
            for t in range(TT):
                a, b = (2 * t) % 4, (2 * t + 1) % 4
                dve.wait_ge(s[f"yg_loaded{a}"], 16 * (t // 2 + 1))
                dve.wait_ge(s[f"yg_loaded{b}"], 16 * (t // 2 + 1))
                then(nc.vector.tensor_scalar(YG[:, a, :], YG[:, a, :], wts[:, 0, t:t + 1], None, ALU.mult))
                then(nc.vector.scalar_tensor_tensor(YG[:, b, :], YG[:, b, :], wts[:, 1, t:t + 1], YG[:, a, :],
                                                    ALU.mult, ALU.add))
                then(nc.vector.tensor_tensor(YG[:, b, :], YG[:, b, :], gate2, ALU.mult))
                nc.vector.tensor_tensor(X[:, t, :], X[:, t, :], YG[:, b, :], ALU.add).then_inc(s["x_moe"], 1)

            def final_norm(gain):
                k = norms[0]
                norms[0] += 1
                dve.wait_ge(s["ssq_ready"], TT * (k + 1))
                nc.vector.tensor_scalar(var4, ssq[:, 0:TT], 1.0 / D, EPS, ALU.mult, ALU.add
                                        ).then_inc(s["var_ready"], 1)
                dve.wait_ge(s["std_ready"], k + 1)
                then(nc.vector.reciprocal(rstd[:, 0:TT], std4))
                for t in range(TT):
                    nc.vector.scalar_tensor_tensor(X[:, t, :], X[:, t, :], rstd[:, t:t + 1], gain, ALU.mult, ALU.mult
                                                   ).then_inc(s["x_final"], 1)

            final_norm(FGB)
            norm(XN4)
            norm_columns("mix", hT, cols[:, V_MIX:V_MIX + KT])
            for c in range(KT):
                g = FIRST["glu_a"] + c
                dve.wait_ge(s["act_emptied"], emptied("act", FIRST["glu_g"] + c))
                nc.vector.tensor_tensor(V[:, c, PAD:VW_], full(g)[:, :], V[:, c, PAD:VW_], ALU.mult
                                        ).then_inc(s["dve_emptied"], 1)
            dve.wait_ge(s["dve_emptied"], emptied("dve", FIRST["glu_a"] + 7))
            dve.wait_ge(s["pads_set"], 2)
            for c in range(0, KT, 2):
                for j in range(CONV_W):
                    for u in (c, c + 1):
                        tap = col(V_DW, u * CONV_W + j)
                        if j:
                            dve.wait_ge(s["dve_step"], steps[0] - 1)
                            ins = nc.vector.scalar_tensor_tensor(CV[:, u, :], V[:, u, j:j + S], tap, CV[:, u, :],
                                                                 ALU.mult, ALU.add)
                        else:
                            ins = nc.vector.tensor_scalar(CV[:, u, :], V[:, u, 0:S], tap, col(V_DWB, u), ALU.mult,
                                                          ALU.add)
                        if j < CONV_W - 1:
                            steps[0] += 1
                            ins.then_inc(s["dve_step"], 1)
                        else:
                            if u == c:
                                dve.wait_ge(s["dve_step"], steps[0])
                            ins.then_inc(s["conv_ready"], 1)
            bank = full(FIRST["ln_mean"])
            dve.wait_ge(s["conv_ready"], KT)
            for c in range(KT):
                ins = nc.vector.tensor_tensor(CV[:, c, :], CV[:, c, :], bank[:, :], ALU.subtract)
                ins.then_inc(s["centred"], 1)
            dve.wait_ge(s["centred"], KT)
            nc.vector.memset(small[:, 154:155], 0.0).then_inc(s["dve_emptied"], 1)
            nc.vector.tensor_scalar(RSQ, full(FIRST["ln_var"])[:, :], EPS, None, ALU.add).then_inc(s["dve_emptied"], 1)
            dve.wait_ge(s["dve_emptied"], emptied("dve", FIRST["ln_var"]))
            nc.vector.memset(small[:, 154:155], 0.0).then_inc(s["ln_var_ready"], 1)
            dve.wait_ge(s["ln_std_ready"], 1)
            then(nc.vector.reciprocal(RSQ, RSQ))
            for c in range(KT):
                nc.vector.tensor_tensor(CV[:, c, :], CV[:, c, :], RSQ, ALU.mult).then_inc(s["ln_scaled"], 1)
            p3 = [PN[:, i, :].rearrange("p (h n) -> p h n", n=NCMP) for i in range(TT)]
            cm = [small[:, 160 + 16 * i:176 + 16 * i] for i in range(TT)]

            def by_head(i):
                return bass.AP(small, 160 + 16 * i, [[320, P], [1, NH], [0, NCMP]])

            for i in range(TT):
                dve.wait_ge(s["cmp_scores_full"], i + 1)
                then(nc.vector.tensor_scalar(PN[:, i, :], banks[4 + i][:, :], 0.125, None, ALU.mult))
                then(nc.vector.tensor_reduce(cm[i], p3[i], AX, ALU.max))
                nc.vector.tensor_tensor(p3[i], p3[i], by_head(i), ALU.subtract).then_inc(s["cmp_shifted"], 1)
            for i in range(TT):
                dve.wait_ge(s["cmp_exp"], i + 1)
                then(nc.vector.tensor_tensor(p3[i], p3[i], bass.AP(k1, K1_MASK + NCMP * i, [[K1_N, P], [0, NH], [1, NCMP]]),
                                             ALU.mult))
                then(nc.vector.tensor_reduce(cm[i], p3[i], AX, ALU.add))
                then(nc.vector.tensor_scalar(cm[i], cm[i], 1e-30, None, ALU.max))
                then(nc.vector.reciprocal(cm[i], cm[i]))
                then(nc.vector.tensor_tensor(cm[i], cm[i], GS[:, i, 0:NH], ALU.mult))
                nc.vector.tensor_tensor(p3[i], p3[i], by_head(i), ALU.mult).then_inc(s["cmp_probs"], 1)
            for c in range(KT):
                g = FIRST["pw"] + c
                nc.vector.tensor_tensor(GC[:, c, :], full(g)[:, :], GC[:, c, :], ALU.mult).then_inc(s["dve_emptied"], 1)

            def nsa_keep_t(w):
                hb, i = w // 4, w % 4
                dve.wait_ge(s["nsa_t_full"], w + 1)
                if hb >= 2:
                    dve.wait_ge(s["nsa_out"], hb - 1)
                n = (i + 1) * P
                nc.vector.tensor_copy(PTN[hb % 2][:, 0:i + 1, i * P:(i + 1) * P],
                                      banks[7][:, 0:n].rearrange("p (j q) -> p j q", q=P)
                                      ).then_inc(s["nsa_t_ready1"], 1)

            def nsa_keep_outputs(c):
                dve.wait_ge(s["nsa_out"], 4 * c + 4)
                rising = bass.AP(banks[c % 2], P - 1, [[C, P], [P, TT], [-1, P]])
                then(nc.vector.tensor_tensor(TMP.rearrange("p (t q) -> p t q", q=P), rising,
                                             GA[:, c, :].rearrange("p (t q) -> p t q", q=P), ALU.mult))
                nc.vector.tensor_tensor(GC[:, c, :], GC[:, c, :], TMP, ALU.add).then_inc(s["nsa_kept"], 1)
                dve.wait_ge(s["nsa_kept"], c + 1)

            def nsa_inverse(w):
                dve.wait_ge(s["nsa_exp"], w + 1)
                nc.vector.reciprocal(rcp[:, w % 8:w % 8 + 1], sums[:, w % 8:w % 8 + 1]).then_inc(s["nsa_rcp"], 1)

            dve.wait_ge(s["dve_emptied"], emptied("dve", FIRST["pw"] + 7))
            dve.wait_ge(s["cmp_t_full"], TT)
            for w in range(8 * NH):
                h, i = w // 8, w % 4
                n = (i + 1) * P
                if w % 8 == 0:
                    dve.wait_ge(s[f"bias_loaded{h % 2}"], 16 * (h // 2 + 1))
                dve.wait_ge(s["nsa_full"], w + 1)
                if w >= 4:
                    dve.wait_ge(s["nsa_t_full"], w - 3)
                nc.vector.tensor_tensor_reduce(out=PN[:, i, 0:n], in0=banks[2 + w % 4][:, 0:n],
                                               in1=BT[h % 2][:, C - n:C], scale=-0.125, scalar=3e38, op0=ALU.add,
                                               op1=ALU.min, accum_out=nmx[:, w % 8:w % 8 + 1]
                                               ).then_inc(s["nsa_scored"], 1)
                if w >= 1:
                    nsa_inverse(w - 1)
                if w >= 2 and w % 2 == 1:
                    nsa_keep_t(w - 2)
                if w >= 16 and w % 16 == 4:
                    nsa_keep_outputs(w // 16 - 1)
            nsa_inverse(8 * NH - 1)
            nsa_keep_t(8 * NH - 1)
            nsa_keep_outputs(NH // 2 - 1)
            residual("wo2", None)
            norm(XN4)
            norm_columns("normx", hT, cols[:, V_XN:V_XN + KT])

            def x_inverse(w):
                dve.wait_ge(s["x_exp"], w + 1)
                nc.vector.reciprocal(rcp[:, w % 8:w % 8 + 1], sums[:, w % 8:w % 8 + 1]).then_inc(s["x_rcp"], 1)

            for w in range(16):
                dve.wait_ge(s["x_full"], w + 1)
                nc.vector.reduce_max(nmx[:, w % 8:w % 8 + 1], banks[2 + w % 4][:, 0:MEM], AX, negate=True
                                     ).then_inc(s["x_scored"], 1)
                if w:
                    x_inverse(w - 1)
            x_inverse(15)
            residual("xo", None)
            norm(XN4)
            norm_columns("ffn", hT, cols[:, V_FFN:V_FFN + KT])
            for j in range(FT // 2):
                for n in range(2):
                    g = FIRST["ffin"] + 4 * j + 2 + n
                    dve.wait_ge(s["act_emptied"], emptied("act", g - 2))
                    nc.vector.tensor_tensor(GT[:, 2 * j + n, :], full(g)[:, :], SA[:, (2 * j + n) % 4, :], ALU.mult
                                            ).then_inc(s["dve_emptied"], 1)
            for t in range(TT):
                for half in range(2):
                    dve.wait_ge(s["ff_full"], 2 * t + half + 1)
                    piece = slice(half * C, half * C + C)
                    ins = nc.vector.tensor_tensor(X[:, t, piece], banks[2 * t + half][:, :], X[:, t, piece], ALU.add)
                ins.then_inc(s["x_ff"], 1)
            dve.wait_ge(s["fg2_loaded"], 16)
            final_norm(FG2)

        @block.gpsimd
        def _(pool):
            nc.gpsimd.memset(A(8192, D), 0.0).then_inc(s["zeros_set"], 1)
            for t in range(32):
                n = first_score(t + 1) - 1
                i = n % 8
                pool.wait_ge(s["rcp_ready"], t + 1)
                if t < 16:
                    nc.gpsimd.tensor_scalar(PB[:, n % 4, :], PB[:, n % 4, :], rcp[:, i:i + 1], 1.0, ALU.mult, ALU.mult
                                            ).then_inc(s["probs_mla"], 1)
                else:
                    nc.gpsimd.tensor_scalar(PB[:, n % 4, :], PB[:, n % 4, :], rcp[:, 8 + i:9 + i], 1.0, ALU.mult,
                                            ALU.mult).then_inc(s["scaled"], 1)
            pool.wait_ge(s["router_loaded"], 80)
            pool.wait_ge(s["act_emptied"], emptied("act", FIRST["up"] - 1))
            nc.gpsimd.tensor_scalar(scale2, scale2, 1.0, 1.0, ALU.mult, ALU.add).then_inc(s["pool_step"], 1)
            pool.wait_ge(s["pool_step"], 1)
            nc.gpsimd.tensor_tensor(scale2, scale2, G2B, ALU.mult).then_inc(s["pool_step"], 1)
            pool.wait_ge(s["pool_step"], 2)
            for t in range(TT):
                pool.wait_ge(s["xn_ready"], TT + t + 1)
                nc.gpsimd.tensor_tensor(H2[:, t, :], XN2[:, t, :], scale2, ALU.mult).then_inc(s["pool_step"], 1)
                pool.wait_ge(s["pool_step"], 3 + t)
                nc.gpsimd.tensor_tensor(H2[:, t, :], H2[:, t, :], shift2, ALU.add).then_inc(s["h2_ready"], 1)
            pool.wait_ge(s["idx_ready"], 1)
            pool.wait_ge(s["h2_stored"], 64)
            for e in range(N_EXP):
                if e >= 2:
                    pool.wait_ge(s["xt_full"], 2 * (e - 1))
                nc.gpsimd.indirect_dma_start(out=XG[:, e % 2, :], out_offset=None, in_=h2_dram[:, :],
                                             in_offset=bass.IndirectOffsetOnAxis(ap=idx[:, e:e + 1], axis=0)
                                             ).then_inc(s[f"xg_loaded{e % 2}"], 16)
            pool.wait_ge(s["ctl_ready"], 1)
            n_over = pool.value_load(ctl[0:1, 7:8], min_val=0, max_val=N_OVER)
            with pool.If(n_over > 0):
                pool.wait_ge(s["xt_full"], 2 * N_EXP)
                for j in range(N_OVER):
                    if j:
                        pool.wait_ge(s["ov_xt_full"], 2 * j)
                    nc.gpsimd.indirect_dma_start(out=XG[:, 0, :], out_offset=None, in_=h2_dram[:, :],
                                                 in_offset=bass.IndirectOffsetOnAxis(
                                                     ap=idx[:, N_EXP + j:N_EXP + j + 1], axis=0)
                                                 ).then_inc(s["ov_gathered"], 16)
                pool.wait_ge(s["ov_stored"], 16 * N_OVER)
            pool.wait_ge(s["y_stored0"], 16 * N_EXP // 2)
            pool.wait_ge(s["y_stored1"], 16 * N_EXP // 2)
            for n in range(2 * TT):
                if n >= 4:
                    pool.wait_ge(s["x_moe"], n // 2 - 1)
                t, a = n // 2, n % 2
                nc.gpsimd.indirect_dma_start(out=YG[:, n % 4, :], out_offset=None, in_=ys_dram[:, :],
                                             in_offset=bass.IndirectOffsetOnAxis(ap=dest[:, 4 * a + t:4 * a + t + 1],
                                                                                 axis=0)
                                             ).then_inc(s[f"yg_loaded{n % 4}"], 16)
            pool.wait_ge(s["x_final"], 4)
            nc.gpsimd.memset(RB[32:33, :], 8 * NEG).then_inc(s["pads_set"], 1)
            pool.wait_ge(s["pads_set"], 1)
            nc.gpsimd.memset(V[:, :, 0:PAD], 0.0).then_inc(s["pads_set"], 1)
            nc.gpsimd.memset(KCT[:, :, 31:32], 0.0).then_inc(s["pads_set"], 1)
            nc.gpsimd.memset(VC4[:, :, :], 0.0).then_inc(s["pads_set"], 1)
            for w in range(8 * NH):
                h, branch, i = w // 8, w // 4 % 2, w % 4
                n, j = (i + 1) * P, w % 8
                pool.wait_ge(s["nsa_rcp"], w + 1)
                gate = 16 * (branch + 1) + h
                nc.gpsimd.tensor_scalar(PN[:, i, 0:n], PN[:, i, 0:n], rcp[:, j:j + 1], GS[:, i, gate:gate + 1],
                                        ALU.mult, ALU.mult).then_inc(s["nsa_probs"], 1)
            for w in range(16):
                j = w % 8
                pool.wait_ge(s["x_rcp"], w + 1)
                nc.gpsimd.tensor_scalar(PX[:, w % 4, :], PX[:, w % 4, :], rcp[:, j:j + 1], 1.0, ALU.mult, ALU.mult
                                        ).then_inc(s["x_probs"], 1)


INPUTS = ["x", "w_ada", "b_ada", "w_in", "w_q_up", "w_kv_up", "w_out", "w_router_group", "w_router_expert",
          "w_expert_gate", "w_expert_up", "w_expert_down", "final_norm_g", "norm2_g", "mem_2", "w_in_2", "conv_pw_w_2",
          "w_out_2", "xq_w_2", "xkv_w_2", "xo_w_2", "ffn_in_w_2", "ffn_out_w_2", "rel_bias_2", "final_norm_g_2"]


def kernel(**inputs):
    import numpy as np
    import concourse.bacc as bacc
    from concourse.bass_utils import run_bass_kernel_spmd

    f32 = np.float32
    arrays = {n: np.ascontiguousarray(inputs[n]) for n in INPUTS}

    def tiles(a):
        return np.asarray(a).reshape(-1, P).T

    w2 = np.asarray(inputs["cmp_w2_2"])[0].transpose(1, 0, 2).reshape(64, 128)
    pos = np.asarray(inputs["cmp_pos_2"])[0].reshape(2, 16, P).transpose(2, 0, 1).reshape(P, 32)
    arrays["cols"] = np.ascontiguousarray(np.concatenate([
        tiles(inputs["norm1_g"]), tiles(inputs["norm2_g"]), tiles(inputs["norm_mix_g_2"]), tiles(inputs["norm_x_g_2"]),
        tiles(inputs["norm_ffn_g_2"]), tiles(inputs["q_a_norm_g"]), tiles(inputs["kv_a_norm_g"]),
        tiles(inputs["subln_g"]), tiles(inputs["conv_dw_b_2"]), tiles(inputs["conv_ln_g_2"]),
        tiles(inputs["conv_ln_b_2"]), tiles(inputs["c"]),
        np.asarray(inputs["conv_dw_w_2"])[0].reshape(CONV_W, KT, P).transpose(2, 1, 0).reshape(P, KT * CONV_W),
        pos, np.concatenate([w2, w2])], axis=1))
    arrays["lam"] = np.concatenate([np.asarray(inputs[n])[0] for n in ("lambda_q1", "lambda_k1", "lambda_q2",
                                                                      "lambda_k2")])
    arrays["b_router"] = np.concatenate([np.asarray(inputs["b_router_group"])[0],
                                         np.asarray(inputs["b_router_expert"])[0]])
    w1 = np.asarray(inputs["cmp_w1_2"])[0]
    arrays["cmp_w1"] = np.ascontiguousarray(w1.transpose(2, 0, 1, 3).reshape(1, 64, 4096))
    arrays["cmp_w1_flat"] = np.ascontiguousarray(w1.reshape(2, 16, P, 64).transpose(2, 0, 1, 3).reshape(P, 1, 2048))

    tok = np.arange(S)
    inv = (f32(10000.0) ** (-np.arange(0, 64, 2, dtype=f32) / f32(64))).astype(f32)
    ang = tok.astype(f32)[:, None] * inv[None, :]
    cos, sin = np.cos(ang).astype(f32), np.sin(ang).astype(f32)
    by_tile = lambda a: a.reshape(TT, P, -1).transpose(1, 0, 2).reshape(P, -1)
    row = np.arange(P)
    k1 = np.zeros((P, K1_N), f32)
    k1[:, K1_ID:K1_ID + P] = np.eye(P)
    falling = tok.reshape(TT, P)[:, ::-1].reshape(S, 1)
    k1[:, K1_MASK:] = by_tile((falling - (np.arange(NCMP) * 16 + 31)[None, :] >= 0).astype(f32))
    k2 = np.zeros((P, K2_N), f32)
    k2[:, K2_COS:K2_SIN] = by_tile(cos)
    k2[:, K2_SIN:K2_LT] = by_tile(np.concatenate([-sin, sin], axis=1))
    k2[:, K2_LT:K2_IOTA] = row[:, None] < row[None, :]
    k2[:, K2_IOTA:K2_TOK] = row[None, :]
    k2[:, K2_TOK:K2_ANTI] = tok.reshape(TT, P).T
    k2[:, K2_ANTI:K2_N] = np.eye(P)[:, ::-1]
    arrays["k1"], arrays["k2"] = k1, k2

    def buckets(dist):
        n = np.maximum(dist, 0)
        large = 16 + (np.log(np.maximum(n, 1).astype(f32) / f32(16)) / f32(np.log(8)) * f32(16)).astype(np.int32)
        b = np.where(n < 16, n, np.minimum(large, 31))
        b = np.where(dist >= 0, b, 32)
        return (b[None, :] == np.arange(33)[:, None]).astype(f32)

    arrays["onehot"] = buckets(511 - np.arange(NG))

    nc = bacc.Bacc("TRN2", target_bir_lowering=False, num_devices=1)
    io, sent = {}, {}
    for name, a in arrays.items():
        sent[f"in_{name}"] = a
        io[name] = nc.dram_tensor(f"in_{name}", a.shape, mybir.dt.from_np(a.dtype), kind="ExternalInput").ap()
    io["out"] = nc.dram_tensor("out", (1, S, D), F32, kind="ExternalOutput").ap()
    build(nc, io)
    r = run_bass_kernel_spmd(nc, [sent], core_ids=[0])
    return r.results[0]["out"]
```

```python
from contextlib import ExitStack

import concourse.bass as bass
from concourse import mybir

F32 = mybir.dt.float32
F32R = mybir.dt.float32r
I32 = mybir.dt.int32
ALU = mybir.AluOpType
ACT = mybir.ActivationFunctionType
AX = mybir.AxisListType.X

P = 128
S = 512
TT = S // P
D = 1024
KT = D // P
EPS = 1e-6
C = 512
SLOT = KT * C
N_DENSE_SLOTS = 4
N_SLOTS = 6
MLA_SCALE = (128 + 64) ** -0.5
DIFF_SCALE = 64 ** -0.5
LAMBDA_INIT = 0.8 - 0.6
NEG = -1e30
N_EXP = 32
D_EXP = 512
CAP = P
N_OVER = 7
N_BLOCKS = N_EXP + N_OVER
CONV_W = 31
PAD = CONV_W - 1
VW_ = PAD + S
NH = 16
NCMP = 32
D_FF = 2816
FT = D_FF // P
NG = 1040
MEM = 256

K1_ID, K1_MASK, K1_N = 0, 128, 256
K2_COS, K2_SIN, K2_LT, K2_IOTA, K2_TOK, K2_ANTI, K2_N = 0, 128, 384, 512, 640, 644, 772
V_N1, V_N2, V_MIX, V_XN, V_FFN, V_QA, V_KVA, V_SUB, V_DWB, V_LNG, V_LNB, V_C = (
    0, 8, 16, 24, 32, 40, 42, 44, 45, 53, 61, 69)
V_DW, V_POS, V_W2, V_N = 77, 77 + KT * CONV_W, 77 + KT * CONV_W + 32, 77 + KT * CONV_W + 32 + 128


GROUPS = []
FIRST = {}
CHUNK_LAST = []
CHUNK_DMAS = []


def plan(stage, engines, chunks=0, dmas=1):
    FIRST[stage] = len(GROUPS)
    GROUPS.extend(engines)
    per = len(engines) // chunks if chunks else 0
    for c in range(chunks):
        CHUNK_LAST.append(FIRST[stage] + per * (c + 1) - 1)
        CHUNK_DMAS.append(dmas)


plan("ada0", ["act"] * 4, 4)
plan("modcols", ["dve"])
plan("c", ["act"] * 4, 1)
plan("ada1", ["act"] * 2, 2)
plan("kpe", ["dve"] * 4, 1)
plan("dq", ["dve"] * 4, 1)
plan("ada2", ["act"] * 2, 2)
plan("dk", ["dve"] * 4, 1)
plan("ada3", ["act"] * 2, 2)
plan("dv", ["act"] * 4, 1)
plan("ada4", ["act"] * 2, 2)
plan("modcols2", ["dve"])
plan("up", ["act"] * 12 + ["dve"] * 4, 1, 2)
plan("wo", ["dve"] * 8, 2)
B1_CHUNKS = len(CHUNK_LAST)
plan("router", ["dve"] * 4)
plan("rank", ["dve"])
plan("over", ["dve"])
plan("slots", ["dve"])
B2_FIRST = len(GROUPS)
plan("toep", ["act"] * 3)
for _n in range(2):
    plan(f"glu_g{_n}", ["act"] * 4, 1)
    plan(f"glu_a{_n}", ["dve"] * 4, 1)
plan("q2", ["act"] * 8, 2)
plan("kvc", ["act"] * 4, 1)
plan("kk", ["act"] * 4, 1, 2)
plan("vv", ["act"] * 4, 1, 2)
plan("gh", ["act"] * 4)
plan("pos", ["act"] * 2)
plan("ga0", ["act"] * 4, 1)
plan("gates_falling", ["act"])
plan("cmp1", ["act"] * 4, 1, 2)
plan("ga1", ["act"] * 4, 1)
plan("ln_mean", ["dve"])
plan("gc0", ["act"] * 4, 1)
plan("ln_var", ["dve"])
plan("gc1", ["act"] * 4, 1)
plan("cmp2", ["act"] * 2)
plan("pw", ["dve"] * 8, 2)
plan("wo2", ["dve"] * 8, 2)
plan("xk", ["act"] * 8, 2)
plan("xv", ["act"] * 4, 2)
plan("xq", ["act"] * 8, 2)
plan("xo", ["dve"] * 8, 2)
plan("ffin", ["act", "act", "dve", "dve"] * (FT // 2), FT // 2, 2)
FFOUT = [4, 4, 4, 4, 4, 2]


def emptied(engine, g):
    return sum(e == engine for e in GROUPS[:g + 1])


CHUNK_DMAS += [1] * len(FFOUT)


def slot_of(c):
    return c % N_DENSE_SLOTS if c < B1_CHUNKS - 2 else (c - B1_CHUNKS) % 2


def before(c):
    return max([i for i in range(c) if slot_of(i) == slot_of(c)], default=-1)


def loaded_value(c):
    return 16 * sum(CHUNK_DMAS[i] for i in range(c + 1) if slot_of(i) == slot_of(c))


HALVES = []
FIRST_HALF = {}
at = B1_CHUNKS - 2
used = 0
for _stage, _n, _cols in (("wo", 2, 2048), ("glu_g0", 1, 2048), ("glu_a0", 1, 2048), ("glu_g1", 1, 2048),
                          ("glu_a1", 1, 2048), ("q2", 2, 2048), ("kvc", 1, 2048), ("kk", 1, 2048),
                          ("vv", 1, 2048), ("ga0", 1, 2048), ("cmp1", 1, 0), ("ga1", 1, 2048), ("gc0", 1, 2048), ("gc1", 1, 2048), ("pw", 2, 2048), ("wo2", 2, 2048), ("xk", 2, 2048),
                          ("xv", 2, 2048), ("xq", 2, 2048), ("xo", 2, 2048), ("ffin", FT // 2, 2048)):
    if _cols:
        FIRST_HALF[_stage] = len(HALVES)
        for _c in range(at, at + _n):
            if _stage == "ffin":
                HALVES.append((_c, 0, _cols, "proj_done", CHUNK_LAST[_c] - 1))
            else:
                used += 1
                HALVES.append((_c, 0, _cols, "half_used", used))
            HALVES.append((_c, 1, _cols, "proj_done", CHUNK_LAST[_c] + 1))
    at += _n
FIRST_HALF["ffout"] = len(HALVES)
used = 0
for _n, _k in enumerate(FFOUT):
    for _half in range(_k // 2):
        used += 1
        HALVES.append((at + _n, _half, 2048, "ff_used", used))


XP = {}
at = 0
for _stage, _n in (("norm1", KT), ("latents", 4), ("kpe", 1), ("dq", 4), ("dk", 4), ("qpe", 2), ("norm2", KT),
                   ("mix", KT), ("mem", KT), ("normx", KT), ("ffn", KT)):
    XP[_stage] = at
    at += _n
NORM_NO = {"norm1": 0, "norm2": 1, "mix": 2, "normx": 3, "ffn": 4}
ADA_GROUP = [FIRST["ada0"] + j for j in range(4)] + [FIRST[f"ada{(j - 2) // 2}"] + j % 2 for j in range(4, 12)]


def first_score(t):
    return t if t < 16 else 16 + 2 * (t - 16)


def unit_of(n):
    return n if n < 16 else 16 + (n - 16) // 2


MORE_SEMS = (["tile_high", "tile_low", "cmp_read", "extras_loaded", "gates_high", "gates_low", "half_used", "w_high", "w_low", "x_high",   "x_kept_low",
                "sq_used", "onehot_loaded", "bias_rows_ready", "bias_stored", "pads_set", "conv_ready", "centred", "squared",
              "ln_var_ready", "ln_std_ready", "ln_scaled", "conv_act_ready", "cmp_bias_loaded", "cmp_scores_full",
              "cmp_shifted", "cmp_exp", "cmp_probs", "cmp_t_full", "cmp_t_ready", "bias_loaded0", "bias_loaded1",
              "nsa_full", "nsa_scored", "nsa_exp", "nsa_rcp", "nsa_probs", "nsa_t_full", "nsa_t_ready0", "nsa_t_ready1",
              "nsa_out", "nsa_kept", "mem_loaded", "x_full", "x_scored", "x_exp", "x_rcp", "x_probs", "x_t_full",
              "x_t_ready", "x_out", "x_kept", "ff_used", "ff_full", "x_ff", "fg2_loaded", "router_loaded", "zeros_set", "zeros_stored", "h2_ready", "h2_stored", "pool_step", "router_exp_in", "router_exp_out", "onehot_ready",
              "idx_ready", "ctl_ready", "gate_full", "up_full", "down_full", "xt_full", "xt_ready", "silu_ready",
              "a_ready", "at_full", "at_ready", "y_ready", "x_moe", "x_final"]
             + [f"{n}{b}" for n in ("gate_loaded", "up_loaded", "down_loaded", "xg_loaded", "y_stored") for b in range(2)]
             + [f"yg_loaded{n}" for n in range(4)]
             + ["ov_" + n for n in ("loaded", "gathered", "xt_full", "xt_ready", "up_full", "silu_ready", "a_ready",
                                    "at_full", "at_ready", "down_full", "y_ready", "stored")])


def build(nc, io):
    ctx = ExitStack()
    with ctx:
        def sb(name, shape, dt=F32):
            return ctx.enter_context(nc.sbuf_tensor(name, shape, dt))

        def sem(name):
            return ctx.enter_context(nc.semaphore(name))

        def dram(name, shape, dt=F32):
            return nc.dram_tensor(name, shape, dt, kind="Internal").ap()

        with ExitStack() as names:
            low_r, high_r, xl_r, lent_r, area0_r, area1_r, area2_r = (
                names.enter_context(nc.sbuf_tensor(name, [P, n], F32R)) for name, n in (
                    ("low_r", 2 * SLOT), ("high_r", SLOT), ("xl_r", SLOT), ("lent_r", 2 * SLOT),
                    ("area0_r", 4096), ("area1_r", 8432 - 4096), ("area2_r", FT * C)))
        slots = sb("slots", [P, N_SLOTS * SLOT])
        area = sb("area", [P, 22016])
        X = sb("X", [P, TT, D])
        late = sb("late", [P, 1024])
        k1 = sb("k1", [P, K1_N])
        cols = sb("cols", [P, V_N])
        ones = sb("ones", [P, P])
        ones_d = sb("ones_d", [P, P])
        ctl = sb("ctl", [P, 8], I32)
        idx = sb("idx", [P, N_BLOCKS], I32)
        dest = sb("dest", [P, 2 * TT], I32)
        wts = sb("wts", [P, 2, TT])
        small = sb("small", [P, 320])
        banks = [ctx.enter_context(nc.psum_tensor(f"bank{i}", [P, C], F32)) for i in range(8)]

        def slot(i):
            return slots[:, i * SLOT:(i + 1) * SLOT]

        def A(off, n, *dims):
            v = area[:, off:off + n]
            return v.rearrange("p (a b) -> p a b", a=dims[0]) if dims else v

        def E(off, n, *dims):
            v = slots[:, 4 * SLOT + off:4 * SLOT + off + n]
            return v.rearrange("p (a b) -> p a b", a=dims[0]) if dims else v

        def AR(off, n, *dims):
            piece, at = (area0_r, 0) if off < 4096 else (area1_r, 4096) if off < 8432 else (area2_r, 8432)
            v = piece[:, off - at:off - at + n]
            return v.rearrange("p (a b) -> p a b", a=dims[0]) if dims else v

        def raw_half(m):
            c, half, n = HALVES[m][:3]
            return slot(slot_of(c))[:, half * n:(half + 1) * n]

        def high_half(m):
            return high_r[:, m % 2 * 2048:m % 2 * 2048 + HALVES[m][2]]

        def low_half(m):
            c, half, n = HALVES[m][:3]
            return low_r[:, slot_of(c) * SLOT + half * n:slot_of(c) * SLOT + (half + 1) * n]

        ID = k1[:, K1_ID:K1_ID + P]
        MASK = k1[:, K1_MASK:K1_N].rearrange("p (a b) -> p a b", a=TT)
        COS = late[:, K2_COS:K2_SIN].rearrange("p (t b) -> p t b", t=TT)
        SIN = late[:, K2_SIN:K2_LT].rearrange("p (t b) -> p t b", t=TT)
        LT = late[:, K2_LT:K2_IOTA]
        IOTA = late[:, K2_IOTA:K2_TOK]
        TOK = late[:, K2_TOK:K2_ANTI]
        ANTI = late[:, K2_ANTI:K2_N]

        def col(v, n):
            return cols[:, v + n:v + n + 1]

        hT = A(0, 4096, KT)
        mixT = A(0, 4096, KT)
        gate1, shift2, scale2, gate2 = (A(4096 + i * D, D) for i in range(4))
        modb = A(4096, 4096, 8)
        DV = A(8192, 2048, TT)
        CTN = A(10240, 2048, TT)
        KPE = A(12288, C)
        DQ = A(12800, 2048, 4)
        DK = A(14848, 2048, 4)
        Z = A(16896, 2048, TT)
        QN = A(16896, 2048, 4)
        RQ = A(18944, 2048, TT)
        KN = A(18944, 2048, 4)
        RT = A(20992, C)
        QPE = A(20992, 1024, 2)
        early = E(0, 2048, 4)
        ada_acc = E(2048, 2048, 4)
        XN1 = E(4096, 4096, TT)
        QRT = E(4096, 1024, TT)
        PT = [E(0, 2048, TT), E(2048, 2048, TT)]
        PB = E(4096, 2048, 4)
        VM = E(6144, 2048, TT)
        PB_MORE = A(18944, 2048, 4)

        def prob_tile(n):
            return PB[:, n % 4, :] if n < 16 or n % 8 < 4 else PB_MORE[:, n % 4, :]

        A1, B1, A2, B2 = (small[:, i * 8:i * 8 + 8] for i in range(4))
        ssq = small[:, 32:48]
        rstd = small[:, 48:64]
        csil = small[:, 64:72]
        lamv = small[:, 72:80]
        nmx = small[:, 80:96]
        sums = small[:, 96:112]
        rcp = small[:, 112:128]
        badar = A(21504, C)
        lamin = A(14848, 256)
        SUBS = A(16896, 2048, 4)
        WOT = E(0, 1024, 2)
        varc, var4, stdc, std4 = small[:, 128:136], small[:, 136:140], small[:, 140:148], small[:, 148:152]

        XN2 = A(8192, 4096, TT)
        XN3 = A(8192, 4096, TT)
        h2T = A(0, 4096, KT)
        H2 = A(12288, 4096, TT)
        G2B = A(20992, D)
        FGB = A(19968, D)
        WR = A(18944, 288, KT)
        BR = A(19300, 36)
        LO = A(4096, 1024, 8)
        HI = A(19364, 8 * N_BLOCKS, 8)
        XG = A(0, 2048, 2)
        XT = [A(2048, 1024, KT), A(3072, 1024, KT)]
        SG = A(4096, 1024, 2)
        AA = A(5120, 1024, 2)
        AT = [A(6144, 512, 4), A(6656, 512, 4)]
        Y = A(8192, 2048, 2)
        YG = [A(10240 + i * D, D) for i in range(4)] + [A(i * D, D) for i in range(4)]

        OH = A(14336, NG)
        RB = A(16000, NH)
        BROW = A(16400, NG)
        XN4 = A(8432, 4096, TT)
        V = A(4096, KT * VW_, KT)
        GC = A(4096, 4096, KT)
        CV = A(8432, 4096, KT)
        Q = A(12528, 4096, KT)
        KK = [A(16624, 2048, 4), A(18672, 2048, 4)]
        VV = E(0, 2048, TT)
        KC, VC = E(2048, 1024, 2), E(3072, 1024, 2)
        GA = E(4096, 4096, KT)
        GS = A(20720, TT * 48, TT)
        GRISE = A(21568, TT * 48, TT)
        KCB = A(21760, 8 * NCMP).rearrange("p (u a n) -> p u a n", u=4, a=2)
        VC4 = A(21040, 4 * 64, 4)
        ZC = A(21296, 2 * 124, 2)
        POSB = A(21544, 2)
        SQ = [late[:, 0:C], late[:, C:2 * C]]
        RSQ = late[:, 0:C]
        PN = A(0, 2048, TT)
        PTN = [A(2048, 2048, TT), A(8432, 2048, TT)]
        PCT = A(10480, 2048, TT)
        BCT = E(2048, 2048, NH)
        TMP = E(2048, C)
        WG = E(4096, KT * 48, KT)
        WP = E(6144, 2048).rearrange("p (a j e) -> p a j e", a=2, e=64)
        WGS = (lent_r[:, 4480:4864].rearrange("p (a b) -> p a b", a=KT),
               lent_r[:, 4096:4480].rearrange("p (a b) -> p a b", a=KT))
        XL = xl_r[:].rearrange("p (a b) -> p a b", a=KT)
        hTS = (AR(0, 4096, KT), XL)
        WOS = (XL, AR(0, 4096, KT))
        CVS = (XL, AR(8432, 4096, KT))
        GCS = (XL, AR(4096, 4096, KT))
        MTS = (lent_r[:, 2048:4096].rearrange("p (a b) -> p a b", a=KT),
               xl_r[:, 0:2048].rearrange("p (a b) -> p a b", a=KT))
        OTS = (AR(4096, 4096, KT), XL)
        GTL = AR(8432, FT * C, FT)
        GTH = [lent_r[:, f * C:(f + 1) * C] for f in range(16)
               ] + [AR(5120 + f * C, C) for f in range(FT - 16)]
        BT = [late[:, 0:C], late[:, C:2 * C]]
        MTOK = E(0, 2048, 2)
        MT = E(2048, 2048, KT)
        XK = E(4096, 2048, KT)
        XV = E(6144, 2048, 2)
        OT = A(4096, 4096, KT)
        XQ = A(12528, 4096, KT)
        PX = A(16624, 1024, 4)
        PTX = [A(17648, 1024, 2), A(18672, 1024, 2)]
        GT = A(8432, FT * C, FT)
        SA = A(19696, 2048, 4)
        FG2 = A(4096, D)

        g_dram = dram("bias_falling", [NH, NG])
        h2_dram = dram("h2_rows", [S, D])
        ys_dram = dram("expert_rows", [N_BLOCKS * CAP, D])

        names = ["w_loaded0", "w_loaded1", "w_loaded2", "w_loaded3", "cols_loaded", "x_loaded", "consts", "bada", "lamload",
                 "proj_done", "act_emptied", "dve_emptied", "ones_set", "ada_acc", "mod_ready",
                 "act_step", "dve_step", "csil_ready",
                 "ssq_ready", "var_ready", "std_ready", "xn_ready", "xpose_full", "bank6_emptied", "bank7_emptied",
                 "latent_var", "latent_std", "latents_ready", "rope_ready",
                 "lam_ready", "lam_exp", "scores_full", "exp_done", "max_ready", "rcp_ready", "scaled",
                 "probs_mla", "probs_diff", "pt_full", "pt_ready", "pv_full", "pv_emptied",
                 "sub_squares", "sub_full", "sub_var", "sub_std", "sub_ready", "x_ready", "out_done"] + MORE_SEMS
        s = {n: sem(n) for n in names}
        w_loaded = [s[f"w_loaded{i}"] for i in range(N_DENSE_SLOTS)]
        xpose_emptied = [s["bank6_emptied"], s["bank7_emptied"]]
        emptied_sem = {"act": s["act_emptied"], "dve": s["dve_emptied"]}
        block = ctx.enter_context(nc.Block())

        def at_least(engine, semaphore, value):
            if not isinstance(value, int) or value > 0:
                engine.wait_ge(semaphore, value)

        def RS(off, n):
            return A(16384 + off, n)

        def RM(t):
            return RS(672 + 32 * t, 32)

        def R3(off, *dims):
            return bass.AP(area, 16384 + off, [[22016, P]] + [list(d) for d in dims])

        def w3(ap):
            return ap.rearrange("(k p) n -> p k n", p=P)

        ADA_PARTS = [[0, 1, 2, 3], [4, 5], [6, 7], [8, 9], [10, 11]]
        GLU_AT = (21, 23, 24, 26)
        CHUNK_NO = {}
        at = 0
        for name, n in (("ada0", 4), ("c", 1), ("ada1", 2), ("kpe", 1), ("dq", 1), ("ada2", 2), ("dk", 1), ("ada3", 2),
                        ("dv", 1), ("ada4", 2), ("up", 1), ("wo", 2),
                        ("glu_g0", 1), ("glu_a0", 1), ("glu_g1", 1), ("glu_a1", 1), ("q2", 2), ("kvc", 1), ("kk", 1),
                        ("vv", 1), ("ga0", 1), ("cmp1", 1), ("ga1", 1), ("gc0", 1), ("gc1", 1),
                        ("pw", 2), ("wo2", 2), ("xk", 2), ("xv", 2), ("xq", 2),
                        ("xo", 2), ("ffin", FT // 2), ("ffout", len(FFOUT))):
            CHUNK_NO[name] = at
            at += n

        @block.sync
        def _(sp):
            def chunk(c, loads):
                prev = before(c)
                if prev >= len(CHUNK_LAST):
                    sp.wait_ge(s["ff_used"], 2 * (prev - len(CHUNK_LAST) + 1))
                elif prev >= 0 and not B1_CHUNKS <= c < B1_CHUNKS + 2:
                    sp.wait_ge(s["proj_done"], CHUNK_LAST[prev] + 1)
                i = slot_of(c)
                for off, src in loads:
                    k, n = src.shape[1], src.shape[2]
                    dst = slot(i)[:, off:off + k * n].rearrange("p (k n) -> p k n", k=k)
                    sp.dma_start(dst, src).then_inc(w_loaded[slot_of(c)], 16)

            w_ada, w_in, w_out = w3(io["w_ada"][0]), w3(io["w_in"][0]), w3(io["w_out"][0])
            sp.dma_start(X[:], io["x"][0].rearrange("(t p) d -> p t d", p=P)).then_inc(s["x_loaded"], 16)

            def ada(part):
                for n, j in enumerate(ADA_PARTS[part]):
                    chunk(CHUNK_NO[f"ada{part}"] + n, [(0, w_ada[:, :, j * C:(j + 1) * C])])

            ada(0)
            chunk(CHUNK_NO["c"], [(0, w_in[:, :, 0:512])])
            ada(1)
            chunk(CHUNK_NO["kpe"], [(0, w_in[:, :, 512:576])])
            chunk(CHUNK_NO["dq"], [(0, w_in[:, :, 576:1088])])
            ada(2)
            sp.wait_ge(s["zeros_set"], 1)
            sp.dma_start(ys_dram[N_EXP * CAP:, :].rearrange("(b p) d -> p b d", p=P),
                         bass.AP(area, 8192, [[22016, P], [0, N_OVER], [1, D]])).then_inc(s["zeros_stored"], 16)
            chunk(CHUNK_NO["dk"], [(0, w_in[:, :, 1088:1600])])
            ada(3)
            chunk(CHUNK_NO["dv"], [(0, w_in[:, :, 1600:2112])])
            ada(4)
            chunk(CHUNK_NO["up"], [(0, w3(io["w_q_up"][0])), (2 * 768, w3(io["w_kv_up"][0]))])
            for n in range(2):
                chunk(CHUNK_NO["wo"] + n, [(0, w_out[:, :, n * C:(n + 1) * C])])
            sp.wait_ge(s["pv_emptied"], 8)
            sp.wait_ge(s["sub_ready"], 4)
            sp.dma_start(G2B, io["norm2_g"][0].partition_broadcast(P)).then_inc(s["router_loaded"], 16)
            sp.dma_start(FGB, io["final_norm_g"].partition_broadcast(P)).then_inc(s["router_loaded"], 16)
            sp.dma_start(WR[:, :, 0:4], w3(io["w_router_group"][0])).then_inc(s["router_loaded"], 16)
            sp.dma_start(WR[:, :, 4:36], w3(io["w_router_expert"][0])).then_inc(s["router_loaded"], 16)
            sp.dma_start(BR, io["b_router"].partition_broadcast(P)).then_inc(s["router_loaded"], 16)

            wg = io["w_expert_gate"][0].rearrange("e (k p) n -> p e k n", p=P)
            wu = io["w_expert_up"][0].rearrange("e (k p) n -> p e k n", p=P)
            wd = io["w_expert_down"][0].rearrange("e (k p) n -> p e k n", p=P)

            def expert_weight(i, w, e, loaded):
                k, n = w.shape[2], w.shape[3]
                sp.dma_start(slot(i).rearrange("p (a k n) -> p a k n", a=1, k=k), w[:, bass.ds(e, 1), :, :]
                             ).then_inc(loaded, 16)

            sp.wait_ge(s["proj_done"], FIRST["wo"] + 4)
            expert_weight(0, wg, 0, s["gate_loaded0"])
            sp.wait_ge(s["proj_done"], FIRST["wo"] + 8)
            expert_weight(1, wu, 0, s["up_loaded0"])
            expert_weight(2, wd, 0, s["down_loaded0"])
            expert_weight(3, wg, 1, s["gate_loaded1"])
            sp.wait_ge(s["x_ready"], 8)
            expert_weight(4, wu, 1, s["up_loaded1"])
            expert_weight(5, wd, 1, s["down_loaded1"])
            for t in range(TT):
                sp.wait_ge(s["h2_ready"], t + 1)
                sp.dma_start(h2_dram[t * P:(t + 1) * P, :], H2[:, t, :]).then_inc(s["h2_stored"], 16)
            with sp.Fori(1, N_EXP // 2) as it:
                for r in range(2):
                    e = 2 * it + r
                    sp.wait_ge(s["gate_full"], e - 1)
                    expert_weight(3 * r, wg, e, s[f"gate_loaded{r}"])
                    sp.wait_ge(s["up_full"], e - 1)
                    expert_weight(3 * r + 1, wu, e, s[f"up_loaded{r}"])
                    sp.wait_ge(s["down_full"], 2 * e - 2)
                    expert_weight(3 * r + 2, wd, e, s[f"down_loaded{r}"])
            sp.wait_ge(s["down_full"], 2 * N_EXP)
            sp.wait_ge(s["ctl_ready"], 1)
            n_over = sp.value_load(ctl[0:1, 7:8], min_val=0, max_val=N_OVER)
            with sp.If(n_over > 0):
                with sp.Fori(0, N_OVER) as j:
                    sp.wait_ge(s["down_full"], 2 * N_EXP + 2 * j)
                    e = sp.value_load(ctl[0:1, bass.ds(j, 1)], min_val=0, max_val=N_EXP - 1)
                    expert_weight(0, wg, e, s["ov_loaded"])
                    expert_weight(1, wu, e, s["ov_loaded"])
                    expert_weight(2, wd, e, s["ov_loaded"])
                sp.wait_ge(s["down_full"], 2 * N_EXP + 2 * N_OVER)
            for t in range(TT):
                sp.wait_ge(s[f"yg_loaded{t}"], 32)
            sp.dma_start(OH[0:33, :], io["onehot"]).then_inc(s["onehot_loaded"], 16)
            sp.dma_start(RB[0:32, :], io["rel_bias_2"]).then_inc(s["onehot_loaded"], 16)
            sp.dma_start(WG, w3(io["w_in_2"][0])[:, :, 4608:4656]).then_inc(s["extras_loaded"], 16)
            sp.dma_start(E(6144, 2048), io["cmp_w1_flat"][:, 0, :]).then_inc(s["extras_loaded"], 16)
            w2, pw, wo2 = w3(io["w_in_2"][0]), w3(io["conv_pw_w_2"][0]), w3(io["w_out_2"][0])
            xq, xkv, xo = w3(io["xq_w_2"][0]), w3(io["xkv_w_2"][0]), w3(io["xo_w_2"][0])
            ffin, ffout = w3(io["ffn_in_w_2"][0]), w3(io["ffn_out_w_2"][0])

            def halves(stage, w, first):
                for n in range(2):
                    chunk(CHUNK_NO[stage] + n, [(0, w[:, :, first + n * C:first + (n + 1) * C])])

            for n in range(2):
                chunk(CHUNK_NO[f"glu_g{n}"], [(0, w2[:, :, 1024 + n * C:1024 + (n + 1) * C])])
                chunk(CHUNK_NO[f"glu_a{n}"], [(0, w2[:, :, n * C:(n + 1) * C])])
            sp.wait_ge(s["act_emptied"], emptied("act", FIRST["toep"] + 2))
            sp.dma_start(g_dram, BROW[0:NH, :]).then_inc(s["bias_stored"], 16)
            halves("q2", w2, 2048)
            chunk(CHUNK_NO["kvc"], [(0, w2[:, :, 3072:3584])])

            def two(stage, first, second):
                c = CHUNK_NO[stage]
                sp.wait_ge(s["proj_done"], CHUNK_LAST[c - 2] + 1)
                for n, at in enumerate((first, second)):
                    sp.dma_start(slot(slot_of(c)).rearrange("p (k n) -> p k n", k=KT)[:, :, n * 256:n * 256 + 256],
                                 w2[:, :, at:at + 256]).then_inc(w_loaded[slot_of(c)], 16)

            two("kk", 3584, 4096)
            two("vv", 3840, 4352)
            chunk(CHUNK_NO["ga0"], [(0, w2[:, :, 5680:6192])])
            c = CHUNK_NO["cmp1"]
            sp.wait_ge(s["proj_done"], CHUNK_LAST[c - 2] + 1)
            for a in range(2):
                sp.dma_start(slot(slot_of(c))[64 * a:64 * a + 64, :], io["cmp_w1"][0]
                             ).then_inc(w_loaded[slot_of(c)], 16)
            chunk(CHUNK_NO["ga1"], [(0, w2[:, :, 6192:6704])])
            chunk(CHUNK_NO["gc0"], [(0, w2[:, :, 4656:5168])])
            sp.wait_ge(s["proj_done"], FIRST["cmp1"] + 4)
            sp.wait_ge(s["bias_stored"], 16)
            for i in range(TT):
                sp.dma_start(BCT[32 * i:32 * i + 32, :, :],
                             bass.AP(g_dram.tensor, 415 - i * P, [[16, NCMP], [NG, NH], [1, P]])
                             ).then_inc(s["cmp_bias_loaded"], 16)
            chunk(CHUNK_NO["gc1"], [(0, w2[:, :, 5168:5680])])
            halves("pw", pw, 0)

            def bias_tile(h):
                sp.dma_start(BT[h % 2], bass.AP(g_dram.tensor, h * NG, [[1, P], [1, C]])
                             ).then_inc(s[f"bias_loaded{h % 2}"], 16)

            sp.wait_ge(s["ln_scaled"], KT)
            bias_tile(0)
            bias_tile(1)
            halves("wo2", wo2, 0)
            for h in range(2, NH):
                sp.wait_ge(s["nsa_scored"], 8 * (h - 1))
                bias_tile(h)
            sp.wait_ge(s["nsa_kept"], NH // 2)
            sp.dma_start(MTOK, io["mem_2"][0].rearrange("(t p) d -> p t d", p=P)).then_inc(s["mem_loaded"], 16)
            halves("xk", xkv, 0)
            halves("xv", xkv, 1024)
            halves("xq", xq, 0)
            halves("xo", xo, 0)
            for j in range(FT // 2):
                if j == 2:
                    sp.wait_ge(s["proj_done"], FIRST["xo"] + 8)
                    sp.dma_start(FG2, io["final_norm_g_2"].partition_broadcast(P)).then_inc(s["fg2_loaded"], 16)
                chunk(CHUNK_NO["ffin"] + j, [(0, ffin[:, :, j * 256:j * 256 + 256]),
                                             (2048, ffin[:, :, D_FF + j * 256:D_FF + j * 256 + 256])])
            k0 = 0
            for n, k in enumerate(FFOUT):
                chunk(CHUNK_NO["ffout"] + n, [(0, ffout[:, k0:k0 + k, :])])
                k0 += k
            for t in range(TT):
                sp.wait_ge(s["x_final"], TT + t + 1)
                sp.dma_start(io["out"][0, t * P:(t + 1) * P, :], X[:, t, :]).then_inc(s["out_done"], 16)
            sp.wait_ge(s["out_done"], 16 * TT)

        @block.tensor
        def _(pe):
            def bank_of(g):
                if g >= 4:
                    engine = GROUPS[g - 4]
                    pe.wait_ge(emptied_sem[engine], emptied(engine, g - 4))
                return banks[g % 4]

            def all_emptied(g):
                for engine in ("act", "dve"):
                    pe.wait_ge(emptied_sem[engine], emptied(engine, g - 1))

            def loaded(c):
                pe.wait_ge(w_loaded[slot_of(c)], loaded_value(c))
                return slot(slot_of(c))

            def accumulate(out, pairs):
                for n, (lhsT, rhs) in enumerate(pairs):
                    last = nc.tensor.matmul(out, lhsT, rhs, start=(n == 0), stop=(n == len(pairs) - 1))
                return last

            def token_major(stage, xT, n_cols, chunk_no, tiles=TT, first=0):
                w = loaded(chunk_no)[:, 0:KT * n_cols].rearrange("p (k n) -> p k n", k=KT)
                for t in range(tiles):
                    g = FIRST[stage] + first + t
                    accumulate(bank_of(g)[:, 0:n_cols],
                               [(xT[:, k, t * P:(t + 1) * P], w[:, k, :]) for k in range(KT)]
                               ).then_inc(s["proj_done"], 1)

            def feature_major(stage, xT, chunk_no, first=0, n_tiles=4, tokens=S):
                w = loaded(chunk_no)[:, 0:KT * n_tiles * P].rearrange("p (k n) -> p k n", k=KT)
                for j in range(n_tiles):
                    g = FIRST[stage] + first + j
                    accumulate(bank_of(g)[:, 0:tokens],
                               [(w[:, k, j * P:(j + 1) * P], xT[:, k, 0:tokens]) for k in range(KT)]
                               ).then_inc(s["proj_done"], 1)

            def split_product(out, pairs, start=True, stop=True):
                for n, (xh, xl, yh, yl) in enumerate(pairs):
                    nc.tensor.matmul(out, xh, yh, start=start and n == 0, stop=False)
                    nc.tensor.matmul(out, xh, yl, start=False, stop=False)
                    last = nc.tensor.matmul(out, xl, yh, start=False, stop=stop and n == len(pairs) - 1)
                return last

            def parts(m, k):
                pe.wait_ge(s["w_low"], m + 1)
                return (high_half(m).rearrange("p (k n) -> p k n", k=k), low_half(m).rearrange("p (k n) -> p k n", k=k))

            def split_groups(stage, n, tiles, width, operands, more_tiles=0):
                for half in range(2):
                    m = FIRST_HALF[stage] + 2 * n + half
                    wh, wl = parts(m, 4)
                    if half and more_tiles:
                        pe.wait_ge(s["tile_low"], more_tiles)
                    for t in range(tiles):
                        g = FIRST[stage] + n * tiles + t
                        out = (banks[g % 4] if half else bank_of(g))[:, 0:width]
                        last = split_product(out, [operands(4 * half + k, k, wh, wl, t) for k in range(4)],
                                             start=half == 0, stop=half == 1)
                        if half:
                            last.then_inc(s["proj_done"], 1)
                    if half == 0:
                        last.then_inc(s["half_used"], 1)

            def split_token_major(stage, x, n_cols, n=0, tiles=TT, more_tiles=0):
                split_groups(stage, n, tiles, n_cols,
                             lambda k, kw, wh, wl, t: (x[0][:, k, t * P:(t + 1) * P], x[1][:, k, t * P:(t + 1) * P],
                                                       wh[:, kw, :], wl[:, kw, :]), more_tiles)

            def split_feature_major(stage, x, n=0, tokens=S):
                split_groups(stage, n, 4, tokens,
                             lambda k, kw, wh, wl, t: (wh[:, kw, t * P:(t + 1) * P], wl[:, kw, t * P:(t + 1) * P],
                                                       x[0][:, k, 0:tokens], x[1][:, k, 0:tokens]))

            def transposes(n, pieces):
                if n >= 2:
                    pe.wait_ge(xpose_emptied[n % 2], n // 2)
                for c0, src in pieces:
                    rows = src.shape[1]
                    last = nc.tensor.transpose(banks[6 + n % 2][0:rows, c0:c0 + P], src, ID)
                last.then_inc(s["xpose_full"], 1)

            def transpose_tokens(stage, XT, n_tiles, width=P, c_first=0):
                for c in range(n_tiles):
                    transposes(XP[stage] + c, [(t * P, XT[:, t, c * width:(c + 1) * width]) for t in range(TT)])

            def transposed_emptied(n):
                pe.wait_ge(xpose_emptied[0], (n + 1) // 2)
                pe.wait_ge(xpose_emptied[1], n // 2)

            def norm_transposes(n, XN):
                pe.wait_ge(s["xn_ready"], TT * (NORM_NO[n] + 1))
                transpose_tokens(n, XN, KT)
                transposed_emptied(XP[n] + KT)
            def ada(part):
                for n, j in enumerate(ADA_PARTS[part]):
                    g = FIRST[f"ada{part}"] + n
                    pe.wait_ge(s["ada_acc"], j + 1)
                    bank = bank_of(g)
                    b = 2 * (j % 2)
                    accumulate(bank[:, :], [(ones[:, :], ada_acc[:, b, :]), (ones[:, :], ada_acc[:, b + 1, :]),
                                            (ID[0:12, j:j + 1].to_broadcast([12, P]), badar[0:12, 0:C])]
                               ).then_inc(s["proj_done"], 1)

            def mod_columns(stage, rows):
                bank = bank_of(FIRST[stage])
                for n in range(16):
                    row = rows[n // 4]
                    last = nc.tensor.matmul(bank[:, n:n + 1], row[0:1, (n % 4) * P:(n % 4 + 1) * P], ones[0:1, 0:1],
                                            start=True, stop=True)
                last.then_inc(s["proj_done"], 1)

            pe.wait_ge(s["consts"], 32)
            pe.wait_ge(s["ones_set"], 1)
            pe.wait_ge(s["bada"], 16)
            ada(0)
            pe.wait_ge(s["act_emptied"], emptied("act", FIRST["modcols"] - 1))
            mod_columns("modcols", [early[:, i, :] for i in range(4)])
            norm_transposes("norm1", XN1)
            token_major("c", hT, C, CHUNK_NO["c"])
            ada(1)
            token_major("kpe", hT, 64, CHUNK_NO["kpe"])
            pe.wait_ge(s["latents_ready"], TT)
            transpose_tokens("latents", Z, 4)
            token_major("dq", hT, C, CHUNK_NO["dq"])
            pe.wait_ge(s["rope_ready"], TT)
            transpose_tokens("kpe", RQ, 1, 64)
            ada(2)
            pe.wait_ge(s["rope_ready"], 2 * TT)
            transpose_tokens("dq", Z, 4)
            token_major("dk", hT, C, CHUNK_NO["dk"])
            ada(3)
            pe.wait_ge(s["rope_ready"], 3 * TT)
            transpose_tokens("dk", RQ, 4)
            token_major("dv", hT, C, CHUNK_NO["dv"])
            ada(4)
            pe.wait_ge(s["act_emptied"], emptied("act", FIRST["modcols2"] - 1))
            mod_columns("modcols2", [modb[:, i, :] for i in (2, 3, 4, 5)])
            transposed_emptied(XP["dk"] + 4)
            w = loaded(CHUNK_NO["up"])
            wq = w[:, 0:1536].rearrange("p (k h n) -> p k h n", k=2, n=192)
            wkv = w[:, 1536:1536 + 2048].rearrange("p (k h n) -> p k h n", k=2, n=256)
            g = FIRST["up"]
            for h in range(4):
                accumulate(bank_of(g)[:, :], [(wq[:, k, h, 0:P], CTN[:, k, :]) for k in range(2)]
                           ).then_inc(s["proj_done"], 1)
                g += 1
            for h in range(4):
                accumulate(bank_of(g)[:, :], [(wkv[:, k, h, 0:P], CTN[:, 2 + k, :]) for k in range(2)]
                           ).then_inc(s["proj_done"], 1)
                g += 1
            for t in range(TT):
                accumulate(bank_of(g)[:, :].rearrange("p (h n) -> p h n", h=4),
                           [(CTN[:, 2 + k, t * P:(t + 1) * P], wkv[:, k, :, P:2 * P]) for k in range(2)]
                           ).then_inc(s["proj_done"], 1)
                g += 1
            for t in range(TT):
                accumulate(bank_of(g)[:, 0:256].rearrange("p (h n) -> p h n", h=4),
                           [(CTN[:, k, t * P:(t + 1) * P], wq[:, k, :, P:192]) for k in range(2)]
                           ).then_inc(s["proj_done"], 1)
                g += 1
            pe.wait_ge(s["rope_ready"], 4 * TT)
            transpose_tokens("qpe", QRT, 2)

            all_emptied(g)
            transposed_emptied(XP["qpe"] + 2)

            def scores(t):
                h, i = t // TT % 4, t % TT
                if t < 16:
                    n, a = t, 64 * (h % 2)
                    if n >= 4:
                        pe.wait_ge(s["exp_done"], n - 3)
                    accumulate(banks[2 + n % 4][:, :],
                               [(QN[:, h, i * P:(i + 1) * P], KN[:, h, :]),
                                (QPE[a:a + 64, h // 2, i * P:(i + 1) * P], KPE[a:a + 64, :])]
                               ).then_inc(s["scores_full"], 1)
                else:
                    for half in range(2):
                        n, a = 16 + 2 * (t - 16) + half, 64 * half
                        pe.wait_ge(s["exp_done"], n - 3)
                        accumulate(banks[2 + n % 4][:, :], [(DQ[a:a + 64, h, i * P:(i + 1) * P], DK[a:a + 64, h, :])]
                                   ).then_inc(s["scores_full"], 1)

            def outputs(h):
                pe.wait_ge(s["pt_ready"], TT * (h + 1))
                if h >= 2:
                    pe.wait_ge(s["pv_emptied"], h - 1)
                V, c0 = (VM, h * P) if h < 4 else (DV, (h - 4) * P)
                accumulate(banks[h % 2][:, :], [(V[:, j, c0:c0 + P], PT[h % 2][:, j, :]) for j in range(TT)]
                           ).then_inc(s["pv_full"], 1)

            scores(0)
            scores(1)
            for t in range(32):
                if t + 2 < 32:
                    scores(t + 2)
                if t < 16:
                    pe.wait_ge(s["probs_mla"], t + 1)
                else:
                    pe.wait_ge(s["probs_diff"], t - 15)
                if t >= 2:
                    pe.wait_ge(s["pt_ready"], t - 1)
                pb = prob_tile(first_score(t))
                for j in range(TT):
                    last = nc.tensor.transpose(banks[6 + t % 2][:, j * P:(j + 1) * P], pb[:, j * P:(j + 1) * P], ID)
                last.then_inc(s["pt_full"], 1)
                if t >= 5 and t % TT == 1:
                    outputs(t // TT - 1)
            outputs(7)

            def sub_sums(h):
                pe.wait_ge(s["sub_squares"], h + 1)
                accumulate(banks[4 + h][:, :], [(ones[:, :], SUBS[:, h, :])]).then_inc(s["sub_full"], 1)

            pe.wait_ge(s["pt_ready"], 32)
            for h in range(3):
                sub_sums(h)

            pe.wait_ge(s["pv_emptied"], 8)
            sub_sums(3)
            pe.wait_ge(s["tile_low"], 4)
            for n in range(2):
                split_token_major("wo", WOS, C, n, more_tiles=KT)
            norm_transposes("norm2", XN2)
            pe.wait_ge(s["router_loaded"], 80)
            for t in range(TT):
                g = FIRST["router"] + t
                accumulate(bank_of(g)[:, 0:36], [(h2T[:, k, t * P:(t + 1) * P], WR[:, k, :]) for k in range(KT)]
                           ).then_inc(s["proj_done"], 1)
            pe.wait_ge(s["onehot_ready"], 1)
            bank = bank_of(FIRST["rank"])
            for t in range(TT):
                accumulate(bank[:, t * 32:t * 32 + 32],
                           [(LT if u == t else ones[:, :], RM(u)) for u in range(t + 1)])
            accumulate(bank[0:32, 128:256], [(RM(u), ones[:, :]) for u in range(TT)]).then_inc(s["proj_done"], 1)
            pe.wait_ge(s["onehot_ready"], 2)
            bank = bank_of(FIRST["over"])
            accumulate(bank[:, 0:32], [(RS(1056, P)[0:32, :], LT[0:32, 0:32])])
            accumulate(bank[:, 32:64], [(RS(1056, P)[0:32, :], ID[0:32, 0:32])]).then_inc(s["proj_done"], 1)
            pe.wait_ge(s["onehot_ready"], 3)
            accumulate(bank_of(FIRST["slots"])[:, 0:N_BLOCKS], [(LO[:, n, :], HI[:, n, :]) for n in range(8)]
                       ).then_inc(s["proj_done"], 1)

            all_emptied(FIRST["slots"] + 1)
            transposed_emptied(XP["norm2"] + KT)

            def moe_transpose_x(e, it, b):
                at_least(pe, s[f"xg_loaded{b}"], 16 * (it + 1))
                at_least(pe, s["xt_ready"], 2 * e)
                at_least(pe, s["at_ready"], e - 1)
                for half in range(2):
                    for k in range(4):
                        c = 4 * half + k
                        last = nc.tensor.transpose(banks[6 + half][:, k * P:(k + 1) * P], XG[:, b, c * P:(c + 1) * P],
                                                   ID)
                    last.then_inc(s["xt_full"], 1)

            def moe_up(e, it, b):
                pe.wait_ge(s["xt_ready"], 2 * e + 2)
                at_least(pe, s["a_ready"], e - 1)
                for which, loaded_sem, full_sem in ((0, f"gate_loaded{b}", "gate_full"), (1, f"up_loaded{b}", "up_full")):
                    pe.wait_ge(s[loaded_sem], 16 * (it + 1))
                    w = slot(3 * b + which).rearrange("p (k n) -> p k n", k=KT)
                    accumulate(banks[2 * which + b][:, :], [(XT[b][:, k, :], w[:, k, :]) for k in range(KT)]
                               ).then_inc(s[full_sem], 1)

            def moe_transpose_a(e, b):
                pe.wait_ge(s["a_ready"], e + 1)
                at_least(pe, s["at_ready"], e)
                for k in range(4):
                    last = nc.tensor.transpose(banks[7][:, k * P:(k + 1) * P], AA[:, b, k * P:(k + 1) * P], ID)
                last.then_inc(s["at_full"], 1)

            def moe_down(e, it, b):
                pe.wait_ge(s["at_ready"], e + 1)
                pe.wait_ge(s[f"down_loaded{b}"], 16 * (it + 1))
                w = slot(3 * b + 2).rearrange("p (k n) -> p k n", k=4)
                for half in range(2):
                    at_least(pe, s["y_ready"], 2 * e - 1 + half)
                    accumulate(banks[4 + half][:, :],
                               [(AT[b][:, k, :], w[:, k, half * C:(half + 1) * C]) for k in range(4)]
                               ).then_inc(s["down_full"], 1)

            def moe_step(it, r):
                e, b = 2 * it + r, r % 2
                pe.wait_ge(s["xt_ready"], 2 * e + 2)
                moe_transpose_a(e - 1, 1 - b)
                moe_up(e, it + r // 2, b)
                moe_transpose_x(e + 1, it + (r + 1) // 2, 1 - b)
                moe_down(e - 1, it + (r - 1) // 2, 1 - b)

            moe_transpose_x(0, 0, 0)
            moe_up(0, 0, 0)
            moe_transpose_x(1, 0, 1)
            moe_step(0, 1)
            moe_step(0, 2)
            with pe.Fori(1, N_EXP // 2 - 1) as it:
                moe_step(it, 1)
                moe_step(it, 2)
            e = N_EXP - 1
            pe.wait_ge(s["xt_ready"], 2 * N_EXP)
            moe_transpose_a(e - 1, 0)
            moe_up(e, e // 2, 1)
            moe_down(e - 1, e // 2, 0)
            moe_transpose_a(e, 1)
            moe_down(e, e // 2, 1)

            pe.wait_ge(s["y_ready"], 2 * N_EXP)
            pe.wait_ge(s["ctl_ready"], 1)
            n_over = pe.value_load(ctl[0:1, 7:8], min_val=0, max_val=N_OVER)
            with pe.If(n_over > 0):
                with pe.Fori(0, N_OVER) as j:
                    pe.wait_ge(s["ov_gathered"], 16 * j + 16)
                    for half in range(2):
                        for k in range(4):
                            c = 4 * half + k
                            last = nc.tensor.transpose(banks[6 + half][:, k * P:(k + 1) * P],
                                                       XG[:, 0, c * P:(c + 1) * P], ID)
                        last.then_inc(s["ov_xt_full"], 1)
                    pe.wait_ge(s["ov_xt_ready"], 2 * j + 2)
                    pe.wait_ge(s["ov_loaded"], 48 * j + 48)
                    for which in range(2):
                        w = slot(which).rearrange("p (k n) -> p k n", k=KT)
                        accumulate(banks[2 * which][:, :], [(XT[0][:, k, :], w[:, k, :]) for k in range(KT)]
                                   ).then_inc(s["ov_up_full"], 1)
                    pe.wait_ge(s["ov_a_ready"], j + 1)
                    for k in range(4):
                        last = nc.tensor.transpose(banks[7][:, k * P:(k + 1) * P], AA[:, 0, k * P:(k + 1) * P], ID)
                    last.then_inc(s["ov_at_full"], 1)
                    pe.wait_ge(s["ov_at_ready"], j + 1)
                    w = slot(2).rearrange("p (k n) -> p k n", k=4)
                    for half in range(2):
                        accumulate(banks[4 + half][:, :],
                                   [(AT[0][:, k, :], w[:, k, half * C:(half + 1) * C]) for k in range(4)]
                                   ).then_inc(s["down_full"], 1)
                    pe.wait_ge(s["ov_y_ready"], 2 * j + 2)
            pe.wait_ge(s["onehot_loaded"], 32)
            pe.wait_ge(s["bias_rows_ready"], 1)
            for n in range(3):
                width = C if n < 2 else NG - 2 * C
                g = FIRST["toep"] + n
                accumulate(bank_of(g)[0:NH, 0:width], [(RB[0:33, :], OH[0:33, n * C:n * C + width])]
                           ).then_inc(s["proj_done"], 1)
            norm_transposes("mix", XN4)
            for n in range(2):
                split_feature_major(f"glu_g{n}", hTS)
                split_feature_major(f"glu_a{n}", hTS)
            for n in range(2):
                split_feature_major("q2", hTS, n)
            split_feature_major("kvc", hTS)
            split_feature_major("kk", hTS)
            split_token_major("vv", hTS, C)
            pe.wait_ge(s["gates_low"], 1)
            for t in range(TT):
                split_product(bank_of(FIRST["gh"] + t)[:, 0:48],
                              [(hTS[0][:, k, t * P:(t + 1) * P], hTS[1][:, k, t * P:(t + 1) * P], WGS[0][:, k, :],
                                WGS[1][:, k, :]) for k in range(KT)]).then_inc(s["proj_done"], 1)
            pe.wait_ge(s["extras_loaded"], 32)
            for a in range(2):
                accumulate(bank_of(FIRST["pos"] + a)[0:64, 0:1],
                           [(WP[:, a, j, :], cols[:, V_POS + 16 * a + j:V_POS + 16 * a + j + 1]) for j in range(16)]
                           ).then_inc(s["proj_done"], 1)
            split_feature_major("ga0", hTS)
            pe.wait_ge(s["act_emptied"], emptied("act", FIRST["gh"] + 3))
            bank = bank_of(FIRST["gates_falling"])
            for t in range(TT):
                last = nc.tensor.matmul(bank[:, t * 48:(t + 1) * 48], ANTI, GRISE[:, t, :], start=True, stop=True)
            last.then_inc(s["proj_done"], 1)
            w = loaded(CHUNK_NO["cmp1"]).rearrange("p (a l e) -> p a l e", a=2, e=64)
            for a in range(2):
                pair = [bank_of(FIRST["cmp1"] + 2 * a + half) for half in range(2)]
                off = 4 * SLOT + 2048 + 1024 * a
                for l in range(32):
                    for half in range(2):
                        last = nc.tensor.matmul(pair[half][0:64, 0:62].rearrange("p (c n) -> p c n", c=2),
                                                w[64 * half:64 * half + 64, a, l, :],
                                                bass.AP(slots, 64 * half * N_SLOTS * SLOT + off + l,
                                                        [[N_SLOTS * SLOT, 64], [C, 2], [16, 31]]),
                                                start=l == 0, stop=l == 31)
                        if l == 31:
                            last.then_inc(s["proj_done"], 1)
            split_feature_major("ga1", hTS)
            pe.wait_ge(s["conv_ready"], KT)
            accumulate(bank_of(FIRST["ln_mean"])[:, :], [(ones_d[:, :], CV[:, c, :]) for c in range(KT)]
                       ).then_inc(s["proj_done"], 1)
            split_feature_major("gc0", hTS)
            bank = bank_of(FIRST["ln_var"])
            for c in range(KT):
                pe.wait_ge(s["squared"], c + 1)
                last = nc.tensor.matmul(bank[:, :], ones_d[:, :], SQ[c % 2], start=(c == 0), stop=(c == KT - 1))
                last.then_inc(s["proj_done" if c == KT - 1 else "sq_used"], 1)
            split_feature_major("gc1", hTS)
            pe.wait_ge(s["act_emptied"], emptied("act", FIRST["cmp1"] + 3))
            accumulate(bank_of(FIRST["cmp2"])[0:64, 0:124], [(cols[0:64, V_W2:V_W2 + 64], ZC[0:64, 0, :])]
                       ).then_inc(s["proj_done"], 1)
            bank = bank_of(FIRST["cmp2"] + 1)
            for u in range(4):
                last = nc.tensor.matmul(bank[0:31, u * 64:u * 64 + 64], ZC[0:64, 1, u * 31:u * 31 + 31],
                                        cols[0:64, V_W2 + 64:V_W2 + P], start=True, stop=True)
            last.then_inc(s["proj_done"], 1)
            transposed_emptied(XP["mix"] + KT)
            pe.wait_ge(s["cmp_bias_loaded"], 64)
            for h in range(NH):
                nc.tensor.matmul(banks[4 + h // 4][:, h % 4 * P:(h % 4 + 1) * P], BCT[:, h, :], ID, start=(h % 4 == 0),
                                 stop=False)
            pe.wait_ge(s["act_emptied"], emptied("act", FIRST["cmp2"] + 1))
            for g in range(4):
                for c in (2 * g, 2 * g + 1):
                    out = banks[4 + g][:, c % 2 * 256:c % 2 * 256 + 256].rearrange("p (a i n) -> p a i n", a=2, i=TT)
                    for i in range(TT):
                        last = nc.tensor.matmul(out[:, :, i, :], Q[:, c, i * P:(i + 1) * P], KCB[:, 2 * (g % 2) + g // 2],
                                                start=False, stop=(c % 2 == 1 and i == TT - 1))
                last.then_inc(s["cmp_scores_full"], 1)
            pe.wait_ge(s["tile_low"], 2 * KT)
            for n in range(2):
                split_feature_major("pw", CVS, n)
            all_emptied(FIRST["pw"] + 8)

            def nsa_scores(w):
                h, branch, i = w // 8, w // 4 % 2, w % 4
                a, g = 64 * (h % 2), h // 4
                if w >= 4:
                    pe.wait_ge(s["nsa_scored"], w - 3)
                n = (i + 1) * P
                accumulate(banks[2 + w % 4][:, 0:n], [(Q[a:a + 64, h // 2, i * P:(i + 1) * P], KK[branch][a:a + 64, g, 0:n])]
                           ).then_inc(s["nsa_full"], 1)

            def nsa_outputs(hb):
                h, branch = hb // 2, hb % 2
                a, g, r, u = 64 * (h % 2), h // 4, 32 * (h % 4), 2 * (h // 4 % 2) + h // 8
                bank = banks[h // 2 % 2]
                if branch == 0:
                    if h >= 4 and h % 2 == 0:
                        pe.wait_ge(s["nsa_kept"], h // 2 - 1)
                    nc.tensor.matmul(bank[a:a + 64, :], VC4[r:r + 32, u, :], PCT[r:r + 32, g, :], start=True, stop=False)
                pe.wait_ge(s["nsa_t_ready0"], 2 * hb + 2)
                pe.wait_ge(s["nsa_t_ready1"], 2 * hb + 2)
                for j in range(TT):
                    c0 = branch * 256 + g * 64
                    last = nc.tensor.matmul(bank[a:a + 64, j * P:C], VV[:, j, c0:c0 + 64], PTN[hb % 2][:, j, j * P:C],
                                            start=False, stop=(branch == 1 and j == TT - 1))
                last.then_inc(s["nsa_out"], 1)

            pe.wait_ge(s["cmp_read"], 1)
            nsa_scores(0)
            nsa_scores(1)
            for i in range(TT):
                pe.wait_ge(s["cmp_probs"], i + 1)
                if i >= 2:
                    pe.wait_ge(s["cmp_t_ready"], i - 1)
                for g in range(4):
                    last = nc.tensor.transpose(banks[6 + i % 2][:, g * P:(g + 1) * P], PN[:, i, g * P:(g + 1) * P], ID)
                last.then_inc(s["cmp_t_full"], 1)
            pe.wait_ge(s["cmp_t_ready"], TT)
            nsa_scores(2)
            for w in range(8 * NH):
                i = w % 4
                if w + 3 < 8 * NH:
                    nsa_scores(w + 3)
                pe.wait_ge(s["nsa_probs"], w + 1)
                if w >= 2:
                    pe.wait_ge(s[f"nsa_t_ready{w % 2}"], w // 2)
                for j in range(i + 1):
                    last = nc.tensor.transpose(banks[6 + w % 2][:, j * P:(j + 1) * P], PN[:, w % 4, j * P:(j + 1) * P],
                                               ID)
                last.then_inc(s["nsa_t_full"], 1)
                if w >= 4 and i == 1:
                    nsa_outputs(w // 4 - 1)
            nsa_outputs(2 * NH - 1)

            pe.wait_ge(s["tile_low"], 3 * KT)
            for n in range(2):
                split_token_major("wo2", GCS, C, n)
            pe.wait_ge(s["mem_loaded"], 16)
            for c in range(KT):
                transposes(XP["mem"] + c, [(t * P, MTOK[:, t, c * P:(c + 1) * P]) for t in range(2)])
            transposed_emptied(XP["mem"] + KT)
            for n in range(2):
                split_feature_major("xk", MTS, n, tokens=MEM)
            for n in range(2):
                split_token_major("xv", MTS, C, n, tiles=2)
            norm_transposes("normx", XN4)
            for n in range(2):
                split_feature_major("xq", hTS, n)
            all_emptied(FIRST["xq"] + 8)

            def x_scores(w):
                h, i = w // 4, w % 4
                if w >= 4:
                    pe.wait_ge(s["x_exp"], w - 3)
                accumulate(banks[2 + w % 4][:, 0:MEM], [(XQ[:, 2 * h + c, i * P:(i + 1) * P], XK[:, 2 * h + c, :])
                                                        for c in range(2)]).then_inc(s["x_full"], 1)

            def x_outputs(h):
                pe.wait_ge(s["x_t_ready"], 4 * h + 4)
                for half in range(2):
                    if h:
                        pe.wait_ge(s["x_kept_low"], 2 * h - 1 + half)
                    c0 = h * 256 + half * P
                    accumulate(banks[half][:, :], [(XV[:, m, c0:c0 + P], PTX[h % 2][:, m, :]) for m in range(2)]
                               ).then_inc(s["x_out"], 1)

            transposed_emptied(XP["normx"] + KT)
            x_scores(0)
            x_scores(1)
            for w in range(16):
                if w + 2 < 16:
                    x_scores(w + 2)
                pe.wait_ge(s["x_probs"], w + 1)
                if w >= 2:
                    pe.wait_ge(s["x_t_ready"], w - 1)
                for m in range(2):
                    last = nc.tensor.transpose(banks[6 + w % 2][:, m * P:(m + 1) * P], PX[:, w % 4, m * P:(m + 1) * P],
                                               ID)
                last.then_inc(s["x_t_full"], 1)
                if w >= 4 and w % 4 == 1:
                    x_outputs(w // 4 - 1)
            x_outputs(3)
            pe.wait_ge(s["x_kept_low"], 8)
            for n in range(2):
                split_token_major("xo", OTS, C, n)

            pe.wait_ge(s["x_t_ready"], 16)
            norm_transposes("ffn", XN4)
            for j in range(FT // 2):
                for n in range(4):
                    if n % 2 == 0:
                        wh, wl = parts(FIRST_HALF["ffin"] + 2 * j + n // 2, KT)
                    c = slice(n % 2 * P, n % 2 * P + P)
                    split_product(bank_of(FIRST["ffin"] + 4 * j + n)[:, :],
                                  [(wh[:, k, c], wl[:, k, c], hTS[0][:, k, :], hTS[1][:, k, :]) for k in range(KT)]
                                  ).then_inc(s["proj_done"], 1)
            all_emptied(FIRST["ffin"] + 2 * FT)
            transposed_emptied(XP["ffn"] + KT)
            for f in range(FT):
                if f % 2 == 0:
                    wh, wl = parts(FIRST_HALF["ffout"] + f // 2, 2)
                    pe.wait_ge(s["tile_low"], 3 * KT + f + 2)
                for t in range(TT):
                    for half in range(2):
                        tokens, out_cols = slice(t * P, (t + 1) * P), slice(half * C, (half + 1) * C)
                        last = split_product(banks[2 * t + half][:, :],
                                             [(GTH[f][:, tokens], GTL[:, f, tokens], wh[:, f % 2, out_cols],
                                               wl[:, f % 2, out_cols])], start=f == 0, stop=f == FT - 1)
                        if f == FT - 1:
                            last.then_inc(s["ff_full"], 1)
                if f % 2 == 1 and f < FT - 1:
                    last.then_inc(s["ff_used"], 1)

        @block.scalar
        def _(act):
            steps = [0]

            def then(ins):
                steps[0] += 1
                ins.then_inc(s["act_step"], 1)
                act.wait_ge(s["act_step"], steps[0])

            def full(g):
                act.wait_ge(s["proj_done"], g + 1)
                return banks[g % 4]

            def empty(ins):
                ins.then_inc(s["act_emptied"], 1)

            act.dma_start(cols[:], io["cols"]).then_inc(s["cols_loaded"], 16)
            act.dma_start(k1[:], io["k1"]).then_inc(s["consts"], 16)
            act.dma_start(late[:, 0:K2_N], io["k2"]).then_inc(s["consts"], 16)
            act.dma_start(badar[0:12, 0:C], io["b_ada"][0].rearrange("(a n) -> a n", a=12)).then_inc(s["bada"], 16)
            act.dma_start(lamin, io["lam"].partition_broadcast(P)).then_inc(s["lamload"], 16)
            act.wait_ge(s["cols_loaded"], 16)
            nc.scalar.activation(csil, cols[:, V_C:V_C + KT], ACT.Silu).then_inc(s["csil_ready"], 1)

            def transposed(n):
                act.wait_ge(s["xpose_full"], n + 1)
                return banks[6 + n % 2]

            def norm(XN, ready=None, first=1):
                k = norms[0]
                norms[0] += 1
                for t in range(TT):
                    if ready is not None:
                        act.wait_ge(ready, first + t)
                    nc.scalar.activation(XN[:, t, :], X[:, t, :], ACT.Square, accum_out=ssq[:, t:t + 1]
                                         ).then_inc(s["ssq_ready"], 1)
                act.wait_ge(s["var_ready"], k + 1)
                nc.scalar.activation(std4, var4, ACT.Sqrt).then_inc(s["std_ready"], 1)

            norms = [0]

            def norm_columns(stage, hT, scale, bias=None):
                for c in range(0, KT, 2):
                    n = XP[stage] + c
                    b = transposed(n)
                    if bias is None:
                        ins = nc.scalar.activation(hT[:, c, :], b[:, :], ACT.Copy, scale=scale[:, c:c + 1])
                    else:
                        ins = nc.scalar.activation(hT[:, c, :], b[:, :], ACT.Identity, bias=bias[:, c:c + 1],
                                                   scale=scale[:, c:c + 1])
                    ins.then_inc(xpose_emptied[n % 2], 1)

            def split_weights(upto_half):
                while highs[0] < upto_half:
                    m = highs[0]
                    c, half = HALVES[m][:2]
                    if m >= 2:
                        act.wait_ge(s[HALVES[m - 2][3]], HALVES[m - 2][4])
                    if half == 0:
                        act.wait_ge(w_loaded[slot_of(c)], loaded_value(c))
                    nc.scalar.activation(high_half(m), raw_half(m), ACT.Copy).then_inc(s["w_high"], 1)
                    highs[0] += 1

            highs = [0]

            def split_columns(stage, scale):
                for c in range(KT):
                    nc.scalar.activation(hTS[0][:, c, :], transposed(XP[stage] + c)[:, :], ACT.Copy,
                                         scale=scale[:, c:c + 1]).then_inc(s["x_high"], 1)

            def ada(part):
                for n, j in enumerate(ADA_PARTS[part]):
                    bank = full(FIRST[f"ada{part}"] + n)
                    out = early[:, j, :] if j < 4 else modb[:, j - 4, :]
                    empty(nc.scalar.activation(out, bank[:, :], ACT.Copy))

            act.wait_ge(s["x_loaded"], 16)
            norm(XN1)
            ada(0)
            act.wait_ge(s["mod_ready"], 1)
            norm_columns("norm1", hT, A1, B1)
            for t in range(TT):
                bank = full(FIRST["c"] + t)
                nc.scalar.activation(Z[:, t, :], bank[:, :], ACT.Copy)
                for half in range(2):
                    piece = slice(256 * half, 256 * half + 256)
                    last = nc.scalar.activation(RQ[:, t, piece], bank[:, piece], ACT.Square,
                                                accum_out=ssq[:, 4 + 2 * t + half:5 + 2 * t + half])
                empty(last)
            act.wait_ge(s["latent_var"], 1)
            nc.scalar.activation(stdc, varc, ACT.Sqrt).then_inc(s["latent_std"], 1)
            ada(1)
            for c in range(4):
                n = XP["latents"] + c
                nc.scalar.activation(CTN[:, c, :], transposed(n)[:, :], ACT.Copy, scale=col(V_QA, c)
                                     ).then_inc(xpose_emptied[n % 2], 1)
            n = XP["kpe"]
            nc.scalar.activation(KPE[0:64, :], transposed(n)[0:64, :], ACT.Copy)
            nc.scalar.activation(KPE[64:128, :], banks[6 + n % 2][0:64, :], ACT.Copy).then_inc(xpose_emptied[n % 2], 1)
            ada(2)
            for c in range(4):
                n = XP["dq"] + c
                nc.scalar.activation(DQ[:, c, :], transposed(n)[:, :], ACT.Copy, scale=DIFF_SCALE
                                     ).then_inc(xpose_emptied[n % 2], 1)
            ada(3)
            for c in range(4):
                n = XP["dk"] + c
                nc.scalar.activation(DK[:, c, :], transposed(n)[:, :], ACT.Copy).then_inc(xpose_emptied[n % 2], 1)
            act.wait_ge(s["zeros_stored"], 16)
            for t in range(TT):
                empty(nc.scalar.activation(DV[:, t, :], full(FIRST["dv"] + t)[:, :], ACT.Copy))
            ada(4)
            g = FIRST["up"]
            for h in range(4):
                empty(nc.scalar.activation(QN[:, h, :], full(g + h)[:, :], ACT.Copy, scale=MLA_SCALE))
            for h in range(4):
                empty(nc.scalar.activation(KN[:, h, :], full(g + 4 + h)[:, :], ACT.Copy))
            for t in range(TT):
                empty(nc.scalar.activation(VM[:, t, :], full(g + 8 + t)[:, :], ACT.Copy))
            for c in range(2):
                n = XP["qpe"] + c
                nc.scalar.activation(QPE[:, c, :], transposed(n)[:, :], ACT.Copy, scale=MLA_SCALE
                                     ).then_inc(xpose_emptied[n % 2], 1)
            split_weights(2)
            act.wait_ge(s["lam_ready"], 1)
            nc.scalar.activation(lamv[:, 2:4], lamv[:, 0:2], ACT.Exp).then_inc(s["lam_exp"], 1)

            def keep_pt(t):
                h, i = t // TT, t % TT
                act.wait_ge(s["pt_full"], t + 1)
                if h >= 2:
                    act.wait_ge(s["pv_full"], h - 1)
                nc.scalar.activation(PT[h % 2][:, :, i * P:(i + 1) * P],
                                     banks[6 + t % 2][:, :].rearrange("p (j q) -> p j q", j=TT), ACT.Copy
                                     ).then_inc(s["pt_ready"], 1)

            def keep_outputs(h):
                act.wait_ge(s["pv_full"], h + 1)
                if h >= 4:
                    nc.scalar.activation(SUBS[:, h - 4, :], banks[h % 2][:, :], ACT.Square
                                         ).then_inc(s["sub_squares"], 1)
                nc.scalar.activation(mixT[:, h, :], banks[h % 2][:, :], ACT.Copy).then_inc(s["pv_emptied"], 1)

            def split_head(h):
                if h < 4:
                    act.wait_ge(s["pv_emptied"], h + 1)
                else:
                    act.wait_ge(s["sub_ready"], h - 3)
                nc.scalar.activation(WOS[0][:, h, :], mixT[:, h, :], ACT.Copy).then_inc(s["tile_high"], 1)

            for t in range(32):
                for n in range(first_score(t), first_score(t + 1)):
                    act.wait_ge(s["max_ready"], n + 1)
                    if 4 <= n < 20:
                        act.wait_ge(s["pt_full"], unit_of(n - 4) + 1)
                    elif n >= 24:
                        act.wait_ge(s["pt_full"], unit_of(n - 8) + 1)
                    nc.scalar.activation(prob_tile(n), banks[2 + n % 4][:, :], ACT.Exp, bias=nmx[:, n % 8:n % 8 + 1],
                                         accum_out=sums[:, n % 8:n % 8 + 1]).then_inc(s["exp_done"], 1)
                if t >= 2:
                    keep_pt(t - 2)
                if t >= 7 and t % TT == 3:
                    keep_outputs(t // TT - 1)
                    if t // TT - 1 < 4:
                        split_head(t // TT - 1)
            keep_pt(30)
            keep_pt(31)
            keep_outputs(7)
            for h in range(4):
                act.wait_ge(s["sub_var"], h + 1)
                nc.scalar.activation(SUBS[:, h, :], SUBS[:, h, :], ACT.Sqrt).then_inc(s["sub_std"], 1)
            for h in range(4, 8):
                split_head(h)
            split_weights(4)
            norm(XN2, s["x_ready"], 5)
            norm_columns("norm2", h2T, A2, B2)
            act.wait_ge(s["router_exp_in"], 1)
            nc.scalar.activation(RS(144, 16), RS(144, 16), ACT.Exp).then_inc(s["router_exp_out"], 1)
            act.wait_ge(s["router_exp_in"], 2)
            nc.scalar.activation(RS(1284, 4), RS(1280, 4), ACT.Exp).then_inc(s["router_exp_out"], 1)

            rows = ys_dram.rearrange("(b p) d -> p b d", p=P)

            def moe_keep_x(e, b):
                for half in range(2):
                    act.wait_ge(s["xt_full"], 2 * e + 1 + half)
                    if half == 0:
                        at_least(act, s["up_full"], e - 1)
                    nc.scalar.activation(XT[b][:, 4 * half:4 * half + 4, :],
                                         banks[6 + half][:, :].rearrange("p (k n) -> p k n", k=4), ACT.Copy
                                         ).then_inc(s["xt_ready"], 1)

            def moe_silu(e, b):
                act.wait_ge(s["gate_full"], e + 1)
                at_least(act, s["a_ready"], e - 1)
                nc.scalar.activation(SG[:, b, :], banks[b][:, :], ACT.Silu).then_inc(s["silu_ready"], 1)

            def moe_store(e, b):
                act.wait_ge(s["y_ready"], 2 * e + 2)
                act.dma_start(rows[:, bass.ds(e, 1), :], Y[:, b:b + 1, :]).then_inc(s[f"y_stored{b}"], 16)

            def moe_step(it, r):
                e, b = 2 * it + r, r % 2
                moe_silu(e, b)
                moe_keep_x(e + 1, 1 - b)
                moe_store(e - 1, 1 - b)

            moe_keep_x(0, 0)
            moe_silu(0, 0)
            moe_keep_x(1, 1)
            moe_step(0, 1)
            moe_step(0, 2)
            with act.Fori(1, N_EXP // 2 - 1) as it:
                moe_step(it, 1)
                moe_step(it, 2)
            e = N_EXP - 1
            moe_silu(e, 1)
            moe_store(e - 1, 0)
            moe_store(e, 1)
            act.wait_ge(s["ctl_ready"], 1)
            n_over = act.value_load(ctl[0:1, 7:8], min_val=0, max_val=N_OVER)
            with act.If(n_over > 0):
                with act.Fori(0, N_OVER) as j:
                    for half in range(2):
                        act.wait_ge(s["ov_xt_full"], 2 * j + 1 + half)
                        nc.scalar.activation(XT[0][:, 4 * half:4 * half + 4, :],
                                             banks[6 + half][:, :].rearrange("p (k n) -> p k n", k=4), ACT.Copy
                                             ).then_inc(s["ov_xt_ready"], 1)
                    act.wait_ge(s["ov_up_full"], 2 * j + 2)
                    nc.scalar.activation(SG[:, 0, :], banks[0][:, :], ACT.Silu).then_inc(s["ov_silu_ready"], 1)
                    act.wait_ge(s["ov_y_ready"], 2 * j + 2)
                    act.dma_start(rows[:, bass.ds(N_EXP + j, 1), :], Y[:, 0:1, :]).then_inc(s["y_stored0"], 16)
            norm(XN3, s["x_moe"], 1)
            norm(XN4, s["x_final"], 1)
            act.wait_ge(s["onehot_loaded"], 32)
            nc.scalar.activation(RB[0:32, :], RB[0:32, :], ACT.Copy, scale=8.0).then_inc(s["act_step"], 1)
            steps[0] += 1
            act.wait_ge(s["act_step"], steps[0])
            act.wait_ge(s["pads_set"], 1)
            nc.scalar.activation(small[:, 153:154], small[:, 152:153], ACT.Copy).then_inc(s["bias_rows_ready"], 1)
            for n in range(3):
                width = C if n < 2 else NG - 2 * C
                bank = full(FIRST["toep"] + n)
                ins = nc.scalar.activation(BROW[0:NH, n * C:n * C + width], bank[0:NH, 0:width], ACT.Copy)
                empty(ins)
            split_weights(FIRST_HALF["glu_g0"] + 1)
            split_columns("mix", cols[:, V_MIX:V_MIX + KT])
            split_weights(FIRST_HALF["glu_g0"] + 2)
            act.wait_ge(s["extras_loaded"], 32)
            nc.scalar.activation(WGS[0], WG, ACT.Copy).then_inc(s["gates_high"], 1)
            act.wait_ge(s["pads_set"], 2)
            for c in range(KT):
                n = c // 4
                if c % 4 == 0:
                    split_weights(FIRST_HALF[f"glu_g{n}"] + 3)
                empty(nc.scalar.activation(V[:, c, PAD:VW_], full(FIRST[f"glu_g{n}"] + c % 4)[:, :], ACT.Sigmoid))
                if c % 4 == 3:
                    split_weights(FIRST_HALF[f"glu_g{n}"] + 6 - 2 * n)
            split_weights(FIRST_HALF["q2"] + 2)
            for c in range(KT):
                if c % 4 == 0:
                    split_weights(FIRST_HALF["q2"] + c // 2 + 3)
                falling = bass.AP(area, 12528 + c * S + P - 1, [[22016, P], [P, TT], [-1, P]])
                empty(nc.scalar.activation(falling, full(FIRST["q2"] + c)[:, :].rearrange("p (t q) -> p t q", q=P),
                                           ACT.Copy))
                if c % 4 == 3:
                    split_weights(FIRST_HALF["q2"] + c // 4 * 2 + 4)
            split_weights(FIRST_HALF["kk"] + 1)
            for n in range(4):
                out = (KC, VC)[n // 2][:, n % 2, :]
                empty(nc.scalar.activation(out, full(FIRST["kvc"] + n)[:, :], ACT.Copy))
            split_weights(FIRST_HALF["vv"] + 1)
            for n in range(4):
                bank = full(FIRST["kk"] + n)
                for half in range(2):
                    for a in range(2):
                        last = nc.scalar.activation(KK[n // 2][64 * a:64 * a + 64, 2 * (n % 2) + half, :],
                                                    bank[64 * half:64 * half + 64, :], ACT.Copy)
                empty(last)
            split_weights(FIRST_HALF["ga0"] + 1)
            for t in range(TT):
                empty(nc.scalar.activation(VV[:, t, :], full(FIRST["vv"] + t)[:, :], ACT.Copy))
            split_weights(FIRST_HALF["ga0"] + 2)
            for t in range(TT):
                empty(nc.scalar.activation(GRISE[:, t, :], full(FIRST["gh"] + t)[:, 0:48], ACT.Sigmoid))
            for a in range(2):
                empty(nc.scalar.activation(POSB[0:64, a:a + 1], full(FIRST["pos"] + a)[0:64, 0:1], ACT.Copy))
            for c in range(4):
                empty(nc.scalar.activation(GA[:, c, :], full(FIRST["ga0"] + c)[:, :], ACT.Sigmoid))
            empty(nc.scalar.activation(GS[:].rearrange("p t n -> p (t n)"), full(FIRST["gates_falling"])[:, 0:TT * 48],
                                       ACT.Copy))
            split_weights(FIRST_HALF["ga1"] + 2)
            act.wait_ge(s["act_emptied"], emptied("act", FIRST["pos"] + 1))
            for n in range(4):
                a, half = n // 2, n % 2
                empty(nc.scalar.activation(ZC[0:64, a, 62 * half:62 * half + 62], full(FIRST["cmp1"] + n)[0:64, 0:62],
                                           ACT.Silu, bias=POSB[0:64, a:a + 1]))
            split_weights(FIRST_HALF["gc0"] + 1)
            for c in range(4):
                empty(nc.scalar.activation(GA[:, 4 + c, :], full(FIRST["ga1"] + c)[:, :], ACT.Sigmoid))
            split_weights(FIRST_HALF["gc0"] + 2)
            split_weights(FIRST_HALF["gc1"] + 1)
            for c in range(KT):
                act.wait_ge(s["centred"], c + 1)
                if c >= 2:
                    act.wait_ge(s["sq_used"], c - 1)
                nc.scalar.activation(SQ[c % 2], CV[:, c, :], ACT.Square).then_inc(s["squared"], 1)
                if c == 1:
                    for n in range(4):
                        empty(nc.scalar.activation(GC[:, n, :], full(FIRST["gc0"] + n)[:, :], ACT.Sigmoid))
                    split_weights(FIRST_HALF["gc1"] + 2)
            act.wait_ge(s["ln_var_ready"], 1)
            nc.scalar.activation(RSQ, RSQ, ACT.Sqrt).then_inc(s["ln_std_ready"], 1)
            for c in range(KT):
                act.wait_ge(s["ln_scaled"], c + 1)
                nc.scalar.activation(CV[:, c, :], CV[:, c, :], ACT.Silu, bias=col(V_LNB, c), scale=col(V_LNG, c)
                                     ).then_inc(s["conv_act_ready"], 1)
            split_weights(FIRST_HALF["pw"] + 1)
            for n in range(4):
                empty(nc.scalar.activation(GC[:, 4 + n, :], full(FIRST["gc1"] + n)[:, :], ACT.Sigmoid))
            for c in range(KT):
                act.wait_ge(s["conv_act_ready"], c + 1)
                nc.scalar.activation(CVS[0][:, c, :], CV[:, c, :], ACT.Copy).then_inc(s["tile_high"], 1)
            act.wait_ge(s["pads_set"], 4)
            bank = full(FIRST["cmp2"])
            for a in range(2):
                last = nc.scalar.activation(KCB[64 * a:64 * a + 64, :, a, 0:31],
                                            bank[0:64, 0:124].rearrange("p (u n) -> p u n", u=4), ACT.Copy)
            empty(last)
            bank = full(FIRST["cmp2"] + 1)
            for r in range(4):
                last = nc.scalar.activation(VC4[32 * r:32 * r + 31, :, :],
                                            bank[0:31, 0:256].rearrange("p (u n) -> p u n", u=4), ACT.Copy)
            empty(last)
            split_weights(FIRST_HALF["pw"] + 2)
            for i in range(TT):
                act.wait_ge(s["cmp_shifted"], i + 1)
                nc.scalar.activation(PN[:, i, :], PN[:, i, :], ACT.Exp).then_inc(s["cmp_exp"], 1)
            split_weights(FIRST_HALF["wo2"] + 2)
            for i in range(TT):
                act.wait_ge(s["cmp_t_full"], i + 1)
                nc.scalar.activation(PCT[:, :, i * P:(i + 1) * P],
                                     banks[6 + i % 2][:, :].rearrange("p (g q) -> p g q", g=4), ACT.Copy
                                     ).then_inc(s["cmp_t_ready"], 1)

            def nsa_keep_t(w):
                hb, i = w // 4, w % 4
                act.wait_ge(s["nsa_t_full"], w + 1)
                if hb >= 2:
                    act.wait_ge(s["nsa_out"], hb - 1)
                n = (i + 1) * P
                nc.scalar.activation(PTN[hb % 2][:, 0:i + 1, i * P:(i + 1) * P],
                                     banks[6][:, 0:n].rearrange("p (j q) -> p j q", q=P), ACT.Copy
                                     ).then_inc(s["nsa_t_ready0"], 1)

            def split_mixed(c):
                act.wait_ge(s["nsa_kept"], c + 1)
                nc.scalar.activation(GCS[0][:, c, :], GC[:, c, :], ACT.Copy).then_inc(s["tile_high"], 1)

            for w in range(8 * NH):
                i = w % 4
                n = (i + 1) * P
                if w >= 16 and w % 16 == 8:
                    split_mixed(w // 16 - 1)
                act.wait_ge(s["nsa_scored"], w + 1)
                nc.scalar.activation(PN[:, i, 0:n], PN[:, i, 0:n], ACT.Exp, bias=nmx[:, w % 8:w % 8 + 1], scale=-1.0,
                                     accum_out=sums[:, w % 8:w % 8 + 1]).then_inc(s["nsa_exp"], 1)
                if w >= 2 and w % 2 == 0:
                    nsa_keep_t(w - 2)
            nsa_keep_t(8 * NH - 2)
            split_mixed(NH // 2 - 1)

            split_weights(FIRST_HALF["xk"] + 1)
            for c in range(KT):
                nc.scalar.activation(MTS[0][:, c, :], transposed(XP["mem"] + c)[:, 0:MEM], ACT.Copy
                                     ).then_inc(s["x_high"], 1)
            split_weights(FIRST_HALF["xk"] + 2)
            for c in range(KT):
                if c % 4 == 0:
                    split_weights(FIRST_HALF["xk"] + c // 2 + 3)
                empty(nc.scalar.activation(XK[:, c, :], full(FIRST["xk"] + c)[:, 0:MEM], ACT.Copy))
                if c % 4 == 3:
                    split_weights(FIRST_HALF["xk"] + c // 4 * 2 + 4)
            norm(XN4, s["dve_emptied"], emptied("dve", FIRST["wo2"] + 4))
            for n in range(4):
                split_weights(FIRST_HALF["xv"] + n // 2 * 2 + 3)
                empty(nc.scalar.activation(XV[:, n % 2, n // 2 * C:n // 2 * C + C], full(FIRST["xv"] + n)[:, :], ACT.Copy))
                if n == 1:
                    split_weights(FIRST_HALF["xv"] + 4)
            split_weights(FIRST_HALF["xq"] + 2)
            split_columns("normx", cols[:, V_XN:V_XN + KT])
            for c in range(KT):
                if c % 4 == 0:
                    split_weights(FIRST_HALF["xq"] + c // 2 + 3)
                empty(nc.scalar.activation(XQ[:, c, :], full(FIRST["xq"] + c)[:, :], ACT.Copy, scale=1.0 / 16))
                if c % 4 == 3:
                    split_weights(FIRST_HALF["xq"] + c // 4 * 2 + 4)

            def x_keep_t(w):
                h, i = w // 4, w % 4
                act.wait_ge(s["x_t_full"], w + 1)
                if h >= 2:
                    act.wait_ge(s["x_out"], 2 * (h - 1))
                nc.scalar.activation(PTX[h % 2][:, :, i * P:(i + 1) * P],
                                     banks[6 + w % 2][:, 0:MEM].rearrange("p (j q) -> p j q", q=P), ACT.Copy
                                     ).then_inc(s["x_t_ready"], 1)

            def x_keep_outputs(h):
                for half in range(2):
                    act.wait_ge(s["x_out"], 2 * h + half + 1)
                    nc.scalar.activation(OTS[0][:, 2 * h + half, :], banks[half][:, :], ACT.Copy).then_inc(s["x_kept"], 1)

            for w in range(16):
                act.wait_ge(s["x_scored"], w + 1)
                if w >= 4:
                    act.wait_ge(s["x_t_full"], w - 3)
                nc.scalar.activation(PX[:, w % 4, :], banks[2 + w % 4][:, 0:MEM], ACT.Exp, bias=nmx[:, w % 8:w % 8 + 1],
                                     accum_out=sums[:, w % 8:w % 8 + 1]).then_inc(s["x_exp"], 1)
                if w >= 1:
                    x_keep_t(w - 1)
                if w >= 5 and w % 4 == 2:
                    x_keep_outputs(w // 4 - 1)
            x_keep_t(15)
            x_keep_outputs(3)
            split_weights(FIRST_HALF["ffin"] + 1)
            norm(XN4, s["dve_emptied"], emptied("dve", FIRST["xo"] + 4))
            split_columns("ffn", cols[:, V_FFN:V_FFN + KT])
            split_weights(FIRST_HALF["ffin"] + 2)

            def split_products(j):
                for f in (2 * j, 2 * j + 1):
                    act.wait_ge(s["dve_emptied"], emptied("dve", FIRST["ffin"] + 4 * j + 2 + f % 2))
                    nc.scalar.activation(GTH[f], GT[:, f, :], ACT.Copy).then_inc(s["tile_high"], 1)

            for j in range(FT // 2):
                if j >= 2:
                    act.wait_ge(s["dve_emptied"], emptied("dve", FIRST["ffin"] + 4 * (j - 2) + 3))
                for n in range(2):
                    empty(nc.scalar.activation(SA[:, (2 * j + n) % 4, :], full(FIRST["ffin"] + 4 * j + n)[:, :], ACT.Silu))
                split_weights(FIRST_HALF["ffin"] + 2 * j + 3)
                if j:
                    split_products(j - 1)
                split_weights(FIRST_HALF["ffin"] + 2 * j + 4)
            split_products(FT // 2 - 1)
            split_weights(len(HALVES))
            norm(A(0, 4096, TT), s["x_ff"], 1)

        @block.vector
        def _(dve):
            steps = [0]

            def then(ins):
                steps[0] += 1
                ins.then_inc(s["dve_step"], 1)
                dve.wait_ge(s["dve_step"], steps[0])

            def full(g):
                dve.wait_ge(s["proj_done"], g + 1)
                return banks[g % 4]

            norms = [0]

            def norm(XN):
                k = norms[0]
                norms[0] += 1
                dve.wait_ge(s["ssq_ready"], TT * (k + 1))
                nc.vector.tensor_scalar(var4, ssq[:, 0:TT], 1.0 / D, EPS, ALU.mult, ALU.add
                                        ).then_inc(s["var_ready"], 1)
                dve.wait_ge(s["std_ready"], k + 1)
                then(nc.vector.reciprocal(rstd[:, 0:TT], std4))
                for t in range(TT):
                    nc.vector.tensor_scalar(XN[:, t, :], X[:, t, :], rstd[:, t:t + 1], None, ALU.mult
                                            ).then_inc(s["xn_ready"], 1)

            def norm_columns(stage, hT, scale, bias=None):
                for c in range(1, KT, 2):
                    n = XP[stage] + c
                    dve.wait_ge(s["xpose_full"], n + 1)
                    if bias is None:
                        ins = nc.vector.tensor_scalar(hT[:, c, :], banks[6 + n % 2][:, :], scale[:, c:c + 1], None,
                                                      ALU.mult)
                    else:
                        ins = nc.vector.tensor_scalar(hT[:, c, :], banks[6 + n % 2][:, :], scale[:, c:c + 1],
                                                      bias[:, c:c + 1], ALU.mult, ALU.add)
                    ins.then_inc(xpose_emptied[n % 2], 1)

            def split_columns(stage, scale):
                for c in range(KT):
                    n = XP[stage] + c
                    highs[0] += 1
                    dve.wait_ge(s["x_high"], highs[0])
                    nc.vector.scalar_tensor_tensor(hTS[1][:, c, :], banks[6 + n % 2][:, :], scale[:, c:c + 1],
                                                   hTS[0][:, c, :], ALU.mult, ALU.subtract
                                                   ).then_inc(xpose_emptied[n % 2], 1)

            highs = [0]

            def ada(part):
                for n, j in enumerate(ADA_PARTS[part]):
                    c = CHUNK_NO[f"ada{part}"] + n
                    dve.wait_ge(w_loaded[c % N_DENSE_SLOTS], loaded_value(c))
                    if j >= 2:
                        dve.wait_ge(s["proj_done"], ADA_GROUP[j - 2] + 1)
                    w = slot(c % N_DENSE_SLOTS).rearrange("p (k n) -> p k n", k=KT)
                    b = 2 * (j % 2)
                    for k in range(KT):
                        acc = ada_acc[:, b + k % 2, :]
                        if k >= 2:
                            dve.wait_ge(s["dve_step"], steps[0] - 1)
                            ins = nc.vector.scalar_tensor_tensor(acc, w[:, k, :], csil[:, k:k + 1], acc, ALU.mult,
                                                                 ALU.add)
                        else:
                            ins = nc.vector.tensor_scalar(acc, w[:, k, :], csil[:, k:k + 1], None, ALU.mult)
                        if k < KT - 1:
                            steps[0] += 1
                            ins.then_inc(s["dve_step"], 1)
                    ins.then_inc(s["ada_acc"], 1)

            ropes = [0]

            def rope(g, t, heads, out):
                n = heads * 64
                bank = full(g)
                x3 = bank[:, 0:n].rearrange("p (h b) -> p h b", b=32)
                o3 = out.rearrange("p (h b) -> p h b", b=32)
                cos = bass.AP(late, K2_COS + t * 32, [[1024, P], [0, 2 * heads], [1, 32]])
                nc.vector.tensor_tensor(o3, x3, cos, ALU.mult)
                swapped = bass.AP(bank, 32, [[C, P], [64, heads], [-32, 2], [1, 32]])
                sin = bass.AP(late, K2_SIN + t * 64, [[1024, P], [0, heads], [32, 2], [1, 32]])
                r4 = RT[:, 0:n].rearrange("p (h a b) -> p h a b", a=2, b=32)
                if ropes[0]:
                    dve.wait_ge(s["rope_ready"], ropes[0])
                ropes[0] += 1
                nc.vector.tensor_tensor(r4, swapped, sin, ALU.mult).then_inc(s["dve_emptied"], 1)
                dve.wait_ge(s["dve_emptied"], emptied("dve", g))
                nc.vector.tensor_tensor(out, out, RT[:, 0:n], ALU.add).then_inc(s["rope_ready"], 1)

            nc.vector.memset(ones_d[:], 1.0 / D)
            nc.vector.memset(ones[:], 1.0).then_inc(s["ones_set"], 1)
            dve.wait_ge(s["csil_ready"], 1)
            dve.wait_ge(s["x_loaded"], 16)
            norm(XN1)
            ada(0)
            dve.wait_ge(s["lamload"], 16)
            for i in range(2):
                nc.vector.tensor_tensor_reduce(out=lamin[:, 128 * i:128 * i + 64], in0=lamin[:, 128 * i:128 * i + 64],
                                               in1=lamin[:, 128 * i + 64:128 * i + 128], scale=1.0, scalar=0.0,
                                               op0=ALU.mult, op1=ALU.add, accum_out=lamv[:, i:i + 1]
                                               ).then_inc(s["lam_ready"], 1)
            bank = full(FIRST["modcols"])
            nc.vector.tensor_copy(B1, bank[:, 0:8])
            nc.vector.scalar_tensor_tensor(A1, bank[:, 8:16], 1.0, cols[:, V_N1:V_N1 + KT], ALU.add, ALU.mult
                                           ).then_inc(s["dve_emptied"], 1)
            dve.wait_ge(s["dve_emptied"], emptied("dve", FIRST["modcols"]))
            nc.vector.memset(small[:, 152:153], 0.0).then_inc(s["mod_ready"], 1)
            norm_columns("norm1", hT, A1, B1)
            ada(1)
            dve.wait_ge(s["act_emptied"], emptied("act", FIRST["c"] + 3))
            nc.vector.tensor_scalar(varc, ssq[:, 4:12], 1.0 / 256, EPS, ALU.mult, ALU.add).then_inc(s["latent_var"], 1)
            dve.wait_ge(s["latent_std"], 1)
            then(nc.vector.reciprocal(rstd[:, 4:12], stdc))
            for t in range(TT):
                for half in range(2):
                    piece = slice(256 * half, 256 * half + 256)
                    ins = nc.vector.tensor_scalar(Z[:, t, piece], Z[:, t, piece],
                                                  rstd[:, 4 + 2 * t + half:5 + 2 * t + half], None, ALU.mult)
                ins.then_inc(s["latents_ready"], 1)
            for t in range(TT):
                rope(FIRST["kpe"] + t, t, 1, RQ[:, t, 0:64])
            ada(2)
            dve.wait_ge(s["xpose_full"], XP["latents"] + 4)
            for t in range(TT):
                rope(FIRST["dq"] + t, t, 8, Z[:, t, :])
            ada(3)
            dve.wait_ge(s["xpose_full"], XP["kpe"] + 1)
            for t in range(TT):
                rope(FIRST["dk"] + t, t, 8, RQ[:, t, :])
            ada(4)
            bank = full(FIRST["modcols2"])
            nc.vector.tensor_copy(B2, bank[:, 0:8])
            nc.vector.scalar_tensor_tensor(A2, bank[:, 8:16], 1.0, cols[:, V_N2:V_N2 + KT], ALU.add, ALU.mult
                                           ).then_inc(s["dve_emptied"], 1)
            for t in range(TT):
                rope(FIRST["up"] + 12 + t, t, 4, QRT[:, t, :])
            dve.wait_ge(s["lam_exp"], 1)
            then(nc.vector.tensor_tensor(lamv[:, 4:5], lamv[:, 3:4], lamv[:, 2:3], ALU.subtract))
            then(nc.vector.tensor_scalar(lamv[:, 5:6], lamv[:, 4:5], -LAMBDA_INIT, None, ALU.add))

            def inverse_sums(t):
                for n in range(first_score(t), first_score(t + 1)):
                    dve.wait_ge(s["exp_done"], n + 1)
                    i = n % 8
                    if t < 16:
                        nc.vector.reciprocal(rcp[:, i:i + 1], sums[:, i:i + 1]).then_inc(s["rcp_ready"], 1)
                    elif n % 2 == 0:
                        nc.vector.reciprocal(rcp[:, i:i + 1], sums[:, i:i + 1])
                    else:
                        then(nc.vector.reciprocal(rcp[:, i:i + 1], sums[:, i:i + 1]))
                        nc.vector.tensor_tensor(rcp[:, 8 + i:9 + i], rcp[:, i:i + 1], lamv[:, 5:6], ALU.mult
                                                ).then_inc(s["rcp_ready"], 1)

            def combine(t):
                n = first_score(t)
                dve.wait_ge(s["scaled"], t - 15)
                nc.vector.scalar_tensor_tensor(prob_tile(n), prob_tile(n), rcp[:, n % 8:n % 8 + 1], prob_tile(n + 1),
                                               ALU.mult, ALU.add).then_inc(s["probs_diff"], 1)

            for t in range(34):
                if t >= 18:
                    combine(t - 2)
                if t < 32:
                    for n in range(first_score(t), first_score(t + 1)):
                        dve.wait_ge(s["scores_full"], n + 1)
                        nc.vector.reduce_max(nmx[:, n % 8:n % 8 + 1], banks[2 + n % 4][:, :], AX, negate=True
                                             ).then_inc(s["max_ready"], 1)
                if 1 <= t < 33:
                    inverse_sums(t - 1)
            for h in range(4):
                dve.wait_ge(s["sub_full"], h + 1)
                nc.vector.tensor_scalar(SUBS[:, h, :], banks[4 + h][:, :], 1.0 / (P * (1 - LAMBDA_INIT) ** 2),
                                        EPS / (1 - LAMBDA_INIT) ** 2, ALU.mult, ALU.add).then_inc(s["sub_var"], 1)
            for h in range(4):
                dve.wait_ge(s["sub_std"], h + 1)
                then(nc.vector.reciprocal(SUBS[:, h, :], SUBS[:, h, :]))
                dve.wait_ge(s["pv_emptied"], 5 + h)
                nc.vector.scalar_tensor_tensor(mixT[:, 4 + h, :], mixT[:, 4 + h, :], col(V_SUB, 0), SUBS[:, h, :],
                                               ALU.mult, ALU.mult).then_inc(s["sub_ready"], 1)

            def residual(stage, gate):
                for n in range(8):
                    g = FIRST[stage] + n
                    half, t = n // 4, n % 4
                    piece = slice(half * C, half * C + C)
                    bank = full(g)
                    if gate is None:
                        nc.vector.tensor_tensor(X[:, t, piece], bank[:, :], X[:, t, piece], ALU.add
                                                ).then_inc(s["dve_emptied"], 1)
                    else:
                        nc.vector.tensor_tensor(WOT[:, n % 2, :], bank[:, :], gate[:, piece], ALU.mult
                                                ).then_inc(s["dve_emptied"], 1)
                        dve.wait_ge(s["dve_emptied"], emptied("dve", g))
                        nc.vector.tensor_tensor(X[:, t, piece], X[:, t, piece], WOT[:, n % 2, :], ALU.add
                                                ).then_inc(s["x_ready"], 1)

            residual("wo", gate1)
            norm(XN2)
            norm_columns("norm2", h2T, A2, B2)

            LG = 0
            dve.wait_ge(s["router_loaded"], 80)
            for t in range(TT):
                bank = full(FIRST["router"] + t)
                nc.vector.tensor_tensor(RS(LG + 36 * t, 36), bank[:, 0:36], BR, ALU.add).then_inc(s["dve_emptied"], 1)
            dve.wait_ge(s["dve_emptied"], emptied("dve", FIRST["router"] + 3))
            G3 = R3(LG, [36, 4], [1, 4])
            iota4 = bass.AP(late, K2_IOTA, [[1024, P], [0, 4], [1, 4]])
            iota8 = bass.AP(late, K2_IOTA, [[1024, P], [0, 4], [1, 8]])
            iota32 = bass.AP(late, K2_IOTA, [[1024, P], [0, 4], [1, 32]])

            def per_token(off, n):
                return R3(off, [1, 4], [0, n])

            def lowest_index(eq, iota, n, out):
                then(nc.vector.tensor_scalar(eq, eq, -1000.0, 1000.0, ALU.mult, ALU.add))
                then(nc.vector.tensor_tensor(eq, eq, iota, ALU.add))
                then(nc.vector.tensor_reduce(RS(out, 4), eq, AX, ALU.min))

            (GM, GSUM, GP, GI, M1, I1, M2, I2) = range(1248, 1280, 4)
            DM, XE, DEN, RD = 1280, 1284, 1288, 1292
            EID, RANK, OSA, OV, BLK, HI8, LO8, D8, T8 = range(1296, 1368, 8)
            then(nc.vector.tensor_reduce(RS(GM, 4), G3, AX, ALU.max))
            then(nc.vector.tensor_tensor(R3(144, [4, 4], [1, 4]), G3, per_token(GM, 4), ALU.subtract))
            then(nc.vector.tensor_scalar(RS(160, 16), RS(144, 16), 0.0, None, ALU.is_equal))
            nc.vector.memset(RS(1372, 1), 0.0).then_inc(s["router_exp_in"], 1)
            lowest_index(R3(160, [4, 4], [1, 4]), iota4, 4, GI)
            then(nc.vector.tensor_tensor(R3(176, [4, 4], [1, 4]), iota4, per_token(GI, 4), ALU.is_equal))
            then(nc.vector.tensor_tensor(R3(192, [32, 4], [8, 4], [1, 8]), R3(LG + 4, [36, 4], [8, 4], [1, 8]),
                                         R3(176, [4, 4], [1, 4], [0, 8]), ALU.mult))
            then(nc.vector.tensor_reduce(R3(320, [8, 4], [1, 8]), R3(192, [32, 4], [1, 8], [8, 4]), AX, ALU.add))
            ES = R3(320, [8, 4], [1, 8])
            ED = R3(352, [8, 4], [1, 8])
            OH = R3(384, [8, 4], [1, 8])
            then(nc.vector.tensor_reduce(RS(M1, 4), ES, AX, ALU.max))
            then(nc.vector.tensor_tensor(ED, ES, per_token(M1, 8), ALU.is_equal))
            lowest_index(ED, iota8, 8, I1)
            then(nc.vector.tensor_tensor(OH, iota8, per_token(I1, 8), ALU.is_equal))
            then(nc.vector.scalar_tensor_tensor(ES, OH, 3 * NEG, ES, ALU.mult, ALU.add))
            then(nc.vector.tensor_reduce(RS(M2, 4), ES, AX, ALU.max))
            then(nc.vector.tensor_tensor(ED, ES, per_token(M2, 8), ALU.is_equal))
            lowest_index(ED, iota8, 8, I2)
            nc.vector.tensor_tensor(RS(DM, 4), RS(M2, 4), RS(M1, 4), ALU.subtract).then_inc(s["router_exp_in"], 1)
            dve.wait_ge(s["router_exp_out"], 1)
            then(nc.vector.tensor_reduce(RS(GSUM, 4), R3(144, [4, 4], [1, 4]), AX, ALU.add))
            then(nc.vector.reciprocal(RS(GP, 4), RS(GSUM, 4)))
            dve.wait_ge(s["router_exp_out"], 2)
            then(nc.vector.tensor_scalar(RS(DEN, 4), RS(XE, 4), 1.0, None, ALU.add))
            then(nc.vector.reciprocal(RS(RD, 4), RS(DEN, 4)))
            then(nc.vector.tensor_tensor(wts[:, 0, :], RS(GP, 4), RS(RD, 4), ALU.mult))
            nc.vector.tensor_tensor(wts[:, 1, :], wts[:, 0, :], RS(XE, 4), ALU.mult)
            nc.vector.scalar_tensor_tensor(RS(EID, 4), RS(GI, 4), 8.0, RS(I1, 4), ALU.mult, ALU.add)
            then(nc.vector.scalar_tensor_tensor(RS(EID + 4, 4), RS(GI, 4), 8.0, RS(I2, 4), ALU.mult, ALU.add))
            for a in range(2):
                then(nc.vector.tensor_tensor(R3(416 + 128 * a, [32, 4], [1, 32]), iota32, per_token(EID + 4 * a, 32),
                                             ALU.is_equal))
            nc.vector.tensor_tensor(RS(672, 128), RS(416, 128), RS(544, 128), ALU.add).then_inc(s["onehot_ready"], 1)
            bank = full(FIRST["rank"])
            nc.vector.tensor_copy(RS(928, 128), bank[:, 0:128])
            counts, over = bank[0:32, 128:256], RS(1056, P)[0:32, :]
            then(nc.vector.tensor_scalar(over, counts, float(CAP), None, ALU.is_gt))
            then(nc.vector.scalar_tensor_tensor(over, counts, 2.0 * CAP, over, ALU.is_gt, ALU.add))
            nc.vector.scalar_tensor_tensor(over, counts, 3.0 * CAP, over, ALU.is_gt, ALU.add
                                           ).then_inc(s["dve_emptied"], 1)
            dve.wait_ge(s["dve_emptied"], emptied("dve", FIRST["rank"]))
            nc.vector.memset(RS(1372, 1), 0.0).then_inc(s["onehot_ready"], 1)

            def of_expert(table, out):
                for a in range(2):
                    then(nc.vector.tensor_tensor(R3(800, [32, 4], [1, 32]), R3(416 + 128 * a, [32, 4], [1, 32]), table,
                                                 ALU.mult))
                    then(nc.vector.tensor_reduce(RS(out + 4 * a, 4), R3(800, [32, 4], [1, 32]), AX, ALU.add))

            of_expert(R3(928, [32, 4], [1, 32]), RANK)
            bank = full(FIRST["over"])
            nc.vector.tensor_copy(RS(1184, 64), bank[:, 0:64]).then_inc(s["dve_emptied"], 1)
            dve.wait_ge(s["dve_emptied"], emptied("dve", FIRST["over"]))
            of_expert(R3(1184, [0, 4], [1, 32]), OSA)
            then(nc.vector.tensor_scalar(RS(OV, 8), RS(RANK, 8), float(CAP), None, ALU.is_ge))
            then(nc.vector.scalar_tensor_tensor(RS(BLK, 8), RS(RANK, 8), 2.0 * CAP, RS(OV, 8), ALU.is_ge, ALU.add))
            then(nc.vector.scalar_tensor_tensor(RS(BLK, 8), RS(RANK, 8), 3.0 * CAP, RS(BLK, 8), ALU.is_ge, ALU.add))
            then(nc.vector.scalar_tensor_tensor(RS(LO8, 8), RS(BLK, 8), -float(CAP), RS(RANK, 8), ALU.mult, ALU.add))
            then(nc.vector.scalar_tensor_tensor(RS(T8, 8), RS(OSA, 8), N_EXP - 1.0, RS(BLK, 8), ALU.add, ALU.add))
            then(nc.vector.tensor_tensor(RS(T8, 8), RS(T8, 8), RS(EID, 8), ALU.subtract))
            then(nc.vector.tensor_tensor(RS(T8, 8), RS(T8, 8), RS(OV, 8), ALU.mult))
            then(nc.vector.tensor_tensor(RS(HI8, 8), RS(T8, 8), RS(EID, 8), ALU.add))
            then(nc.vector.scalar_tensor_tensor(RS(D8, 8), RS(HI8, 8), float(CAP), RS(LO8, 8), ALU.mult, ALU.add))
            nc.vector.tensor_copy(dest[:, :], RS(D8, 8))
            for n in range(8):
                nc.vector.tensor_scalar(LO[:, n, :], IOTA, RS(LO8 + n, 1), None, ALU.is_equal)
                ins = nc.vector.tensor_scalar(HI[:, n, :], IOTA[:, 0:N_BLOCKS], RS(HI8 + n, 1), TOK[:, n % 4:n % 4 + 1],
                                              ALU.is_equal, ALU.mult)
            ins.then_inc(s["onehot_ready"], 1)
            bank = full(FIRST["slots"])
            nc.vector.tensor_copy(idx[:, :], bank[:, 0:N_BLOCKS]).then_inc(s["dve_emptied"], 1)
            dve.wait_ge(s["dve_emptied"], emptied("dve", FIRST["slots"]))
            nc.vector.memset(RS(1372, 1), 0.0).then_inc(s["idx_ready"], 1)
            J1, J2 = R3(1400, [32, N_OVER], [1, 32]), R3(1400 + 224, [32, N_OVER], [1, 32])
            j7 = bass.AP(late, K2_IOTA, [[1024, P], [1, N_OVER], [0, 32]])
            then(nc.vector.tensor_tensor(RS(1216, 32), RS(1184, 32), RS(1216, 32), ALU.add))
            then(nc.vector.tensor_tensor(J1, R3(1184, [0, N_OVER], [1, 32]), j7, ALU.is_le))
            then(nc.vector.tensor_tensor(J2, R3(1216, [0, N_OVER], [1, 32]), j7, ALU.is_gt))
            then(nc.vector.tensor_tensor(J1, J1, J2, ALU.mult))
            then(nc.vector.tensor_tensor(J1, J1, bass.AP(late, K2_IOTA, [[1024, P], [0, N_OVER], [1, 32]]), ALU.mult))
            then(nc.vector.tensor_reduce(RS(T8, N_OVER), J1, AX, ALU.add))
            nc.vector.tensor_copy(ctl[:, 0:N_OVER], RS(T8, N_OVER))
            nc.vector.tensor_copy(ctl[:, 7:8], RS(1216 + 31, 1)).then_inc(s["ctl_ready"], 1)

            def moe_keep_a(e, b):
                dve.wait_ge(s["at_full"], e + 1)
                at_least(dve, s["down_full"], 2 * e - 2)
                nc.vector.tensor_copy(AT[b], banks[7][:, :].rearrange("p (k n) -> p k n", k=4)
                                      ).then_inc(s["at_ready"], 1)

            def moe_multiply(e, b):
                dve.wait_ge(s["silu_ready"], e + 1)
                dve.wait_ge(s["up_full"], e + 1)
                at_least(dve, s["at_full"], e - 1)
                nc.vector.tensor_tensor(AA[:, b, :], banks[2 + b][:, :], SG[:, b, :], ALU.mult
                                        ).then_inc(s["a_ready"], 1)

            def moe_keep_y(e, it, b):
                at_least(dve, s[f"y_stored{b}"], 16 * it)
                for half in range(2):
                    dve.wait_ge(s["down_full"], 2 * e + 1 + half)
                    piece = slice(half * C, (half + 1) * C)
                    nc.vector.tensor_tensor(Y[:, b, piece], banks[4 + half][:, :], gate2[:, piece], ALU.mult
                                            ).then_inc(s["y_ready"], 1)

            def moe_step(it, r):
                e, b = 2 * it + r, r % 2
                moe_keep_a(e - 1, 1 - b)
                moe_multiply(e, b)
                moe_keep_y(e - 1, it + (r - 1) // 2, 1 - b)

            moe_multiply(0, 0)
            moe_step(0, 1)
            moe_step(0, 2)
            with dve.Fori(1, N_EXP // 2 - 1) as it:
                moe_step(it, 1)
                moe_step(it, 2)
            e = N_EXP - 1
            moe_step(e // 2, 1)
            moe_keep_a(e, 1)
            moe_keep_y(e, e // 2, 1)
            n_over = dve.value_load(ctl[0:1, 7:8], min_val=0, max_val=N_OVER)
            with dve.If(n_over > 0):
                dve.wait_ge(s["y_stored0"], 16 * N_EXP // 2)
                with dve.Fori(0, N_OVER) as j:
                    dve.wait_ge(s["ov_silu_ready"], j + 1)
                    nc.vector.tensor_tensor(AA[:, 0, :], banks[2][:, :], SG[:, 0, :], ALU.mult
                                            ).then_inc(s["ov_a_ready"], 1)
                    dve.wait_ge(s["ov_at_full"], j + 1)
                    nc.vector.tensor_copy(AT[0], banks[7][:, :].rearrange("p (k n) -> p k n", k=4)
                                          ).then_inc(s["ov_at_ready"], 1)
                    dve.wait_ge(s["y_stored0"], 16 * N_EXP // 2 + 16 * j)
                    for half in range(2):
                        dve.wait_ge(s["down_full"], 2 * N_EXP + 2 * j + 1 + half)
                        piece = slice(half * C, (half + 1) * C)
                        nc.vector.tensor_tensor(Y[:, 0, piece], banks[4 + half][:, :], gate2[:, piece], ALU.mult
                                                ).then_inc(s["ov_y_ready"], 1)
            for t in range(TT):
                dve.wait_ge(s[f"yg_loaded{t}"], 32)
                then(nc.vector.scalar_tensor_tensor(X[:, t, :], YG[2 * t], wts[:, 0, t:t + 1], X[:, t, :],
                                                    ALU.mult, ALU.add))
                nc.vector.scalar_tensor_tensor(X[:, t, :], YG[2 * t + 1], wts[:, 1, t:t + 1], X[:, t, :],
                                               ALU.mult, ALU.add).then_inc(s["x_moe"], 1)

            def final_norm(gain):
                k = norms[0]
                norms[0] += 1
                dve.wait_ge(s["ssq_ready"], TT * (k + 1))
                nc.vector.tensor_scalar(var4, ssq[:, 0:TT], 1.0 / D, EPS, ALU.mult, ALU.add
                                        ).then_inc(s["var_ready"], 1)
                dve.wait_ge(s["std_ready"], k + 1)
                then(nc.vector.reciprocal(rstd[:, 0:TT], std4))
                for t in range(TT):
                    nc.vector.scalar_tensor_tensor(X[:, t, :], X[:, t, :], rstd[:, t:t + 1], gain, ALU.mult, ALU.mult
                                                   ).then_inc(s["x_final"], 1)

            final_norm(FGB)
            norm(XN4)
            split_columns("mix", cols[:, V_MIX:V_MIX + KT])
            def gate_glu(c):
                dve.wait_ge(s["act_emptied"], emptied("act", FIRST[f"glu_g{c // 4}"] + c % 4))
                nc.vector.tensor_tensor(V[:, c, PAD:VW_], full(FIRST[f"glu_a{c // 4}"] + c % 4)[:, :], V[:, c, PAD:VW_],
                                        ALU.mult).then_inc(s["dve_emptied"], 1)

            for c in range(4):
                gate_glu(c)
            dve.wait_ge(s["pads_set"], 2)
            for c in range(0, KT, 2):
                if c == 0 or c == 4:
                    dve.wait_ge(s["dve_emptied"], emptied("dve", FIRST[f"glu_a{c // 4}"] + 3))
                for j in range(CONV_W):
                    if c == 0 and j in GLU_AT:
                        gate_glu(4 + GLU_AT.index(j))
                    for u in (c, c + 1):
                        tap = col(V_DW, u * CONV_W + j)
                        if j:
                            dve.wait_ge(s["dve_step"], steps[0] - 1)
                            ins = nc.vector.scalar_tensor_tensor(CV[:, u, :], V[:, u, j:j + S], tap, CV[:, u, :],
                                                                 ALU.mult, ALU.add)
                        else:
                            ins = nc.vector.tensor_scalar(CV[:, u, :], V[:, u, 0:S], tap, col(V_DWB, u), ALU.mult,
                                                          ALU.add)
                        if j < CONV_W - 1:
                            steps[0] += 1
                            ins.then_inc(s["dve_step"], 1)
                        else:
                            if u == c:
                                dve.wait_ge(s["dve_step"], steps[0])
                            ins.then_inc(s["conv_ready"], 1)
            bank = full(FIRST["ln_mean"])
            dve.wait_ge(s["conv_ready"], KT)
            for c in range(KT):
                ins = nc.vector.tensor_tensor(CV[:, c, :], CV[:, c, :], bank[:, :], ALU.subtract)
                ins.then_inc(s["centred"], 1)
            dve.wait_ge(s["centred"], KT)
            nc.vector.memset(small[:, 154:155], 0.0).then_inc(s["dve_emptied"], 1)
            nc.vector.tensor_scalar(RSQ, full(FIRST["ln_var"])[:, :], EPS, None, ALU.add).then_inc(s["dve_emptied"], 1)
            dve.wait_ge(s["dve_emptied"], emptied("dve", FIRST["ln_var"]))
            nc.vector.memset(small[:, 154:155], 0.0).then_inc(s["ln_var_ready"], 1)
            dve.wait_ge(s["ln_std_ready"], 1)
            then(nc.vector.reciprocal(RSQ, RSQ))
            for c in range(KT):
                nc.vector.tensor_tensor(CV[:, c, :], CV[:, c, :], RSQ, ALU.mult).then_inc(s["ln_scaled"], 1)
            p3 = [PN[:, i, :].rearrange("p (h n) -> p h n", n=NCMP) for i in range(TT)]
            cm = [small[:, 160 + 16 * i:176 + 16 * i] for i in range(TT)]

            def by_head(i):
                return bass.AP(small, 160 + 16 * i, [[320, P], [1, NH], [0, NCMP]])

            dve.wait_ge(s["proj_done"], FIRST["gc1"] + 4)
            for g in range(4):
                dve.wait_ge(s["cmp_scores_full"], g + 1)
                ins = nc.vector.tensor_scalar(PN[:, :, g * P:(g + 1) * P].rearrange("p i (a n) -> p a i n", a=4),
                                              banks[4 + g][:, :].rearrange("p (a i n) -> p a i n", a=4, i=TT), 0.125, None,
                                              ALU.mult)
            ins.then_inc(s["cmp_read"], 1)
            dve.wait_ge(s["cmp_read"], 1)
            for i in range(TT):
                then(nc.vector.tensor_reduce(cm[i], p3[i], AX, ALU.max))
                nc.vector.tensor_tensor(p3[i], p3[i], by_head(i), ALU.subtract).then_inc(s["cmp_shifted"], 1)
            for i in range(TT):
                dve.wait_ge(s["cmp_exp"], i + 1)
                then(nc.vector.tensor_tensor(p3[i], p3[i], bass.AP(k1, K1_MASK + NCMP * i, [[K1_N, P], [0, NH], [1, NCMP]]),
                                             ALU.mult))
                then(nc.vector.tensor_reduce(cm[i], p3[i], AX, ALU.add))
                then(nc.vector.tensor_scalar(cm[i], cm[i], 1e-30, None, ALU.max))
                then(nc.vector.reciprocal(cm[i], cm[i]))
                then(nc.vector.tensor_tensor(cm[i], cm[i], GS[:, i, 0:NH], ALU.mult))
                nc.vector.tensor_tensor(p3[i], p3[i], by_head(i), ALU.mult).then_inc(s["cmp_probs"], 1)
            for c in range(KT):
                g = FIRST["pw"] + c
                nc.vector.tensor_tensor(GC[:, c, :], full(g)[:, :], GC[:, c, :], ALU.mult).then_inc(s["dve_emptied"], 1)

            def nsa_keep_t(w):
                hb, i = w // 4, w % 4
                dve.wait_ge(s["nsa_t_full"], w + 1)
                if hb >= 2:
                    dve.wait_ge(s["nsa_out"], hb - 1)
                n = (i + 1) * P
                nc.vector.tensor_copy(PTN[hb % 2][:, 0:i + 1, i * P:(i + 1) * P],
                                      banks[7][:, 0:n].rearrange("p (j q) -> p j q", q=P)
                                      ).then_inc(s["nsa_t_ready1"], 1)

            def nsa_keep_outputs(c):
                dve.wait_ge(s["nsa_out"], 4 * c + 4)
                rising = bass.AP(banks[c % 2], P - 1, [[C, P], [P, TT], [-1, P]])
                then(nc.vector.tensor_tensor(TMP.rearrange("p (t q) -> p t q", q=P), rising,
                                             GA[:, c, :].rearrange("p (t q) -> p t q", q=P), ALU.mult))
                nc.vector.tensor_tensor(GC[:, c, :], GC[:, c, :], TMP, ALU.add).then_inc(s["nsa_kept"], 1)
                dve.wait_ge(s["nsa_kept"], c + 1)

            def nsa_inverse(w):
                dve.wait_ge(s["nsa_exp"], w + 1)
                nc.vector.reciprocal(rcp[:, w % 8:w % 8 + 1], sums[:, w % 8:w % 8 + 1]).then_inc(s["nsa_rcp"], 1)

            dve.wait_ge(s["dve_emptied"], emptied("dve", FIRST["pw"] + 7))
            dve.wait_ge(s["cmp_t_full"], TT)
            for w in range(8 * NH):
                h, i = w // 8, w % 4
                n = (i + 1) * P
                if w % 8 == 0:
                    dve.wait_ge(s[f"bias_loaded{h % 2}"], 16 * (h // 2 + 1))
                dve.wait_ge(s["nsa_full"], w + 1)
                if w >= 4:
                    dve.wait_ge(s["nsa_t_full"], w - 3)
                nc.vector.tensor_tensor_reduce(out=PN[:, i, 0:n], in0=banks[2 + w % 4][:, 0:n],
                                               in1=BT[h % 2][:, C - n:C], scale=-0.125, scalar=3e38, op0=ALU.add,
                                               op1=ALU.min, accum_out=nmx[:, w % 8:w % 8 + 1]
                                               ).then_inc(s["nsa_scored"], 1)
                if w >= 1:
                    nsa_inverse(w - 1)
                if w >= 2 and w % 2 == 1:
                    nsa_keep_t(w - 2)
                if w >= 16 and w % 16 == 4:
                    nsa_keep_outputs(w // 16 - 1)
            nsa_inverse(8 * NH - 1)
            nsa_keep_t(8 * NH - 1)
            nsa_keep_outputs(NH // 2 - 1)
            residual("wo2", None)
            for c in range(KT):
                n = XP["mem"] + c
                highs[0] += 1
                dve.wait_ge(s["x_high"], highs[0])
                nc.vector.tensor_tensor(MTS[1][:, c, :], banks[6 + n % 2][:, 0:MEM], MTS[0][:, c, :], ALU.subtract
                                        ).then_inc(xpose_emptied[n % 2], 1)
            norm(XN4)
            split_columns("normx", cols[:, V_XN:V_XN + KT])

            def x_inverse(w):
                dve.wait_ge(s["x_exp"], w + 1)
                nc.vector.reciprocal(rcp[:, w % 8:w % 8 + 1], sums[:, w % 8:w % 8 + 1]).then_inc(s["x_rcp"], 1)

            def x_low_outputs(h):
                for c in (2 * h, 2 * h + 1):
                    dve.wait_ge(s["x_kept"], c + 1)
                    nc.vector.tensor_tensor(OTS[1][:, c, :], banks[c % 2][:, :], OTS[0][:, c, :], ALU.subtract
                                            ).then_inc(s["x_kept_low"], 1)

            for w in range(16):
                dve.wait_ge(s["x_full"], w + 1)
                nc.vector.reduce_max(nmx[:, w % 8:w % 8 + 1], banks[2 + w % 4][:, 0:MEM], AX, negate=True
                                     ).then_inc(s["x_scored"], 1)
                if w:
                    x_inverse(w - 1)
                if w >= 7 and w % 4 == 3:
                    x_low_outputs(w // 4 - 1)
            x_inverse(15)
            x_low_outputs(3)
            residual("xo", None)
            norm(XN4)
            split_columns("ffn", cols[:, V_FFN:V_FFN + KT])
            for j in range(FT // 2):
                for n in range(2):
                    g = FIRST["ffin"] + 4 * j + 2 + n
                    dve.wait_ge(s["act_emptied"], emptied("act", g - 2))
                    nc.vector.tensor_tensor(GT[:, 2 * j + n, :], full(g)[:, :], SA[:, (2 * j + n) % 4, :], ALU.mult
                                            ).then_inc(s["dve_emptied"], 1)
            for t in range(TT):
                for half in range(2):
                    dve.wait_ge(s["ff_full"], 2 * t + half + 1)
                    piece = slice(half * C, half * C + C)
                    ins = nc.vector.tensor_tensor(X[:, t, piece], banks[2 * t + half][:, :], X[:, t, piece], ALU.add)
                ins.then_inc(s["x_ff"], 1)
            dve.wait_ge(s["fg2_loaded"], 16)
            final_norm(FG2)

        @block.gpsimd
        def _(pool):
            nc.gpsimd.memset(A(8192, D), 0.0).then_inc(s["zeros_set"], 1)
            lows = [0]

            def low_weights(upto_half):
                while lows[0] < upto_half:
                    m = lows[0]
                    pool.wait_ge(s["w_high"], m + 1)
                    nc.gpsimd.tensor_tensor(low_half(m), raw_half(m), high_half(m), ALU.subtract
                                            ).then_inc(s["w_low"], 1)
                    lows[0] += 1

            def low_tile(number, low, whole, high):
                pool.wait_ge(s["tile_high"], number)
                nc.gpsimd.tensor_tensor(low, whole, high, ALU.subtract).then_inc(s["tile_low"], 1)

            def low_head(h):
                low_tile(h + 1, WOS[1][:, h, :], mixT[:, h, :], WOS[0][:, h, :])

            low_weights(2)
            for t in range(32):
                if t >= 9 and t % TT == 1 and t // TT <= 5:
                    low_head(t // TT - 2)
                n = first_score(t + 1) - 1
                i = n % 8
                pool.wait_ge(s["rcp_ready"], t + 1)
                if t < 16:
                    nc.gpsimd.tensor_scalar(prob_tile(n), prob_tile(n), rcp[:, i:i + 1], 1.0, ALU.mult, ALU.mult
                                            ).then_inc(s["probs_mla"], 1)
                else:
                    nc.gpsimd.tensor_scalar(prob_tile(n), prob_tile(n), rcp[:, 8 + i:9 + i], 1.0, ALU.mult,
                                            ALU.mult).then_inc(s["scaled"], 1)
            for h in range(4, 8):
                low_head(h)
            low_weights(4)
            pool.wait_ge(s["router_loaded"], 80)
            pool.wait_ge(s["act_emptied"], emptied("act", FIRST["up"] - 1))
            nc.gpsimd.tensor_scalar(scale2, scale2, 1.0, 1.0, ALU.mult, ALU.add).then_inc(s["pool_step"], 1)
            pool.wait_ge(s["pool_step"], 1)
            nc.gpsimd.tensor_tensor(scale2, scale2, G2B, ALU.mult).then_inc(s["pool_step"], 1)
            pool.wait_ge(s["pool_step"], 2)
            for t in range(TT):
                pool.wait_ge(s["xn_ready"], TT + t + 1)
                nc.gpsimd.tensor_tensor(H2[:, t, :], XN2[:, t, :], scale2, ALU.mult).then_inc(s["pool_step"], 1)
                pool.wait_ge(s["pool_step"], 3 + t)
                nc.gpsimd.tensor_tensor(H2[:, t, :], H2[:, t, :], shift2, ALU.add).then_inc(s["h2_ready"], 1)
            pool.wait_ge(s["idx_ready"], 1)
            pool.wait_ge(s["h2_stored"], 64)
            for e in range(N_EXP):
                if e >= 2:
                    pool.wait_ge(s["xt_full"], 2 * (e - 1))
                nc.gpsimd.indirect_dma_start(out=XG[:, e % 2, :], out_offset=None, in_=h2_dram[:, :],
                                             in_offset=bass.IndirectOffsetOnAxis(ap=idx[:, e:e + 1], axis=0)
                                             ).then_inc(s[f"xg_loaded{e % 2}"], 16)
            pool.wait_ge(s["ctl_ready"], 1)
            n_over = pool.value_load(ctl[0:1, 7:8], min_val=0, max_val=N_OVER)
            with pool.If(n_over > 0):
                pool.wait_ge(s["xt_full"], 2 * N_EXP)
                for j in range(N_OVER):
                    if j:
                        pool.wait_ge(s["ov_xt_full"], 2 * j)
                    nc.gpsimd.indirect_dma_start(out=XG[:, 0, :], out_offset=None, in_=h2_dram[:, :],
                                                 in_offset=bass.IndirectOffsetOnAxis(
                                                     ap=idx[:, N_EXP + j:N_EXP + j + 1], axis=0)
                                                 ).then_inc(s["ov_gathered"], 16)
                pool.wait_ge(s["y_stored0"], 16 * N_EXP // 2 + 16 * N_OVER)
            pool.wait_ge(s["y_stored0"], 16 * N_EXP // 2)
            pool.wait_ge(s["y_stored1"], 16 * N_EXP // 2)
            for n in range(2 * TT):
                t, a = n // 2, n % 2
                nc.gpsimd.indirect_dma_start(out=YG[n], out_offset=None, in_=ys_dram[:, :],
                                             in_offset=bass.IndirectOffsetOnAxis(ap=dest[:, 4 * a + t:4 * a + t + 1],
                                                                                 axis=0)
                                             ).then_inc(s[f"yg_loaded{t}"], 16)
            pool.wait_ge(s["x_final"], 4)
            nc.gpsimd.memset(RB[32:33, :], 8 * NEG).then_inc(s["pads_set"], 1)
            pool.wait_ge(s["pads_set"], 1)
            nc.gpsimd.memset(V[:, :, 0:PAD], 0.0).then_inc(s["pads_set"], 1)
            nc.gpsimd.memset(A(21760, 8 * NCMP), 0.0).then_inc(s["pads_set"], 1)
            nc.gpsimd.memset(VC4[:, :, :], 0.0).then_inc(s["pads_set"], 1)
            low_weights(FIRST_HALF["glu_a0"])
            pool.wait_ge(s["gates_high"], 1)
            nc.gpsimd.tensor_tensor(WGS[1], WG, WGS[0], ALU.subtract).then_inc(s["gates_low"], 1)
            low_weights(FIRST_HALF["pw"] + 1)
            for c in range(KT):
                low_tile(KT + c + 1, CVS[1][:, c, :], CV[:, c, :], CVS[0][:, c, :])
            low_weights(FIRST_HALF["wo2"] + 2)

            def low_mixed(c):
                low_tile(2 * KT + c + 1, GCS[1][:, c, :], GC[:, c, :], GCS[0][:, c, :])

            for w in range(8 * NH):
                h, branch, i = w // 8, w // 4 % 2, w % 4
                n, j = (i + 1) * P, w % 8
                if w >= 16 and w % 16 == 12:
                    low_mixed(w // 16 - 1)
                pool.wait_ge(s["nsa_rcp"], w + 1)
                gate = 16 * (branch + 1) + h
                nc.gpsimd.tensor_scalar(PN[:, i, 0:n], PN[:, i, 0:n], rcp[:, j:j + 1], GS[:, i, gate:gate + 1],
                                        ALU.mult, ALU.mult).then_inc(s["nsa_probs"], 1)
            low_mixed(NH // 2 - 1)
            low_weights(FIRST_HALF["xo"] + 2)
            for w in range(16):
                j = w % 8
                pool.wait_ge(s["x_rcp"], w + 1)
                nc.gpsimd.tensor_scalar(PX[:, w % 4, :], PX[:, w % 4, :], rcp[:, j:j + 1], 1.0, ALU.mult, ALU.mult
                                        ).then_inc(s["x_probs"], 1)
            low_weights(FIRST_HALF["ffin"] + 2)

            def low_products(j):
                for f in (2 * j, 2 * j + 1):
                    low_tile(3 * KT + f + 1, GTL[:, f, :], GT[:, f, :], GTH[f])

            for j in range(FT // 2):
                low_weights(FIRST_HALF["ffin"] + 2 * j + 3)
                if j:
                    low_products(j - 1)
                low_weights(FIRST_HALF["ffin"] + 2 * j + 4)
            low_products(FT // 2 - 1)
            low_weights(len(HALVES))


INPUTS = ["x", "w_ada", "b_ada", "w_in", "w_q_up", "w_kv_up", "w_out", "w_router_group", "w_router_expert",
          "w_expert_gate", "w_expert_up", "w_expert_down", "final_norm_g", "norm2_g", "mem_2", "w_in_2", "conv_pw_w_2",
          "w_out_2", "xq_w_2", "xkv_w_2", "xo_w_2", "ffn_in_w_2", "ffn_out_w_2", "rel_bias_2", "final_norm_g_2"]


def kernel(**inputs):
    import numpy as np
    import concourse.bacc as bacc
    from concourse.bass_utils import run_bass_kernel_spmd

    f32 = np.float32
    arrays = {n: np.ascontiguousarray(inputs[n]) for n in INPUTS}

    def tiles(a):
        return np.asarray(a).reshape(-1, P).T

    w2 = np.asarray(inputs["cmp_w2_2"])[0].transpose(1, 0, 2).reshape(64, 128)
    pos = np.asarray(inputs["cmp_pos_2"])[0].reshape(2, 16, P).transpose(2, 0, 1).reshape(P, 32)
    arrays["cols"] = np.ascontiguousarray(np.concatenate([
        tiles(inputs["norm1_g"]), tiles(inputs["norm2_g"]), tiles(inputs["norm_mix_g_2"]), tiles(inputs["norm_x_g_2"]),
        tiles(inputs["norm_ffn_g_2"]), tiles(inputs["q_a_norm_g"]), tiles(inputs["kv_a_norm_g"]),
        tiles(inputs["subln_g"]), tiles(inputs["conv_dw_b_2"]), tiles(inputs["conv_ln_g_2"]),
        tiles(inputs["conv_ln_b_2"]), tiles(inputs["c"]),
        np.asarray(inputs["conv_dw_w_2"])[0].reshape(CONV_W, KT, P).transpose(2, 1, 0).reshape(P, KT * CONV_W),
        pos, np.concatenate([w2, w2])], axis=1))
    arrays["lam"] = np.concatenate([np.asarray(inputs[n])[0] for n in ("lambda_q1", "lambda_k1", "lambda_q2",
                                                                      "lambda_k2")])
    arrays["b_router"] = np.concatenate([np.asarray(inputs["b_router_group"])[0],
                                         np.asarray(inputs["b_router_expert"])[0]])
    w1 = np.asarray(inputs["cmp_w1_2"])[0]
    arrays["cmp_w1"] = np.ascontiguousarray(w1.transpose(2, 0, 1, 3).reshape(1, 64, 4096))
    arrays["cmp_w1_flat"] = np.ascontiguousarray(w1.reshape(2, 16, P, 64).transpose(2, 0, 1, 3).reshape(P, 1, 2048))

    tok = np.arange(S)
    inv = (f32(10000.0) ** (-np.arange(0, 64, 2, dtype=f32) / f32(64))).astype(f32)
    ang = tok.astype(f32)[:, None] * inv[None, :]
    cos, sin = np.cos(ang).astype(f32), np.sin(ang).astype(f32)
    by_tile = lambda a: a.reshape(TT, P, -1).transpose(1, 0, 2).reshape(P, -1)
    row = np.arange(P)
    k1 = np.zeros((P, K1_N), f32)
    k1[:, K1_ID:K1_ID + P] = np.eye(P)
    falling = tok.reshape(TT, P)[:, ::-1].reshape(S, 1)
    k1[:, K1_MASK:] = by_tile((falling - (np.arange(NCMP) * 16 + 31)[None, :] >= 0).astype(f32))
    k2 = np.zeros((P, K2_N), f32)
    k2[:, K2_COS:K2_SIN] = by_tile(cos)
    k2[:, K2_SIN:K2_LT] = by_tile(np.concatenate([-sin, sin], axis=1))
    k2[:, K2_LT:K2_IOTA] = row[:, None] < row[None, :]
    k2[:, K2_IOTA:K2_TOK] = row[None, :]
    k2[:, K2_TOK:K2_ANTI] = tok.reshape(TT, P).T
    k2[:, K2_ANTI:K2_N] = np.eye(P)[:, ::-1]
    arrays["k1"], arrays["k2"] = k1, k2

    def buckets(dist):
        n = np.maximum(dist, 0)
        large = 16 + (np.log(np.maximum(n, 1).astype(f32) / f32(16)) / f32(np.log(8)) * f32(16)).astype(np.int32)
        b = np.where(n < 16, n, np.minimum(large, 31))
        b = np.where(dist >= 0, b, 32)
        return (b[None, :] == np.arange(33)[:, None]).astype(f32)

    arrays["onehot"] = buckets(511 - np.arange(NG))

    nc = bacc.Bacc("TRN2", target_bir_lowering=False, num_devices=1)
    io, sent = {}, {}
    for name, a in arrays.items():
        sent[f"in_{name}"] = a
        io[name] = nc.dram_tensor(f"in_{name}", a.shape, mybir.dt.from_np(a.dtype), kind="ExternalInput").ap()
    io["out"] = nc.dram_tensor("out", (1, S, D), F32, kind="ExternalOutput").ap()
    build(nc, io)
    r = run_bass_kernel_spmd(nc, [sent], core_ids=[0])
    return r.results[0]["out"]
```
